# Optimizing a Trainium2 kernel written in Bass

```python
import math
import jax, jax.numpy as jnp
from jax import lax
import numpy as np

D_MODEL = 1024
BATCH = 1
SEQ = 1024
DEPTH = 2
DEC_BATCH = 1
DEC_SEQ = 1024
PAST_LEN = 128

N_GROUPS = 4
GROUP_W = D_MODEL // N_GROUPS
HEAD_DIM = 64
CONV_A_W = 3
MLA_HEADS = GROUP_W // HEAD_DIM
MLA_NOPE = 64
MLA_ROPE = 32
MLA_V = GROUP_W // MLA_HEADS
MLA_Q_RANK = 3 * D_MODEL // 16
MLA_KV_RANK = D_MODEL // 8
ROPE_THETA = 10000.0
CONV_C_W = 31
SWA_HEADS = GROUP_W // HEAD_DIM
SWA_KV_HEADS = 2
SWA_G = SWA_HEADS // SWA_KV_HEADS
WINDOW = 128
BLOCK = 128
N_BUCKETS = 32
MAX_DIST = 128
EPS = 1e-6
NEG = -1e30

IN_SIZES = (
    GROUP_W, GROUP_W, GROUP_W, GROUP_W,
    MLA_Q_RANK, MLA_KV_RANK, MLA_ROPE, GROUP_W,
    GROUP_W, GROUP_W, GROUP_W,
    SWA_HEADS * HEAD_DIM, SWA_KV_HEADS * HEAD_DIM,
    SWA_KV_HEADS * HEAD_DIM, GROUP_W,
)
IN_WIDTH = sum(IN_SIZES)

kernel_name = "hybrid_parallel_group_encoder"

def _split_points():
    return [int(v) for v in np.cumsum(IN_SIZES)[:-1]]

def _rmsnorm(x, g):
    xf = x.astype(jnp.float32)
    y = xf * lax.rsqrt(jnp.mean(xf * xf, axis=-1, keepdims=True) + EPS)
    return (y * g.astype(jnp.float32)).astype(x.dtype)

def _layernorm(x, g, b):
    xf = x.astype(jnp.float32)
    mu = jnp.mean(xf, axis=-1, keepdims=True)
    xc = xf - mu
    y = xc * lax.rsqrt(jnp.mean(xc * xc, axis=-1, keepdims=True) + EPS)
    return (y * g.astype(jnp.float32) + b.astype(jnp.float32)).astype(x.dtype)

def _depthwise_conv(x, w, b):
    k = w.shape[0]
    p = (k - 1) // 2
    y = lax.conv_general_dilated(
        x, w[:, None, :].astype(x.dtype), window_strides=(1,), padding=[(p, p)],
        dimension_numbers=("NWC", "WIO", "NWC"), feature_group_count=x.shape[-1])
    return y + b.astype(x.dtype)

def _rope_tables(s):
    inv = ROPE_THETA ** (-jnp.arange(0, MLA_ROPE, 2, dtype=jnp.float32) / MLA_ROPE)
    ang = jnp.arange(s, dtype=jnp.float32)[:, None] * inv[None, :]
    return jnp.cos(ang), jnp.sin(ang)

def _rope(t, cos, sin):
    c = cos[:, None, :].astype(t.dtype)
    s = sin[:, None, :].astype(t.dtype)
    t1, t2 = jnp.split(t, 2, axis=-1)
    return jnp.concatenate([t1 * c - t2 * s, t1 * s + t2 * c], axis=-1)

def _t5_buckets(rel):
    half = N_BUCKETS // 2
    max_exact = half // 2
    n = np.abs(rel)
    large = max_exact + (np.log(np.maximum(n, 1) / max_exact) / math.log(MAX_DIST / max_exact)
                         * (half - max_exact)).astype(np.int32)
    large = np.minimum(large, half - 1)
    return (rel > 0).astype(np.int32) * half + np.where(n < max_exact, n, large).astype(np.int32)

def _short_conv_mixer(bg, cg, hv, w, b):
    return bg * _depthwise_conv(cg * hv, w, b)

def _mla_mixer(q_lat, kv_lat, k_rope, g_q, w_q_up, g_kv, w_kv_up, cos, sin):
    bsz, s, _ = q_lat.shape
    nb = s // BLOCK
    q = (_rmsnorm(q_lat, g_q) @ w_q_up).reshape(bsz, s, MLA_HEADS, MLA_NOPE + MLA_ROPE)
    q_nope, q_rot = q[..., :MLA_NOPE], _rope(q[..., MLA_NOPE:], cos, sin)
    kv = (_rmsnorm(kv_lat, g_kv) @ w_kv_up).reshape(bsz, s, MLA_HEADS, MLA_NOPE + MLA_V)
    k_nope, v = kv[..., :MLA_NOPE], kv[..., MLA_NOPE:]
    k_rot = _rope(k_rope[:, :, None, :], cos, sin)[:, :, 0, :]
    scale = (MLA_NOPE + MLA_ROPE) ** -0.5
    qn = q_nope.reshape(bsz, nb, BLOCK, MLA_HEADS, MLA_NOPE).transpose(1, 0, 2, 3, 4)
    qr = q_rot.reshape(bsz, nb, BLOCK, MLA_HEADS, MLA_ROPE).transpose(1, 0, 2, 3, 4)

    def attend(args):
        qn_b, qr_b = args
        sc = (jnp.einsum('bqhd,bkhd->bhqk', qn_b, k_nope)
              + jnp.einsum('bqhr,bkr->bhqk', qr_b, k_rot)).astype(jnp.float32) * scale
        p = jax.nn.softmax(sc, axis=-1).astype(v.dtype)
        return jnp.einsum('bhqk,bkhd->bqhd', p, v)

    o = lax.map(attend, (qn, qr))
    return o.transpose(1, 0, 2, 3, 4).reshape(bsz, s, MLA_HEADS * MLA_V)

def _conformer_conv_mixer(va, vb, w_dw, b_dw, ln_g, ln_b, w_pw):
    u = va * jax.nn.sigmoid(vb)
    u = _depthwise_conv(u, w_dw, b_dw)
    u = jax.nn.silu(_layernorm(u, ln_g, ln_b))
    return u @ w_pw

def _windowed_gqa(q, k, v, sink, rel_bias):
    bsz, s, _ = q.shape
    nb = s // BLOCK
    q = q.reshape(bsz, nb, BLOCK, SWA_KV_HEADS, SWA_G, HEAD_DIM)

    def band(t):
        t = t.reshape(bsz, s, SWA_KV_HEADS, HEAD_DIM)
        t = jnp.pad(t, ((0, 0), (BLOCK, BLOCK), (0, 0), (0, 0)))
        t = t.reshape(bsz, nb + 2, BLOCK, SWA_KV_HEADS, HEAD_DIM)
        return jnp.concatenate([t[:, :-2], t[:, 1:-1], t[:, 2:]], axis=2)

    kb, vb = band(k), band(v)
    sc = jnp.einsum('bnqkgd,bnjkd->bnkgqj', q, kb).astype(jnp.float32) * (HEAD_DIM ** -0.5)
    rel = np.arange(3 * BLOCK)[None, :] - BLOCK - np.arange(BLOCK)[:, None]
    bias = rel_bias.astype(jnp.float32)[_t5_buckets(rel)]
    bias = bias.transpose(2, 0, 1).reshape(SWA_KV_HEADS, SWA_G, BLOCK, 3 * BLOCK)
    key_pos = np.arange(nb)[:, None] * BLOCK - BLOCK + np.arange(3 * BLOCK)[None, :]
    valid = (np.abs(rel) <= WINDOW)[None] & ((key_pos >= 0) & (key_pos < s))[:, None, :]
    sc = jnp.where(valid[None, :, None, None], sc + bias, NEG)
    sink_l = sink.astype(jnp.float32).reshape(1, 1, SWA_KV_HEADS, SWA_G, 1, 1)
    m = jnp.maximum(jnp.max(sc, axis=-1, keepdims=True), sink_l)
    e = jnp.exp(sc - m)
    p = e / (jnp.sum(e, axis=-1, keepdims=True) + jnp.exp(sink_l - m))
    o = jnp.einsum('bnkgqj,bnjkd->bnqkgd', p.astype(vb.dtype), vb)
    return o.reshape(bsz, s, SWA_HEADS * HEAD_DIM)

def _layer(x, g_pre, g_post, w_in, w_out, conv_a_w, conv_a_b, mla_g_q, mla_w_q_up,
           mla_g_kv, mla_w_kv_up, conf_w_dw, conf_b_dw, conf_ln_g, conf_ln_b, conf_w_pw,
           swa_sink, rel_bias, cos, sin):
    h = _rmsnorm(x, g_pre)
    proj = h @ w_in
    (a_b, a_c, a_h, a_g, b_ql, b_kvl, b_kr, b_g, c_va, c_vb, c_g,
     d_q, d_k, d_v, d_g) = jnp.split(proj, _split_points(), axis=-1)
    ya = _short_conv_mixer(a_b, a_c, a_h, conv_a_w, conv_a_b) * jax.nn.silu(a_g)
    yb = _mla_mixer(b_ql, b_kvl, b_kr, mla_g_q, mla_w_q_up, mla_g_kv, mla_w_kv_up,
                    cos, sin) * jax.nn.silu(b_g)
    yc = _conformer_conv_mixer(c_va, c_vb, conf_w_dw, conf_b_dw, conf_ln_g, conf_ln_b,
                               conf_w_pw) * jax.nn.silu(c_g)
    yd = _windowed_gqa(d_q, d_k, d_v, swa_sink, rel_bias) * jax.nn.silu(d_g)
    out = jnp.concatenate([ya, yb, yc, yd], axis=-1) @ w_out
    return x + _rmsnorm(out, g_post)

def _trunk(x, g_pre, g_post, w_in, w_out, conv_a_w, conv_a_b, mla_g_q, mla_w_q_up,
           mla_g_kv, mla_w_kv_up, conf_w_dw, conf_b_dw, conf_ln_g, conf_ln_b, conf_w_pw,
           swa_sink, rel_bias):
    cos, sin = _rope_tables(x.shape[1])
    for l in range(DEPTH):
        x = _layer(x, g_pre[l], g_post[l], w_in[l], w_out[l], conv_a_w[l], conv_a_b[l],
                   mla_g_q[l], mla_w_q_up[l], mla_g_kv[l], mla_w_kv_up[l],
                   conf_w_dw[l], conf_b_dw[l], conf_ln_g[l], conf_ln_b[l], conf_w_pw[l],
                   swa_sink[l], rel_bias, cos, sin)
    return x

def setup_inputs(seed: int = 0) -> dict:
    key = jax.random.key(seed)
    ks = jax.random.split(key, 20)
    f = jnp.float32
    nrm = lambda k, shape, sc: jax.random.normal(k, shape, f) * sc
    return {
        "x_prompt": jax.random.normal(ks[0], (BATCH, SEQ, D_MODEL), f),
        "x_sample": jax.random.normal(ks[1], (DEC_BATCH, DEC_SEQ, D_MODEL), f),
        "g_pre": 1.0 + nrm(ks[2], (DEPTH, D_MODEL), 0.01),
        "g_post": 1.0 + nrm(ks[3], (DEPTH, D_MODEL), 0.01),
        "w_in": nrm(ks[4], (DEPTH, D_MODEL, IN_WIDTH), D_MODEL ** -0.5),
        "w_out": nrm(ks[5], (DEPTH, N_GROUPS * GROUP_W, D_MODEL), (N_GROUPS * GROUP_W) ** -0.5),
        "conv_a_w": nrm(ks[6], (DEPTH, CONV_A_W, GROUP_W), CONV_A_W ** -0.5),
        "conv_a_b": nrm(ks[7], (DEPTH, GROUP_W), 0.01),
        "mla_g_q": 1.0 + nrm(ks[8], (DEPTH, MLA_Q_RANK), 0.01),
        "mla_w_q_up": nrm(ks[9], (DEPTH, MLA_Q_RANK, MLA_HEADS * (MLA_NOPE + MLA_ROPE)), MLA_Q_RANK ** -0.5),
        "mla_g_kv": 1.0 + nrm(ks[10], (DEPTH, MLA_KV_RANK), 0.01),
        "mla_w_kv_up": nrm(ks[11], (DEPTH, MLA_KV_RANK, MLA_HEADS * (MLA_NOPE + MLA_V)), MLA_KV_RANK ** -0.5),
        "conf_w_dw": nrm(ks[12], (DEPTH, CONV_C_W, GROUP_W), CONV_C_W ** -0.5),
        "conf_b_dw": nrm(ks[13], (DEPTH, GROUP_W), 0.01),
        "conf_ln_g": 1.0 + nrm(ks[14], (DEPTH, GROUP_W), 0.01),
        "conf_ln_b": nrm(ks[15], (DEPTH, GROUP_W), 0.01),
        "conf_w_pw": nrm(ks[16], (DEPTH, GROUP_W, GROUP_W), GROUP_W ** -0.5),
        "swa_sink": nrm(ks[17], (DEPTH, SWA_HEADS), 0.5),
        "rel_bias": nrm(ks[18], (N_BUCKETS, SWA_HEADS), 0.5),
    }

def reference(x_prompt, x_sample, g_pre, g_post, w_in, w_out, conv_a_w, conv_a_b,
              mla_g_q, mla_w_q_up, mla_g_kv, mla_w_kv_up, conf_w_dw, conf_b_dw,
              conf_ln_g, conf_ln_b, conf_w_pw, swa_sink, rel_bias):
    y_prompt = _trunk(x_prompt, g_pre, g_post, w_in, w_out, conv_a_w, conv_a_b, mla_g_q,
                      mla_w_q_up, mla_g_kv, mla_w_kv_up, conf_w_dw, conf_b_dw, conf_ln_g,
                      conf_ln_b, conf_w_pw, swa_sink, rel_bias)
    y_sample = _trunk(x_sample, g_pre, g_post, w_in, w_out, conv_a_w, conv_a_b, mla_g_q,
                      mla_w_q_up, mla_g_kv, mla_w_kv_up, conf_w_dw, conf_b_dw, conf_ln_g,
                      conf_ln_b, conf_w_pw, swa_sink, rel_bias)
    return (y_prompt, y_sample)


_drawn_inputs = setup_inputs


def setup_inputs(seed=0):
    import zlib

    import numpy as np

    out = dict(_drawn_inputs(seed))
    spreads = {}
    factors = {'g_post': 5.161,
     'conv_a_b': 5.527,
     'mla_g_q': 8.0,
     'mla_g_kv': 8.0,
     'conf_b_dw': 4.748,
     'conf_ln_g': 7.963,
     'conf_ln_b': 8.0,
     'swa_sink': 64.0}
    for name, (base, spread) in spreads.items():
        noise = np.random.default_rng([zlib.crc32(name.encode()), seed]).standard_normal(out[name].shape)
        drawn = base * np.exp(spread * noise) if base else spread * noise
        out[name] = __import__('jax').numpy.asarray(drawn.astype(out[name].dtype))
    for name, factor in factors.items():
        out[name] = (out[name] * factor).astype(out[name].dtype)
    return out
```

```python
import math
from contextlib import ExitStack

import numpy as np
import concourse.bass as bass
from concourse import mybir

F32 = mybir.dt.float32
F32R = mybir.dt.float32r
ACT = mybir.ActivationFunctionType
ALU = mybir.AluOpType
AX = mybir.AxisListType

P = 128
D = 1024
T = 1024
L = 2
S = 2
KD = D // P
NT = T // P
HALF = 512
GW = D // 4
HD = 64
HEADS = GW // HD
NOPE, ROPE = 64, 32
QR, KVR = 3 * D // 16, D // 8
TAPS_A, TAPS_C = 3, 31
PAD_C = (TAPS_C - 1) // 2
BUCKETS, WINDOW, MAX_DIST = 32, 128, 128
EPS = 1e-6
NEG = -1e30
EARLY = 4
B_SCALE = (NOPE + ROPE) ** -0.5
D_SCALE = HD ** -0.5

CHUNKS = ["dq0", "dq1", "dk", "dv", "dg0", "dg1",
          "cvb0", "cva0", "cvb1", "cva1", "cg0", "cg1",
          "ac0", "ah0", "ab0", "ag0", "ac1", "ah1", "ab1", "ag1",
          "bq0", "bq1", "bkv", "bg0", "bg1"]
C = {name: n for n, name in enumerate(CHUNKS)}
NC = len(CHUNKS)
LATER = ["pw0", "pw1", "bcast_kv", "dv_t", "bv0", "bv1", "rope", "rope_sw",
         "bk0", "bqn0", "bk1", "bqn1"]
for _n, _name in enumerate(LATER):
    C[_name] = NC + _n
RAW = CHUNKS[:16] + ["w_pw"] + CHUNKS[16:] + ["w_q", "w_kv"] + [f"w_out{k}" for k in range(KD)]
POS = {name: n for n, name in enumerate(RAW)}
RAWS = 3
STATS = 3
XS = 4
XP = 2
TH = ["dg0", "dg1", "cvb0", "cvb1", "cg0", "cg1", "ag0", "ag1", "bg0", "cz0", "cz1", "bg1"]
TH = {name: n + 1 for n, name in enumerate(TH)}
CAT = {"ag0": 0, "ag1": 1, "bg0": 2, "bg1": 3, "cg0": 4, "cg1": 5, "dg0": 6, "dg1": 7}

P_AW, P_AB = 0, 2 * TAPS_A
P_CW = P_AB + 2
P_CB = P_CW + 2 * TAPS_C
P_LG, P_LB = P_CB + 2, P_CB + 4
P_GQ, P_GKV = P_CB + 6, P_CB + 8
P_SINK = P_GKV + 1
P_N = P_SINK + HEADS


NB = HEADS * NT
W_OUT_AT = {NB * 5 // 8 + 2 * k: k for k in range(EARLY)}


class Chain:

    def __init__(self, eng, sem):
        self.eng, self.sem, self.n = eng, sem, 0

    def add(self, ins):
        self.n += 1
        ins.then_inc(self.sem, 1)
        return self.n

    def wait(self, n=None):
        n = self.n if n is None else n
        if n > 0:
            self.eng.wait_ge(self.sem, n)


def build(nc, x, w_in, w_out, w_q, w_kv, w_pw, par, g_pre, g_post, rel_bias, onehot, band, rope, y):
    with ExitStack() as ctx:
        base = nc.sbuf_base
        top = [(base + 63) // 64 * 64]

        def region(kb):
            at = top[0]
            top[0] += int(kb * 1024)
            assert top[0] <= nc.sbuf_usable_end, (top[0], nc.sbuf_usable_end)
            return at

        def at(name, shape, dt, addr):
            return nc.alloc_sbuf_tensor_at(name, shape, dt, offset=addr)

        def sem(name):
            return ctx.enter_context(nc.semaphore(name))

        r_big = region(64)
        r_cat = region(32)
        r_stat = region(24)
        r_raw = region(12)
        r_x = region(16)
        r_u = region(8.25)
        r_d = region(16)
        r_b = region(12)
        r_bias = region(6)
        r_rope = region(8)
        r_g = region(4)
        r_pw = region(4)
        r_small = region(3)
        r_xp = region(4 * XP)
        r_gpre = region(4)

        K = 1024
        hT = at("hT", [P, 2, KD, T], F32R, r_big)
        woR = [at(f"woR{k}", [P, 2, D], F32R, a) for k, a in enumerate(
            [r_b, r_u, r_big + 56 * K, r_stat + 16 * K] + [r_big + 8 * K * k for k in range(KD - EARLY)])]
        Qst = at("Qst", [P, HEADS, T], F32R, r_big)
        Kst = at("Kst", [P, 2, 2, T], F32R, r_big + 16 * K)
        Vd = at("Vd", [P, NT, 2, 2, HD], F32R, r_big + 32 * K)
        Pd = at("Pd", [P, 2, 2, 384], F32, r_big + 40 * K)
        PTd = at("PTd", [P, 2, 2, 768], F32R, r_big + 46 * K)
        Vb = at("Vb", [P, NT, HEADS, 2, HD], F32R, r_big)
        PTb = at("PTb", [P, 2, 2, NT, 256], F32R, r_big + 16 * K)
        Pb = at("Pb", [P, 2, T], F32, r_big + 48 * K)
        qrF = at("qrF", [P, 2, T], F32, r_big + 48 * K)
        qrR = at("qrR", [P, 2, T], F32R, r_big + 56 * K)
        cat = at("cat", [P, KD, T], F32, r_cat)
        stat = at("stat", [P, STATS, 2, KD, P], F32R, r_stat)
        catR = at("catR", [P, 2, 2, KD, P], F32R, r_stat)
        qlR = at("qlR", [P, 2, 2, T], F32R, r_stat)
        kvR = at("kvR", [P, 2, T], F32R, r_stat + 16 * K)
        raw = at("raw", [P, RAWS, 1024], F32, r_raw)
        xs = at("xs", [P, XS, D], F32, r_x)
        xp = at("xp", [P, XP, D], F32, r_xp)
        gpre = at("gpre", [P, D], F32, r_gpre)
        accC = at("accC", [P, 2, T], F32, r_x)
        cLo = at("cLo", [P, 2, T], F32R, r_x)
        th = at("th", [P, T], F32, r_x + 8 * K)
        aC = at("aC", [P, T], F32, r_x + 12 * K)
        Qo = at("Qo", [P, 2, T], F32R, r_x)
        Ko = at("Ko", [P, 2, T], F32R, r_x + 8 * K)
        UP = T + 2 * PAD_C + 2
        uC = at("uC", [P, 2, UP], F32, r_u)
        cHi = at("cHi", [P, 2, T], F32R, r_u)
        rbc = at("rbc", [P, T], F32, r_u)
        krt = at("krt", [P, T], F32, r_u + 4 * K)
        rawD = at("rawD", [P, 4, T], F32, r_d)
        Qe = at("Qe", [P, 2, T], F32R, r_d)
        Ke = at("Ke", [P, 2, T], F32R, r_d + 8 * K)
        rawB = at("rawB", [P, 3, T], F32, r_b)
        wup = at("wup", [P, 2, 3, 512], F32R, r_b)
        aU = at("aU", [P, T + 2], F32, r_b)
        bias = at("bias", [P, HEADS, 384], F32, r_bias)
        ropeT = at("ropeT", [P, 2, T], F32, r_rope)
        gvec = at("gvec", [P, D], F32, r_g)
        wpR = at("wpR", [P, 2, 2, GW], F32R, r_pw)

        small = [r_small]

        def sm(name, cols, dt=F32, rows=P):
            t = at(name, [rows, cols], dt, small[0])
            small[0] += (4 * cols + 31) // 32 * 32
            assert small[0] <= top[0]
            return t

        ident = sm("ident", P)
        ones = sm("ones", 2)
        expo = sm("expo", NT)
        parT = sm("parT", P_N)
        ss = sm("ss", NT)
        rs = sm("rs", NT)
        mcol = sm("mcol", NT)
        cvar = sm("cvar", NT)
        crs = sm("crs", NT)
        bvar = sm("bvar", 3 * NT)
        brs = sm("brs", 2 * NT)
        rsq = sm("rsq", NT)
        ngs = sm("ngs", HEADS)
        oss = sm("oss", NT)
        ors = sm("ors", NT)
        dmx = sm("dmx", 4)
        dnm = sm("dnm", 4)
        des = sm("des", 4)
        dsm = sm("dsm", 4)
        dex = sm("dex", 4)
        drc = sm("drc", 4)
        bmx = sm("bmx", NB)
        bnb = sm("bnb", NB)
        bsm = sm("bsm", NB)
        brc = sm("brc", NB)
        tmpD = at("tmpD", [P, 2, P], F32, r_pw)
        tmpB = at("tmpB", [P, 2, 256], F32, r_pw)
        rbB = at("rbB", [P, 2, 256], F32, r_pw + 2 * K)
        junk = at("junk", [P, D], F32, r_b + 8 * K)
        oh = at("oh", [BUCKETS, 512], F32, r_cat)
        rb = at("rb", [BUCKETS, HEADS], F32, r_cat + 2 * K)
        bandT = at("bandT", [HEADS, 512], F32, r_cat + 4 * K)
        bvec = at("bvec", [HEADS, 512], F32, r_cat + 6 * K)

        ps = ctx.enter_context(nc.psum_tensor("ps", [P, 8, 512], F32))
        vec_dram = nc.dram_tensor("bias_by_distance", (HEADS, P, 512), F32, kind="Internal")

        p_ld, p_st, p_rd, p_id, p_mm, p_bv = (sem(n) for n in ("p_ld", "p_st", "p_rd", "p_id", "p_mm", "p_bv"))
        with nc.Block() as block:
            @block.gpsimd
            def _(pool):
                pool.memset(ident[:, :], 0.0).then_inc(p_id, 1)
                pool.memset(ones[:, :], 1.0)
                pool.memset(expo[:, :], -0.5)
                pool.wait_ge(p_id, 1)
                pool.affine_select(out=ident[:, :], in_=ident[:, :], compare_op=ALU.not_equal, fill=1.0,
                                   base=0, pattern=[[-1, P]], channel_multiplier=1).then_inc(p_id, 1)

            @block.sync
            def _(sp):
                sp.dma_start(oh[:, :], onehot).then_inc(p_ld, 16)
                sp.dma_start(rb[:, :], rel_bias).then_inc(p_ld, 16)
                sp.dma_start(bandT[:, :], band).then_inc(p_ld, 16)
                sp.dma_start(ropeT[:, :, :], rope.rearrange("a p t -> p a t")).then_inc(p_rd, 16)
                sp.wait_ge(p_bv, 1)
                sp.dma_start(vec_dram.ap(), bvec[:, :].unsqueeze(1).broadcast_to([HEADS, P, 512])).then_inc(p_st, 16)
                sp.wait_ge(p_st, 16)
                sp.dma_start(bias[:, :, :], bass.AP(vec_dram, P - 1, [[511, P], [512 * P, HEADS], [1, 384]])
                             ).then_inc(p_rd, 16)
                for n in range(XP):
                    sp.dma_start(xp[:, n, :], x[0, n * P:(n + 1) * P, :]).then_inc(p_rd, 16)
                sp.dma_start(gpre[:, :], g_pre[0:1].broadcast_to([P, D])).then_inc(p_rd, 16)
                for i in range(RAWS):
                    sp.dma_start(raw[:, i, :], w_in[0, i]).then_inc(p_rd, 16)
                sp.dma_start(parT[:, :], par[0]).then_inc(p_rd, 16)
                sp.wait_ge(p_rd, 16 * (2 + XP + 1 + RAWS + 1))

            @block.tensor
            def _(pe):
                pe.wait_ge(p_ld, 48)
                pe.matmul(ps[0:HEADS, 0, :], rb[:, :], oh[:, :], start=True, stop=True).then_inc(p_mm, 1)

            @block.vector
            def _(dve):
                dve.wait_ge(p_mm, 1)
                dve.tensor_tensor(bvec[:, :], ps[0:HEADS, 0, :], bandT[:, :], ALU.add).then_inc(p_bv, 1)

        names = ("next_ld gpost_ld sq_ok rs_ok xn_ok xt_ok hhi hlo whi wlo ch_done th_ok th_used "
                 "pads_ok own_dve own_act own_pool conv_own conv_ok st_cp mcol_ok xc_ok xsq_ok cvar_ok crs_ok y_ok "
                 "chi_ok clo_ok st_b bsq_ok bstat_ok brs_ok dst_hi dst_lo vd_hi vd_lo lat_hi lat_lo kr_ok "
                 "ke_hi ke_lo ko_ok zero_ok ds_mm ds_ok dm_ok de_ok dr_ok dp_ok dt_mm dpt_hi dpt_lo do_mm do_tmp do_ok "
                 "rbc_ok vb_hi vb_lo qr_ok qr_hi qr_lo kt_ok k_hi k_lo q_hi q_lo qrope_ok "
                 "bs_mm bm_ok be_ok br_ok bt_mm bpt_hi bpt_lo bo_mm bo_tmp bo_ok "
                 "chi2 clo2 o_mm osq_ok ovar_ok ors_ok o1_ok o2_ok "
                 "free0 free1").split()
        q = {n: sem(n) for n in names}
        x_ld = [sem(f"x_ld{i}") for i in range(XS)]
        y_st = [sem(f"y_st{i}") for i in range(XS)]
        w_ld = [sem(f"w_ld{i}") for i in range(RAWS)]
        per_pass = list(q.values()) + x_ld + y_st + w_ld

        read_by = {"dv_t": ("vd_lo", 1), "bv0": ("vb_lo", NT // 2), "bv1": ("vb_lo", NT)}
        for p in range(2):
            read_by |= {f"bk{p}": ("kt_ok", p + 1), f"bqn{p}": ("q_lo", 2 * p + 2),
                        f"cva{p}": ("th_used", TH[f"cvb{p}"]), f"cvb{p}": ("th_ok", TH[f"cvb{p}"])}
        read_by |= {name: ("th_used", TH[name]) for name in CAT}
        counts = [0, 0]
        by_number = {n: name for name, n in C.items()}
        for n in sorted(by_number):
            if by_number[n] not in read_by:
                counts[n % 2] += 1
                read_by[by_number[n]] = (f"free{n % 2}", counts[n % 2])

        def x_tile(n):
            return xp[:, n, :] if n < XP else xs[:, (n - XP) % XS, :]

        def x_landed(n):
            return x_ld[(n - XP) % XS], 16 * ((n - XP) // XS + 1)

        def residual_landed(n):
            before = len([m for m in range(XP, NT) if (m - XP) % XS == n % XS])
            return x_ld[n % XS], 16 * (before + n // XS + 1)

        def free_at(name):
            s_, value = read_by[name]
            return q[s_], value

        def pair(c):
            return ps[:, 2 * (c % 2):2 * (c % 2) + 2, :].rearrange("p b n -> p (b n)")

        def chunk_ps(name):
            return pair(C[name])

        def keys(n):
            k0, k1 = max(0, n - 1), min(NT - 1, n + 1)
            return k0, k1 - k0 + 1, (k0 - n + 1) * P

        DU = [(n, kv) for n in range(NT) for kv in range(2)]
        CONV_STEPS = {C["cg0"] + i: t for i, t in enumerate(
            np.array_split(np.arange(TAPS_C), C["bq0"] - C["cg0"]))}

        with nc.Fori(0, L) as layer:
          with nc.Fori(0, S) as seq:
            with nc.Block() as block:

                @block.sync
                def _(sp):
                    lay = bass.ds(layer, 1)
                    sq_ = bass.ds(seq, 1)

                    def load_g(src, s_):
                        sp.dma_start(gvec[:, :], src[lay].broadcast_to([P, D])).then_inc(s_, 16)

                    def load_x(src, n, slot):
                        sp.dma_start(xs[:, slot, :], src[sq_, n * P:(n + 1) * P, :]
                                     .rearrange("o p d -> (o p) d")).then_inc(x_ld[slot], 16)

                    def load_norm(src):
                        for n in range(XP, NT):
                            if n >= XP + XS:
                                sp.wait_ge(q["xt_ok"], n - XS + 1)
                            load_x(src, n, (n - XP) % XS)

                    def prefetch(src, seq_, lay_):
                        for n in range(XP):
                            sp.dma_start(xp[:, n, :], src[seq_, n * P:(n + 1) * P, :].rearrange("o p d -> (o p) d")
                                         ).then_inc(q["next_ld"], 16)
                        sp.dma_start(gpre[:, :], g_pre[lay_].broadcast_to([P, D])).then_inc(q["next_ld"], 16)
                        for i in range(RAWS):
                            sp.dma_start(raw[:, i, :], w_in[lay_, i].rearrange("o p n -> (o p) n")
                                         ).then_inc(q["next_ld"], 16)
                        sp.dma_start(parT[:, :], par[lay_].rearrange("o p c -> (o p) c")).then_inc(q["next_ld"], 16)

                    def load_raw(name):
                        i = POS[name]
                        if i >= RAWS:
                            sp.wait_ge(q["wlo"], i - RAWS + 1)
                        dst = raw[:, i % RAWS, :]
                        if name in CHUNKS:
                            src = w_in[lay, C[name]].rearrange("o p n -> (o p) n")
                        elif name == "w_pw":
                            dst, src = dst[:, 0:2 * GW], w_pw[lay].rearrange("o p n -> (o p) n")
                        elif name == "w_q":
                            src = w_q[lay].rearrange("o p n -> (o p) n")
                        elif name == "w_kv":
                            dst, src = dst[:, 0:512], w_kv[lay].rearrange("o p n -> (o p) n")
                        else:
                            k = int(name[5:])
                            src = w_out[lay, k * P:(k + 1) * P, :].rearrange("o p n -> (o p) n")
                        sp.dma_start(dst, src).then_inc(w_ld[i % RAWS], 16)

                    with sp.If(layer < 1):
                        load_norm(x)
                    with sp.Else():
                        load_norm(y)

                    for name in RAW[RAWS:]:
                        load_raw(name)
                    load_g(g_post, q["gpost_ld"])

                    def residual(src):
                        for n in range(NT):
                            if n < XS:
                                sp.wait_ge(q["bs_mm"], NB)
                            else:
                                sp.wait_ge(y_st[n % XS], 16)
                            load_x(src, n, n % XS)
                            if n >= 1:
                                store(n - 1)

                    def store(n):
                        sp.wait_ge(q["o2_ok"], n + 1)
                        sp.dma_start(y[sq_, n * P:(n + 1) * P, :].rearrange("o p d -> (o p) d"),
                                     xs[:, n % XS, :]).then_inc(y_st[n % XS], 16)

                    sp.wait_ge(q["wlo"], len(RAW))
                    with sp.If(seq < 1):
                        with sp.If(layer < 1):
                            prefetch(x, bass.ds(1, 1), lay)
                        with sp.Else():
                            prefetch(y, bass.ds(1, 1), lay)
                    with sp.Else():
                        prefetch(y, bass.ds(0, 1), bass.ds(L - 1, 1))
                    with sp.If(layer < 1):
                        residual(x)
                    with sp.Else():
                        residual(y)
                    store(NT - 1)
                    sp.wait_ge(q["next_ld"], 16 * (XP + 1 + RAWS + 1))
                    for i in range(XS):
                        sp.wait_ge(y_st[i], 16 * (NT // XS))

                @block.tensor
                def _(pe):
                    mm, tr = pe.matmul, pe.transpose
                    three = ((0, 0), (0, 1), (1, 0))

                    def x_transpose(n):
                        pe.wait_ge(q["xn_ok"], n + 1)
                        if n >= 2:
                            pe.wait_ge(q["hlo"], n - 1)
                        b = 4 + 2 * (n % 2)
                        for k in range(KD):
                            last = tr(ps[:, b + k // 4, k % 4 * P:(k % 4 + 1) * P],
                                      x_tile(n)[:, k * P:(k + 1) * P], ident[:, :])
                        last.then_inc(q["xt_ok"], 1)

                    def wait_pair(c):
                        if c >= 2:
                            pe.wait_ge(*free_at(by_number[c - 2]))

                    def project(name, halves=(0, 1)):
                        c = C[name]
                        pe.wait_ge(q["wlo"], POS[name] + 1)
                        wait_pair(c)
                        for k in range(KD):
                            for a, b in three:
                                for h in halves:
                                    last = mm(ps[:, 2 * (c % 2) + h, :], stat[:, c % STATS, a, k, :],
                                              hT[:, b, k, h * HALF:(h + 1) * HALF],
                                              start=(k == 0 and (a, b) == (0, 0)),
                                              stop=(k == KD - 1 and (a, b) == (1, 0)))
                        if halves[-1]:
                            last.then_inc(q["ch_done"], 1)

                    def column_sums(bank, col, parts):
                        for n in range(NT):
                            for j, t in enumerate(parts):
                                last = mm(ps[:, bank, col + n:col + n + 1], t[:, n * P:(n + 1) * P],
                                          ones[0:t.shape[0], 0:1], start=(j == 0), stop=(j == len(parts) - 1))
                        return last

                    def spread(dst, src):
                        for n in range(NT):
                            last = tr(dst[:, n * P:(n + 1) * P], src[:, n:n + 1].broadcast_to([P, P]),
                                      ident[:, :])
                        return last

                    bank45 = ps[:, 4:6, :].rearrange("p b n -> p (b n)")
                    for n in range(NT // 2):
                        x_transpose(n)
                    for j in range(2):
                        x_transpose(NT // 2 + 2 * j)
                        x_transpose(NT // 2 + 2 * j + 1)
                        pe.wait_ge(q["hlo"], NT // 2)
                        project(CHUNKS[j], (0,))
                    pe.wait_ge(q["hlo"], NT)
                    for name in CHUNKS:
                        project(name, (1,) if name in CHUNKS[:2] else (0, 1))
                        if name == "bq0":
                            pe.wait_ge(q["conv_ok"], 2)
                            column_sums(6, 0, [accC[:, 0, :], accC[:, 1, :]]).then_inc(q["st_cp"], 1)
                        if name == "bq1":
                            pe.wait_ge(q["mcol_ok"], 1)
                            spread(bank45, mcol).then_inc(q["st_cp"], 1)
                            pe.wait_ge(q["bsq_ok"], 1)
                            column_sums(7, 0, [aC]).then_inc(q["st_b"], 1)
                        if name == "bkv":
                            pe.wait_ge(q["xsq_ok"], 2)
                            column_sums(6, 16, [uC[:, 0, 0:T], uC[:, 1, 0:T]]).then_inc(q["st_cp"], 1)
                            pe.wait_ge(q["bsq_ok"], 2)
                            pe.wait_ge(q["bstat_ok"], 1)
                            column_sums(7, NT, [aC[0:QR - P]]).then_inc(q["st_b"], 1)
                        if name == "bg0":
                            pe.wait_ge(q["crs_ok"], 1)
                            spread(bank45, crs).then_inc(q["st_cp"], 1)
                            pe.wait_ge(q["bsq_ok"], 3)
                            pe.wait_ge(q["bstat_ok"], 2)
                            column_sums(7, 2 * NT, [aC]).then_inc(q["st_b"], 1)

                    pe.wait_ge(q["clo_ok"], 2)
                    for m in range(2):
                        c = C[f"pw{m}"]
                        wait_pair(c)
                        for j in range(2):
                            for a, b in three:
                                z = (cHi, cLo)[b]
                                for h in range(2):
                                    last = mm(ps[:, 2 * (c % 2) + h, :], wpR[:, a, j, m * P:(m + 1) * P],
                                              z[:, j, h * HALF:(h + 1) * HALF],
                                              start=(j == 0 and (a, b) == (0, 0)),
                                              stop=(j == 1 and (a, b) == (1, 0)))
                        last.then_inc(q["ch_done"], 1)
                    pe.wait_ge(q["brs_ok"], 1)
                    wait_pair(C["bcast_kv"])
                    spread(chunk_ps("bcast_kv"), brs[:, NT:2 * NT]).then_inc(q["ch_done"], 1)
                    wait_pair(C["dv_t"])
                    for n in range(NT):
                        last = tr(chunk_ps("dv_t")[:, n * P:(n + 1) * P], rawD[:, 3, n * P:(n + 1) * P],
                                  ident[:, :])
                    last.then_inc(q["ch_done"], 1)

                    def d_scores(u):
                        n, kv = DU[u]
                        k0, nk, _ = keys(n)
                        if u >= 2:
                            pe.wait_ge(q["ds_ok"], u - 1)
                        else:
                            pe.wait_ge(*free_at(("dv_t", "bcast_kv")[u]))
                        for g in range(2):
                            for part in range(2):
                                last = mm(ps[:, 2 * (u % 2) + g, 0:nk * P],
                                          Qst[:, 2 * kv + g, n * P:(n + 1) * P],
                                          Kst[:, kv, part, k0 * P:(k0 + nk) * P],
                                          start=(part == 0), stop=(part == 1))
                        last.then_inc(q["ds_mm"], 1)

                    def d_transpose(u):
                        n, kv = DU[u]
                        _, nk, _ = keys(n)
                        pe.wait_ge(q["dp_ok"], u + 1)
                        if u >= 1:
                            pe.wait_ge(q["dpt_lo"], u)
                        else:
                            pe.wait_ge(q["y_ok"], 2)
                        for b in range(nk):
                            for g in range(2):
                                last = tr(bank45[:, (2 * b + g) * P:(2 * b + g + 1) * P],
                                          Pd[:, u % 2, g, b * P:(b + 1) * P], ident[:, :])
                        last.then_inc(q["dt_mm"], 1)

                    def d_out(u):
                        n, kv = DU[u]
                        k0, nk, _ = keys(n)
                        pe.wait_ge(q["dpt_lo"], u + 1)
                        if u >= 2:
                            pe.wait_ge(q["do_ok"], u - 1)
                        for b in range(nk):
                            for part in range(2):
                                last = mm(ps[:, 6 + u % 2, 0:2 * P], Vd[:, k0 + b, kv, :, :],
                                          PTd[:, u % 2, part, b * 2 * P:(b + 1) * 2 * P],
                                          start=(b == 0 and part == 0), stop=(b == nk - 1 and part == 1))
                        last.then_inc(q["do_mm"], 1)

                    pe.wait_ge(q["dst_lo"], 8)
                    pe.wait_ge(q["vd_lo"], 1)
                    pe.wait_ge(q["bstat_ok"], 3)
                    NU = len(DU)
                    for i in range(NU + 2):
                        if i < NU:
                            d_scores(i)
                        if 1 <= i <= NU:
                            d_transpose(i - 1)
                        if i >= 2:
                            d_out(i - 2)

                    pe.wait_ge(q["wlo"], POS["w_kv"] + 1)
                    for c, t0 in (("bv0", 0), ("bv1", NT // 2)):
                        pe.wait_ge(q["ds_ok"], NU)
                        wait_pair(C[c])
                        for i in range(NT // 2):
                            for a, b in three:
                                last = mm(chunk_ps(c)[:, i * GW:(i + 1) * GW],
                                          kvR[:, a, (t0 + i) * P:(t0 + i + 1) * P], wup[:, b, 2, GW:2 * GW],
                                          start=((a, b) == (0, 0)), stop=((a, b) == (1, 0)))
                        last.then_inc(q["ch_done"], 1)

                    def q_up(name, col):
                        c = C[name]
                        for kt, rows in ((0, P), (1, QR - P)):
                            for a, b in three:
                                for h in range(2):
                                    last = mm(ps[:, 2 * (c % 2) + h, :], wup[0:rows, a, kt, col:col + P],
                                              qlR[0:rows, kt, b, h * HALF:(h + 1) * HALF],
                                              start=(kt == 0 and (a, b) == (0, 0)),
                                              stop=(kt == 1 and (a, b) == (1, 0)))
                        last.then_inc(q["ch_done"], 1)

                    for name, col in (("rope", GW), ("rope_sw", GW + P)):
                        wait_pair(C[name])
                        q_up(name, col)

                    def heads_up(p):
                        c = C[f"bk{p}"]
                        wait_pair(c)
                        if p:
                            pe.wait_ge(q["be_ok"], 2 * NT)
                        for a, b in three:
                            for h in range(2):
                                last = mm(ps[:, 2 * (c % 2) + h, :], wup[:, a, 2, p * P:(p + 1) * P],
                                          kvR[:, b, h * HALF:(h + 1) * HALF],
                                          start=((a, b) == (0, 0)), stop=((a, b) == (1, 0)))
                        last.then_inc(q["ch_done"], 1)
                        wait_pair(C[f"bqn{p}"])
                        q_up(f"bqn{p}", p * P)

                    def b_scores(u):
                        h, i = divmod(u, NT)
                        if i == 0:
                            pe.wait_ge(q["k_lo"], h + 1)
                            pe.wait_ge(q["q_lo"], h + 1)
                            pe.wait_ge(q["qrope_ok"], h + 1)
                            pe.wait_ge(q["ko_ok"], 1)
                            pe.wait_ge(q["zero_ok"], 2)
                        if u % (2 * NT) < 2:
                            p = u // (2 * NT)
                            pe.wait_ge(*free_at((f"bqn{p}", f"bk{p}")[u % 2]))
                        if u >= 2:
                            pe.wait_ge(q["be_ok"], u - 1)
                        Q, Kk, rows = ((Qe, Ke, NOPE + ROPE), (Qo, Ko, P))[h % 2]
                        for a, b in three:
                            for half in range(2):
                                last = mm(ps[:, 2 * (u % 2) + half, :], Q[0:rows, a, i * P:(i + 1) * P],
                                          Kk[0:rows, b, half * HALF:(half + 1) * HALF],
                                          start=((a, b) == (0, 0)), stop=((a, b) == (1, 0)))
                        last.then_inc(q["bs_mm"], 1)

                    def b_transpose(u):
                        pe.wait_ge(q["be_ok"], u + 1)
                        for half in range(2):
                            if u >= 1:
                                pe.wait_ge(q["bpt_lo"], 2 * u + half - 1)
                            else:
                                pe.wait_ge(q["dpt_lo"], NU)
                            for k in range(NT // 2):
                                col = half * HALF + k * P
                                last = tr(ps[:, 4 + half, k * P:(k + 1) * P], Pb[:, u % 2, col:col + P], ident[:, :])
                            last.then_inc(q["bt_mm"], 1)

                    def b_out(w, half):
                        h = 2 * w // NT
                        bank = ps[:, 6 + w % 2, :]
                        if half == 0:
                            if w >= 2:
                                pe.wait_ge(q["bo_ok"], w - 1)
                            else:
                                pe.wait_ge(q["do_ok"], NU)
                            pe.wait_ge(q["br_ok"], 2 * w + 2)
                            for i in range(2):
                                tr(bank[:, 256 + i * P:256 + (i + 1) * P],
                                   brc[:, 2 * w + i:2 * w + i + 1].broadcast_to([P, P]), ident[:, :])
                            pe.wait_ge(q["bpt_lo"], 4 * w + 4)
                        for k in range(half * NT // 2, (half + 1) * NT // 2):
                            for part in range(2):
                                last = mm(bank[:, 0:256], Vb[:, k, h, :, :], PTb[:, w % 2, part, k, :],
                                          start=(k == 0 and part == 0), stop=(k == NT - 1 and part == 1))
                        if half:
                            last.then_inc(q["bo_mm"], 1)

                    heads_up(0)
                    pe.wait_ge(q["vb_lo"], NT)
                    for i in range(NB + 3):
                        if i == 2 * NT:
                            heads_up(1)
                        if i < NB:
                            b_scores(i)
                        if 1 <= i <= NB:
                            b_transpose(i - 1)
                        if i >= 3:
                            b_out(*divmod(i - 3, 2))

                    for n in range(NT):
                        pe.wait_ge(q["clo2"], n + 1)
                        if n >= 2:
                            pe.wait_ge(q["o2_ok"], n - 1)
                        for k in range(KD):
                            if n == 0:
                                pe.wait_ge(q["wlo"], POS[f"w_out{k}"] + 1)
                            for a, b in three:
                                for h in range(2):
                                    last = mm(ps[:, 2 * (n % 2) + h, :], catR[:, n % 2, a, k, :],
                                              woR[k][:, b, h * HALF:(h + 1) * HALF],
                                              start=(k == 0 and (a, b) == (0, 0)),
                                              stop=(k == KD - 1 and (a, b) == (1, 0)))
                        last.then_inc(q["o_mm"], 1)

                @block.gpsimd
                def _(pool):
                    own = Chain(pool, q["own_pool"])

                    def rsqrt(dst, src, signal):
                        pool.tensor_tensor(dst, src, expo[:, 0:src.shape[1]], ALU.pow).then_inc(signal, 1)

                    for n in range(NT):
                        pool.wait_ge(q["sq_ok"], n + 1)
                        own.add(pool.tensor_scalar(ss[:, n:n + 1], ss[:, n:n + 1], 1.0 / D, EPS, ALU.mult, ALU.add))
                        own.wait()
                        rsqrt(rs[:, n:n + 1], ss[:, n:n + 1], q["rs_ok"])
                    pool.wait_ge(q["cvar_ok"], 1)
                    rsqrt(crs[:, :], cvar[:, :], q["crs_ok"])
                    pool.wait_ge(q["bstat_ok"], 3)
                    own.add(pool.tensor_tensor(brs[:, 0:NT], bvar[:, 0:NT], expo[:, :], ALU.pow))
                    rsqrt(brs[:, NT:2 * NT], bvar[:, 2 * NT:3 * NT], q["brs_ok"])
                    own.wait()
                    pool.tensor_scalar(rsq[:, :], brs[:, 0:NT], B_SCALE, None, ALU.mult).then_inc(q["brs_ok"], 1)
                    for u, (n, kv) in enumerate(DU):
                        _, nk, _ = keys(n)
                        pool.wait_ge(q["dr_ok"], u + 1)
                        pool.tensor_scalar(Pd[:, u % 2, 0, 0:nk * P], Pd[:, u % 2, 0, 0:nk * P],
                                           drc[:, 2 * (u % 2):2 * (u % 2) + 1], None, ALU.mult)
                        pool.tensor_scalar(Pd[:, u % 2, 1, 0:nk * P], Pd[:, u % 2, 1, 0:nk * P],
                                           drc[:, 2 * (u % 2) + 1:2 * (u % 2) + 2], None,
                                           ALU.mult).then_inc(q["dp_ok"], 1)
                    for n in range(NT):
                        pool.wait_ge(q["ovar_ok"], n + 1)
                        rsqrt(ors[:, n:n + 1], oss[:, n:n + 1], q["ors_ok"])

                @block.scalar
                def _(act):
                    own = Chain(act, q["own_act"])
                    bank45 = ps[:, 4:6, :].rearrange("p b n -> p (b n)")

                    def square_x(n):
                        if n >= XP:
                            act.wait_ge(*x_landed(n))
                        if n >= 1:
                            act.wait_ge(q["sq_ok"], n)
                        act.activation(junk[:, :], x_tile(n), ACT.Square,
                                       accum_out=ss[:, n:n + 1]).then_inc(q["sq_ok"], 1)

                    def h_hi(n):
                        act.wait_ge(q["xt_ok"], n + 1)
                        b = 4 + 2 * (n % 2)
                        act.activation(hT[:, 0, :, n * P:(n + 1) * P],
                                       ps[:, b:b + 2, :].rearrange("p b (k t) -> p (b k) t", t=P),
                                       ACT.Copy).then_inc(q["hhi"], 1)

                    def split_hi(name):
                        i = POS[name]
                        if i >= RAWS:
                            act.wait_ge(w_ld[i % RAWS], 16 * (i // RAWS))
                        src = raw[:, i % RAWS, :]
                        if name in CHUNKS:
                            c = C[name]
                            if c >= STATS:
                                act.wait_ge(q["ch_done"], c - STATS + 1)
                            dst, src = stat[:, c % STATS, 0, :, :], src.rearrange("p (k m) -> p k m", m=P)
                        elif name == "w_pw":
                            dst, src = wpR[:, 0, :, :], src[:, 0:2 * GW].rearrange("p (k m) -> p k m", m=GW)
                        elif name == "w_q":
                            dst, src = wup[:, 0, 0:2, :], src.rearrange("p (k m) -> p k m", m=512)
                        elif name == "w_kv":
                            dst, src = wup[:, 0, 2, :], src[:, 0:512]
                        else:
                            if name == "w_out0":
                                act.wait_ge(q["k_lo"], HEADS)
                                act.wait_ge(q["qrope_ok"], HEADS)
                            dst = woR[int(name[5:])][:, 0, :]
                        act.activation(dst, src, ACT.Copy).then_inc(q["whi"], 1)

                    def tanh_half(name, src):
                        n = TH[name]
                        if n > 1:
                            act.wait_ge(q["th_used"], n - 1)
                        return act.activation(th[:, :], src, ACT.Tanh, scale=0.5).then_inc(q["th_ok"], 1)

                    def evacuate(name):
                        kind = name.rstrip("01")
                        act_reads = kind in ("dq", "dk", "dv", "bq", "bkv", "ac", "cvb") or name in TH
                        if not act_reads:
                            return
                        act.wait_ge(q["ch_done"], C[name] + 1)
                        if name in TH:
                            tanh_half(name, chunk_ps(name))
                            return
                        if kind[0] == "d":
                            dst = rawD[:, C[name], :]
                        elif kind == "ac":
                            if name == "ac1":
                                act.wait_ge(q["th_used"], TH["ag0"])
                                act.wait_ge(*free_at("ag0"))
                            dst = aC[:, :]
                        else:
                            if name == "bq0":
                                act.wait_ge(*free_at("ag1"))
                            dst = rawB[:, C[name] - C["bq0"], :]
                        act.activation(dst, chunk_ps(name), ACT.Copy).then_inc(free_at(name)[0], 1)

                    def b_square(j):
                        rows = (P, QR - P, P)[j]
                        act.wait_ge(*free_at(("bq0", "bq1", "bkv")[j]))
                        if j:
                            act.wait_ge(q["st_b"], j)
                        act.activation(aC[0:rows, :], rawB[0:rows, j, :], ACT.Square).then_inc(q["bsq_ok"], 1)

                    for n in range(NT + 1):
                        if n < NT:
                            square_x(n)
                        if n == 2:
                            split_hi(CHUNKS[0])
                            split_hi(CHUNKS[1])
                        if n >= 1:
                            h_hi(n - 1)
                    ahead = [n for n in RAW if n in CHUNKS or n == "w_pw"][2:]
                    for c, name in enumerate(CHUNKS):
                        if ahead:
                            split_hi(ahead.pop(0))
                            if ahead and ahead[0] == "w_pw":
                                split_hi(ahead.pop(0))
                        evacuate(name)
                        if name in ("bq0", "bq1", "bkv"):
                            b_square(("bq0", "bq1", "bkv").index(name))
                        if name == "bkv":
                            pass
                        if name == "bq1":
                            for j in range(2):
                                act.wait_ge(q["xc_ok"], j + 1)
                                act.activation(uC[:, j, 0:T], accC[:, j, :], ACT.Square).then_inc(q["xsq_ok"], 1)
                        if name == "bg0":
                            for j in range(2):
                                act.wait_ge(q["y_ok"], j + 1)
                                tanh_half(f"cz{j}", accC[:, j, :])
                            for j in range(2):
                                act.wait_ge(q["th_used"], TH[f"cz{j}"])
                                if j == 0:
                                    act.wait_ge(q["st_cp"], 3)
                                act.activation(cHi[:, j, :], accC[:, j, :], ACT.Copy).then_inc(q["chi_ok"], 1)

                    act.wait_ge(q["ch_done"], NC)
                    for j, rows, dst in ((0, P, qlR[:, 0, 0, :]), (1, QR - P, qlR[0:QR - P, 1, 0, :]), (2, P, kvR[:, 0, :])):
                        act.activation(dst, rawB[0:rows, j, :], ACT.Copy,
                                       scale=parT[0:rows, P_GQ + j:P_GQ + j + 1]).then_inc(q["lat_hi"], 1)
                    for h in range(HEADS):
                        r = HD * (h % 2)
                        act.activation(Qst[r:r + HD, h, :], rawD[r:r + HD, h // 2, :], ACT.Copy).then_inc(q["dst_hi"], 1)
                    for kv in range(2):
                        r = HD * kv
                        for r2 in range(0, P, HD):
                            act.activation(Kst[r2:r2 + HD, kv, 0, :], rawD[r:r + HD, 2, :], ACT.Copy).then_inc(q["dst_hi"], 1)
                    act.wait_ge(q["ch_done"], C["bcast_kv"] + 1)
                    act.activation(rbc[:, :], chunk_ps("bcast_kv"), ACT.Copy).then_inc(free_at("bcast_kv")[0], 1)
                    act.wait_ge(q["ch_done"], C["dv_t"] + 1)
                    act.activation(Vd[:, :, :, 0, :], chunk_ps("dv_t").rearrange("p (t v d) -> p t v d", t=NT, v=2),
                                   ACT.Copy).then_inc(q["vd_hi"], 1)
                    act.wait_ge(q["kr_ok"], 1)
                    act.wait_ge(q["dst_lo"], 8)
                    act.activation(Ke[HD:HD + ROPE, 0, :], rawB[HD:HD + ROPE, 1, :], ACT.Copy).then_inc(q["ke_hi"], 1)
                    act.wait_ge(q["ke_lo"], 1)
                    act.activation(Ko[ROPE:2 * ROPE, :, :], Ke[HD:HD + ROPE, :, :].bitcast(F32), ACT.Copy).then_inc(q["ko_ok"], 1)
                    act.wait_ge(q["lat_lo"], 3)
                    split_hi("w_q")
                    split_hi("w_kv")

                    def d_exp(u):
                        n, kv = DU[u]
                        _, nk, _ = keys(n)
                        s2 = 2 * (u % 2)
                        act.wait_ge(q["dm_ok"], u + 1)
                        for g in range(2):
                            act.activation(Pd[:, u % 2, g, 0:nk * P], Pd[:, u % 2, g, 0:nk * P], ACT.Exp,
                                           bias=dnm[:, s2 + g:s2 + g + 1], accum_out=dsm[:, s2 + g:s2 + g + 1])
                        act.activation(dex[:, s2:s2 + 2], des[:, s2:s2 + 2], ACT.Exp).then_inc(q["de_ok"], 1)

                    def d_hi(u):
                        n, kv = DU[u]
                        _, nk, _ = keys(n)
                        act.wait_ge(q["dt_mm"], u + 1)
                        if u >= 2:
                            act.wait_ge(q["do_mm"], u - 1)
                        act.activation(PTd[:, u % 2, 0, 0:nk * 2 * P], bank45[:, 0:nk * 2 * P], ACT.Copy).then_inc(q["dpt_hi"], 1)

                    def d_half(u):
                        act.wait_ge(q["do_mm"], u + 1)
                        if u == 0:
                            act.wait_ge(q["ch_done"], C["pw1"] + 1)
                        if u >= 2:
                            act.wait_ge(q["do_ok"], u - 1)
                        b = ps[:, 6 + u % 2, :]
                        act.activation(tmpD[0:HD, u % 2, :], b[HD:P, 0:P], ACT.Copy)
                        act.activation(tmpD[HD:P, u % 2, :], b[0:HD, P:2 * P], ACT.Copy).then_inc(q["do_tmp"], 1)

                    NU = len(DU)
                    for i in range(NU + 3):
                        if i < NU:
                            d_exp(i)
                        if 1 <= i <= NU:
                            d_hi(i - 1)
                        if 2 <= i <= NU + 1:
                            d_half(i - 2)

                    for n in range(NT):
                        name = ("bv0", "bv1")[2 * n // NT]
                        i = n % (NT // 2)
                        if i == 0:
                            act.wait_ge(q["ch_done"], C[name] + 1)
                        act.activation(Vb[:, n, :, 0, :], chunk_ps(name)[:, i * GW:(i + 1) * GW]
                                       .rearrange("p (h d) -> p h d", d=HD), ACT.Copy,
                                       scale=brs[:, NT + n:NT + n + 1]).then_inc(q["vb_hi"], 1)
                    act.wait_ge(q["qr_ok"], 1)
                    act.activation(qrR[:, 0, :], qrF[:, 0, :], ACT.Copy).then_inc(q["qr_hi"], 1)

                    def head_hi(p):
                        act.wait_ge(q["kt_ok"], p + 1)
                        act.activation(Ke[0:HD, 0, :], krt[0:HD, :], ACT.Copy).then_inc(q["k_hi"], 1)
                        act.activation(Ko[HD:P, 0, :], krt[HD:P, :], ACT.Copy).then_inc(q["k_hi"], 1)
                        name = f"bqn{p}"
                        act.wait_ge(q["ch_done"], C[name] + 1)
                        act.activation(Qe[0:HD, 0, :], chunk_ps(name)[0:HD, :], ACT.Copy).then_inc(q["q_hi"], 1)
                        act.activation(Qo[HD:P, 0, :], chunk_ps(name)[HD:P, :], ACT.Copy).then_inc(q["q_hi"], 1)

                    def b_exp(u):
                        act.wait_ge(q["bm_ok"], u + 1)
                        if u >= 2:
                            act.wait_ge(q["bt_mm"], 2 * u - 2)
                        elif u == 0:
                            act.wait_ge(q["qr_lo"], 1)
                        act.activation(Pb[:, u % 2, :], pair(u), ACT.Exp, bias=bnb[:, u:u + 1],
                                       scale=rsq[:, u % NT:u % NT + 1], accum_out=bsm[:, u:u + 1]).then_inc(q["be_ok"], 1)

                    def b_hi(u):
                        w = u // 2
                        if w >= 2:
                            act.wait_ge(q["bo_mm"], w - 1)
                        for half in range(2):
                            act.wait_ge(q["bt_mm"], 2 * u + half + 1)
                            act.activation(PTb[:, w % 2, 0, half * NT // 2:(half + 1) * NT // 2, u % 2 * P:(u % 2 + 1) * P],
                                           ps[:, 4 + half, :].rearrange("p (k t) -> p k t", t=P), ACT.Copy
                                           ).then_inc(q["bpt_hi"], 1)

                    def b_half(w):
                        h = 2 * w // NT
                        act.wait_ge(q["bo_mm"], w + 1)
                        if w >= 2:
                            act.wait_ge(q["bo_ok"], w - 1)
                        r, o = ((0, HD), (HD, 0))[h % 2]
                        b = ps[:, 6 + w % 2, :]
                        act.activation(tmpB[r:r + HD, w % 2, :], b[o:o + HD, 0:256], ACT.Copy)
                        act.activation(rbB[r:r + HD, w % 2, :], b[r:r + HD, 256:512], ACT.Copy).then_inc(q["bo_tmp"], 1)

                    def cat_hi(n):
                        if n >= 2:
                            act.wait_ge(q["o_mm"], n - 1)
                        act.activation(catR[:, n % 2, 0, :, :], cat[:, :, n * P:(n + 1) * P], ACT.Copy).then_inc(q["chi2"], 1)

                    head_hi(0)
                    for i in range(NB + 4):
                        if i == 2 * NT:
                            head_hi(1)
                        if 1 <= i <= NB:
                            b_hi(i - 1)
                        if i < NB:
                            b_exp(i)
                        if i >= 5 and i % 2 == 1:
                            b_half((i - 5) // 2)
                        if i in W_OUT_AT:
                            split_hi(f"w_out{W_OUT_AT[i]}")
                    act.wait_ge(q["bo_mm"], NB // 2)
                    for k in range(EARLY, EARLY + 2):
                        split_hi(f"w_out{k}")
                    act.wait_ge(q["bo_ok"], NB // 2)
                    cat_hi(0)
                    for k in range(EARLY + 2, KD):
                        split_hi(f"w_out{k}")
                    cat_hi(1)
                    for n in range(NT):
                        if n >= 1 and n + 1 < NT:
                            cat_hi(n + 1)
                        act.wait_ge(q["o_mm"], n + 1)
                        if n >= 1:
                            act.wait_ge(q["osq_ok"], n)
                        act.activation(junk[:, :], pair(n), ACT.Square, accum_out=oss[:, n:n + 1]).then_inc(q["osq_ok"], 1)

                @block.vector
                def _(dve):
                    own = Chain(dve, q["own_dve"])
                    conv = Chain(dve, q["conv_own"])
                    tt, ts, stt = dve.tensor_tensor, dve.tensor_scalar, dve.scalar_tensor_tensor
                    bank45 = ps[:, 4:6, :].rearrange("p b n -> p (b n)")

                    def minus(dst, a, hi):
                        return tt(dst, a, hi.bitcast(F32), ALU.subtract)

                    def norm_x(n):
                        dve.wait_ge(q["rs_ok"], n + 1)
                        stt(x_tile(n), x_tile(n), rs[:, n:n + 1], gpre[:, :],
                            ALU.mult, ALU.mult).then_inc(q["xn_ok"], 1)

                    def h_lo(n):
                        dve.wait_ge(q["hhi"], n + 1)
                        b = 4 + 2 * (n % 2)
                        minus(hT[:, 1, :, n * P:(n + 1) * P],
                              ps[:, b:b + 2, :].rearrange("p b (k t) -> p (b k) t", t=P),
                              hT[:, 0, :, n * P:(n + 1) * P]).then_inc(q["hlo"], 1)

                    def split_lo(name):
                        i = POS[name]
                        dve.wait_ge(q["whi"], i + 1)
                        src = raw[:, i % RAWS, :]
                        if name in CHUNKS:
                            s_ = stat[:, C[name] % STATS]
                            minus(s_[:, 1, :, :], src.rearrange("p (k m) -> p k m", m=P), s_[:, 0, :, :]).then_inc(q["wlo"], 1)
                        elif name == "w_pw":
                            minus(wpR[:, 1, :, :], src[:, 0:2 * GW].rearrange("p (k m) -> p k m", m=GW), wpR[:, 0, :, :]).then_inc(q["wlo"], 1)
                        elif name == "w_q":
                            minus(wup[:, 1, 0:2, :], src.rearrange("p (k m) -> p k m", m=512), wup[:, 0, 0:2, :]).then_inc(q["wlo"], 1)
                        elif name == "w_kv":
                            minus(wup[:, 1, 2, :], src[:, 0:512], wup[:, 0, 2, :]).then_inc(q["wlo"], 1)
                        else:
                            k = int(name[5:])
                            minus(woR[k][:, 1, :], src, woR[k][:, 0, :]).then_inc(q["wlo"], 1)

                    def gate(name):
                        dve.wait_ge(q["th_ok"], TH[name])
                        stt(cat[:, CAT[name], :], th[:, :], 1.0, chunk_ps(name), ALU.add, ALU.mult
                            ).then_inc(q["th_used"], 1)

                    def evacuate(name):
                        kind, j = name.rstrip("01"), int(name[-1]) if name[-1].isdigit() else 0
                        if kind == "cva":
                            dve.wait_ge(q["ch_done"], C[name] + 1)
                            dve.wait_ge(q["th_ok"], TH[f"cvb{j}"])
                            stt(uC[:, j, PAD_C:PAD_C + T], th[:, :], 1.0, chunk_ps(name), ALU.add, ALU.mult
                                ).then_inc(q["th_used"], 1)
                        elif kind == "ah":
                            dve.wait_ge(q["ch_done"], C[name] + 1)
                            dve.wait_ge(*free_at(f"ac{j}"))
                            tt(aU[:, 1:T + 1], chunk_ps(name), aC[:, :], ALU.mult).then_inc(free_at(name)[0], 1)
                            dve.wait_ge(*free_at(name))
                            own.wait()
                            w = P_AW + TAPS_A * j
                            own.add(ts(aC[:, :], aU[:, 0:T], parT[:, w:w + 1], parT[:, P_AB + j:P_AB + j + 1], ALU.mult, ALU.add))
                            for t in range(1, TAPS_A):
                                own.wait()
                                own.add(stt(aC[:, :], aU[:, t:t + T], parT[:, w + t:w + t + 1], aC[:, :], ALU.mult, ALU.add))
                        elif kind == "ab":
                            dve.wait_ge(q["ch_done"], C[name] + 1)
                            own.wait()
                            tt(aC[:, :], chunk_ps(name), aC[:, :], ALU.mult).then_inc(free_at(name)[0], 1)
                        elif kind == "ag":
                            dve.wait_ge(q["th_ok"], TH[name])
                            own.add(stt(cat[:, CAT[name], :], th[:, :], 1.0, chunk_ps(name), ALU.add, ALU.mult))
                            own.wait()
                            dve.wait_ge(*free_at(f"ab{j}"))
                            stt(cat[:, CAT[name], :], cat[:, CAT[name], :], 0.5, aC[:, :], ALU.mult, ALU.mult
                                ).then_inc(q["th_used"], 1)
                        elif kind[1:] == "g":
                            gate(name)

                    def conv_taps(taps):
                        for t in taps:
                            for j in range(2):
                                w = parT[:, P_CW + TAPS_C * j + int(t):P_CW + TAPS_C * j + int(t) + 1]
                                if t == 0:
                                    conv.add(ts(accC[:, j, :], uC[:, j, 0:T], w, None, ALU.mult))
                                else:
                                    conv.wait(conv.n - 1)
                                    conv.add(stt(accC[:, j, :], uC[:, j, int(t):int(t) + T], w, accC[:, j, :],
                                                 ALU.mult, ALU.add))

                    for n in range(NT + 1):
                        if n < NT:
                            norm_x(n)
                        if n == 2:
                            split_lo(CHUNKS[0])
                            split_lo(CHUNKS[1])
                        if n >= 1:
                            h_lo(n - 1)
                    own.add(dve.memset(aU[:, 0:1], 0.0))
                    own.add(dve.memset(aU[:, T + 1:T + 2], 0.0))
                    own.add(dve.memset(uC[:, :, 0:PAD_C], 0.0))
                    own.add(dve.memset(uC[:, :, PAD_C + T:UP], 0.0))
                    own.add(ts(ngs[:, :], parT[:, P_SINK:P_SINK + HEADS], -1.0, None, ALU.mult))

                    ahead = [n for n in RAW if n in CHUNKS or n == "w_pw"][2:]
                    for c, name in enumerate(CHUNKS):
                        if ahead:
                            split_lo(ahead.pop(0))
                            if ahead and ahead[0] == "w_pw":
                                split_lo(ahead.pop(0))
                        evacuate(name)
                        if c in CONV_STEPS:
                            if c == C["cg0"]:
                                dve.wait_ge(*free_at("cva0"))
                                dve.wait_ge(*free_at("cva1"))
                                own.wait()
                            conv_taps(CONV_STEPS[c])
                        if name == "ag1":
                            conv.wait()
                            for j in range(2):
                                ts(accC[:, j, :], accC[:, j, :], 0.5, parT[:, P_CB + j:P_CB + j + 1],
                                   ALU.mult, ALU.add).then_inc(q["conv_ok"], 1)
                        if name == "bq0":
                            dve.wait_ge(q["st_cp"], 1)
                            ts(mcol[:, :], ps[:, 6, 0:NT], 1.0 / GW, None, ALU.mult).then_inc(q["mcol_ok"], 1)
                        if name == "bq1":
                            dve.wait_ge(q["st_cp"], 2)
                            for j in range(2):
                                tt(accC[:, j, :], accC[:, j, :], bank45, ALU.subtract).then_inc(q["xc_ok"], 1)
                            dve.wait_ge(q["st_b"], 1)
                            ts(bvar[:, 0:NT], ps[:, 7, 0:NT], 1.0 / QR, EPS, ALU.mult, ALU.add).then_inc(q["bstat_ok"], 1)
                        if name == "bkv":
                            dve.wait_ge(q["st_cp"], 3)
                            ts(cvar[:, :], ps[:, 6, 16:16 + NT], 1.0 / GW, EPS, ALU.mult, ALU.add).then_inc(q["cvar_ok"], 1)
                            dve.wait_ge(q["st_b"], 2)
                            dve.wait_ge(q["bstat_ok"], 1)
                            stt(bvar[:, 0:NT], ps[:, 7, NT:2 * NT], 1.0 / QR, bvar[:, 0:NT], ALU.mult, ALU.add
                                ).then_inc(q["bstat_ok"], 1)
                        if name == "bg0":
                            dve.wait_ge(q["st_cp"], 4)
                            dve.wait_ge(q["xsq_ok"], 2)
                            for j in range(2):
                                own.add(tt(accC[:, j, :], accC[:, j, :], bank45, ALU.mult))
                            for j in range(2):
                                own.wait(own.n - 1 + j)
                                ts(accC[:, j, :], accC[:, j, :], parT[:, P_LG + j:P_LG + j + 1],
                                   parT[:, P_LB + j:P_LB + j + 1], ALU.mult, ALU.add).then_inc(q["y_ok"], 1)
                            dve.wait_ge(q["st_b"], 3)
                            ts(bvar[:, 2 * NT:3 * NT], ps[:, 7, 2 * NT:3 * NT], 1.0 / KVR, EPS, ALU.mult, ALU.add
                               ).then_inc(q["bstat_ok"], 1)
                            for j in range(2):
                                dve.wait_ge(q["th_ok"], TH[f"cz{j}"])
                                stt(accC[:, j, :], th[:, :], 1.0, accC[:, j, :], ALU.add, ALU.mult
                                    ).then_inc(q["th_used"], 1)
                            for j in range(2):
                                dve.wait_ge(q["chi_ok"], j + 1)
                                minus(cLo[:, j, :], accC[:, j, :], cHi[:, j, :]).then_inc(q["clo_ok"], 1)

                    dve.wait_ge(*free_at("bq1"))
                    k_r, k_s = slice(HD, HD + ROPE), slice(HD + ROPE, P)
                    dve.wait_ge(q["lat_hi"], 3)
                    for j, rows, dst in ((0, P, qlR[:, 0, :, :]), (1, QR - P, qlR[0:QR - P, 1, :, :]), (2, P, kvR[:, :, :])):
                        stt(dst[:, 1, :], rawB[0:rows, j, :], parT[0:rows, P_GQ + j:P_GQ + j + 1],
                            dst[:, 0, :].bitcast(F32), ALU.mult, ALU.subtract).then_inc(q["lat_lo"], 1)
                    for m in range(2):
                        dve.wait_ge(q["ch_done"], C[f"pw{m}"] + 1)
                        dve.wait_ge(*free_at(f"cg{m}"))
                        stt(cat[:, 4 + m, :], chunk_ps(f"pw{m}"), 0.25, cat[:, 4 + m, :], ALU.mult, ALU.mult
                            ).then_inc(free_at(f"pw{m}")[0], 1)
                    own.add(tt(krt[k_r, :], rawB[k_s, 1, :], ropeT[k_s, 1, :], ALU.mult))
                    own.add(tt(rawB[k_r, 1, :], rawB[k_r, 1, :], ropeT[k_r, 0, :], ALU.mult))
                    own.wait()
                    tt(rawB[k_r, 1, :], rawB[k_r, 1, :], krt[k_r, :], ALU.add).then_inc(q["kr_ok"], 1)
                    for h in range(HEADS):
                        r = HD * (h % 2)
                        dve.wait_ge(q["dst_hi"], h + 1)
                        minus(Qst[HD - r:P - r, h, :], rawD[r:r + HD, h // 2, :], Qst[r:r + HD, h, :]).then_inc(q["dst_lo"], 1)
                    dve.wait_ge(q["dst_hi"], 8)
                    for kv in range(2):
                        r = HD * kv
                        for r2 in range(0, P, HD):
                            minus(Kst[r2:r2 + HD, kv, 1, :], rawD[r:r + HD, 2, :], Kst[r:r + HD, kv, 0, :]).then_inc(q["dst_lo"], 1)
                    dve.wait_ge(q["vd_hi"], 1)
                    minus(Vd[:, :, :, 1, :], chunk_ps("dv_t").rearrange("p (t v d) -> p t v d", t=NT, v=2),
                          Vd[:, :, :, 0, :]).then_inc(q["vd_lo"], 1)
                    dve.wait_ge(q["ke_hi"], 1)
                    minus(Ke[k_r, 1, :], rawB[k_r, 1, :], Ke[k_r, 0, :]).then_inc(q["ke_lo"], 1)
                    dve.memset(Ko[0:ROPE, :, :].bitcast(F32), 0.0).then_inc(q["zero_ok"], 1)
                    dve.memset(Qo[0:ROPE, :, :].bitcast(F32), 0.0).then_inc(q["zero_ok"], 1)
                    split_lo("w_q")
                    split_lo("w_kv")

                    def d_max(u):
                        n, kv = DU[u]
                        k0, nk, b0 = keys(n)
                        s2 = 2 * (u % 2)
                        dve.wait_ge(q["ds_mm"], u + 1)
                        if u >= 2:
                            dve.wait_ge(q["dt_mm"], u - 1)
                        stt(Pd[:, u % 2, :, 0:nk * P], ps[:, s2:s2 + 2, 0:nk * P], D_SCALE,
                            bias[:, 2 * kv:2 * kv + 2, b0:b0 + nk * P], ALU.mult, ALU.add).then_inc(q["ds_ok"], 1)
                        dve.wait_ge(q["ds_ok"], u + 1)
                        own.add(dve.tensor_reduce(dmx[:, s2:s2 + 2], Pd[:, u % 2, :, 0:nk * P], AX.X, ALU.max))
                        own.wait()
                        own.add(stt(dnm[:, s2:s2 + 2], dmx[:, s2:s2 + 2], -1.0, ngs[:, 2 * kv:2 * kv + 2], ALU.mult, ALU.min))
                        own.wait()
                        tt(des[:, s2:s2 + 2], dnm[:, s2:s2 + 2], parT[:, P_SINK + 2 * kv:P_SINK + 2 * kv + 2],
                           ALU.add).then_inc(q["dm_ok"], 1)

                    def d_recip(u):
                        s2 = 2 * (u % 2)
                        dve.wait_ge(q["de_ok"], u + 1)
                        own.add(tt(dsm[:, s2:s2 + 2], dsm[:, s2:s2 + 2], dex[:, s2:s2 + 2], ALU.add))
                        own.wait()
                        dve.reciprocal(drc[:, s2:s2 + 2], dsm[:, s2:s2 + 2]).then_inc(q["dr_ok"], 1)

                    def d_lo(u):
                        n, kv = DU[u]
                        _, nk, _ = keys(n)
                        dve.wait_ge(q["dpt_hi"], u + 1)
                        minus(PTd[:, u % 2, 1, 0:nk * 2 * P], bank45[:, 0:nk * 2 * P],
                              PTd[:, u % 2, 0, 0:nk * 2 * P]).then_inc(q["dpt_lo"], 1)

                    def d_combine(u):
                        n, kv = DU[u]
                        dve.wait_ge(q["do_tmp"], u + 1)
                        b, t = ps[:, 6 + u % 2, :], tmpD[:, u % 2, :]
                        own.add(tt(t[0:HD, :], b[0:HD, 0:P], t[0:HD, :], ALU.add))
                        own.add(tt(t[HD:P, :], b[HD:P, P:2 * P], t[HD:P, :], ALU.add))
                        own.wait()
                        y_ = cat[:, 6 + kv, n * P:(n + 1) * P]
                        stt(y_, t, 0.5, y_, ALU.mult, ALU.mult).then_inc(q["do_ok"], 1)

                    NU = len(DU)
                    for i in range(NU + 3):
                        if i < NU:
                            d_max(i)
                        if 1 <= i <= NU:
                            d_lo_u = i - 1
                        if i < NU:
                            d_recip(i)
                        if 1 <= i <= NU:
                            d_lo(d_lo_u)
                        if 2 <= i <= NU + 1:
                            d_combine(i - 2)

                    for n in range(NT):
                        name = ("bv0", "bv1")[2 * n // NT]
                        i = n % (NT // 2)
                        dve.wait_ge(q["vb_hi"], (n | 1) + 1)
                        stt(Vb[:, n, :, 1, :], chunk_ps(name)[:, i * GW:(i + 1) * GW].rearrange("p (h d) -> p h d", d=HD),
                                brs[:, NT + n:NT + n + 1], Vb[:, n, :, 0, :].bitcast(F32), ALU.mult, ALU.subtract
                                ).then_inc(q["vb_lo"], 1)
                    dve.wait_ge(q["ch_done"], C["rope"] + 1)
                    tt(qrF[:, 0, :], chunk_ps("rope"), ropeT[:, 0, :], ALU.mult).then_inc(free_at("rope")[0], 1)
                    dve.wait_ge(q["ch_done"], C["rope_sw"] + 1)
                    tt(qrF[:, 1, :], chunk_ps("rope_sw"), ropeT[:, 1, :], ALU.mult).then_inc(free_at("rope_sw")[0], 1)
                    dve.wait_ge(*free_at("rope"))
                    dve.wait_ge(*free_at("rope_sw"))
                    tt(qrF[:, 0, :], qrF[:, 0, :], qrF[:, 1, :], ALU.add).then_inc(q["qr_ok"], 1)
                    dve.wait_ge(q["qr_hi"], 1)
                    minus(qrR[:, 1, :], qrF[:, 0, :], qrR[:, 0, :]).then_inc(q["qr_lo"], 1)
                    dve.wait_ge(q["qr_lo"], 1)

                    def head_lo(p):
                        name = f"bk{p}"
                        dve.wait_ge(q["ch_done"], C[name] + 1)
                        if p:
                            dve.wait_ge(q["k_lo"], 2)
                        else:
                            own.wait()
                            dve.wait_ge(q["kr_ok"], 1)
                            dve.wait_ge(*free_at("bcast_kv"))
                        tt(krt[:, :], chunk_ps(name), rbc[:, :], ALU.mult).then_inc(q["kt_ok"], 1)
                        for j, h in enumerate((2 * p, 2 * p + 1)):
                            Q, r = ((Qe, HD), (Qo, ROPE))[j]
                            dve.tensor_copy(Q[r:r + ROPE, :, :], qrR[ROPE * h:ROPE * (h + 1), :, :].bitcast(F32)).then_inc(q["qrope_ok"], 1)
                        for j, (rows, Kk) in enumerate(((slice(0, HD), Ke), (slice(HD, P), Ko))):
                            dve.wait_ge(q["k_hi"], 2 * p + j + 1)
                            minus(Kk[rows, 1, :], krt[rows, :], Kk[rows, 0, :]).then_inc(q["k_lo"], 1)
                        name = f"bqn{p}"
                        for j, (rows, Q) in enumerate(((slice(0, HD), Qe), (slice(HD, P), Qo))):
                            dve.wait_ge(q["q_hi"], 2 * p + j + 1)
                            minus(Q[rows, 1, :], chunk_ps(name)[rows, :], Q[rows, 0, :]).then_inc(q["q_lo"], 1)

                    def b_max(u):
                        dve.wait_ge(q["bs_mm"], u + 1)
                        own.add(dve.tensor_reduce(bmx[:, u:u + 1], pair(u), AX.X, ALU.max))
                        own.wait()
                        ts(bnb[:, u:u + 1], bmx[:, u:u + 1], rsq[:, u % NT:u % NT + 1], -1.0,
                           ALU.mult, ALU.mult).then_inc(q["bm_ok"], 1)

                    def b_lo(u):
                        w = u // 2
                        for half in range(2):
                            dve.wait_ge(q["bpt_hi"], 2 * u + half + 1)
                            dst = PTb[:, w % 2, :, half * NT // 2:(half + 1) * NT // 2, u % 2 * P:(u % 2 + 1) * P]
                            minus(dst[:, 1], ps[:, 4 + half, :].rearrange("p (k t) -> p k t", t=P), dst[:, 0]
                                  ).then_inc(q["bpt_lo"], 1)

                    def b_recip(u):
                        dve.wait_ge(q["be_ok"], u + 1)
                        dve.reciprocal(brc[:, u:u + 1], bsm[:, u:u + 1]).then_inc(q["br_ok"], 1)

                    def b_combine(w):
                        h, i = divmod(2 * w, NT)
                        dve.wait_ge(q["bo_tmp"], w + 1)
                        r = HD * (h % 2)
                        rows = slice(r, r + HD)
                        b, t = ps[:, 6 + w % 2, :], tmpB[rows, w % 2, :]
                        own.add(tt(t, b[rows, 0:256], t, ALU.add))
                        own.wait()
                        own.add(tt(t, t, rbB[rows, w % 2, :], ALU.mult))
                        own.wait()
                        y_ = cat[rows, 2 + h // 2, i * P:(i + 2) * P]
                        stt(y_, t, 0.5, y_, ALU.mult, ALU.mult).then_inc(q["bo_ok"], 1)

                    def cat_lo(n):
                        dve.wait_ge(q["chi2"], n + 1)
                        minus(catR[:, n % 2, 1, :, :], cat[:, :, n * P:(n + 1) * P], catR[:, n % 2, 0, :, :]).then_inc(q["clo2"], 1)

                    head_lo(0)
                    for i in range(NB + 4):
                        if i == 2 * NT:
                            head_lo(1)
                        if i < NB:
                            b_max(i)
                        if 1 <= i <= NB:
                            b_recip(i - 1)
                            b_lo(i - 1)
                        if i >= 5 and i % 2 == 1:
                            b_combine((i - 5) // 2)
                        if i in W_OUT_AT:
                            split_lo(f"w_out{W_OUT_AT[i]}")

                    for k in range(EARLY, EARLY + 2):
                        split_lo(f"w_out{k}")
                    cat_lo(0)
                    for k in range(EARLY + 2, KD):
                        split_lo(f"w_out{k}")
                    cat_lo(1)
                    dve.wait_ge(q["gpost_ld"], 16)
                    for n in range(NT):
                        if n >= 1 and n + 1 < NT:
                            cat_lo(n + 1)
                        dve.wait_ge(q["osq_ok"], n + 1)
                        ts(oss[:, n:n + 1], oss[:, n:n + 1], 1.0 / D, EPS, ALU.mult, ALU.add).then_inc(q["ovar_ok"], 1)
                        dve.wait_ge(q["ors_ok"], n + 1)
                        stt(pair(n), pair(n), ors[:, n:n + 1], gvec[:, :], ALU.mult, ALU.mult).then_inc(q["o1_ok"], 1)
                        dve.wait_ge(q["o1_ok"], n + 1)
                        dve.wait_ge(*residual_landed(n))
                        tt(xs[:, n % XS, :], xs[:, n % XS, :], pair(n), ALU.add).then_inc(q["o2_ok"], 1)

            nc.all_engine_barrier()
            nc.sync.sem_clear(range(per_pass[0].num, per_pass[-1].num + 1))
            nc.all_engine_barrier()


def _buckets(rel):
    half = BUCKETS // 2
    exact = half // 2
    n = np.abs(rel)
    large = exact + (np.log(np.maximum(n, 1) / exact) / math.log(MAX_DIST / exact) * (half - exact)).astype(np.int32)
    large = np.minimum(large, half - 1)
    return (rel > 0).astype(np.int32) * half + np.where(n < exact, n, large).astype(np.int32)


def _constants():
    dist = np.arange(512) - 255
    onehot = (np.arange(BUCKETS)[:, None] == _buckets(dist)[None, :]).astype(np.float32)
    band = np.broadcast_to(np.where(np.abs(dist) <= WINDOW, 0.0, NEG).astype(np.float32), (HEADS, 512))
    inv = np.float32(10000.0) ** (-np.arange(0, ROPE, 2, dtype=np.float32) / np.float32(ROPE))
    ang = np.arange(T, dtype=np.float32)[None, :] * inv[:, None]
    cos, sin = np.cos(ang), np.sin(ang)
    rope = np.stack([np.tile(np.concatenate([cos, cos]), (4, 1)), np.tile(np.concatenate([-sin, sin]), (4, 1))])
    return onehot, np.ascontiguousarray(band), rope.astype(np.float32)


def _columns():
    sizes = [GW, GW, GW, GW, QR, KVR, ROPE, GW, GW, GW, GW, HEADS * HD, 2 * HD, 2 * HD, GW]
    names = ["ab", "ac", "ah", "ag", "bq", "bkv", "bkr", "bg", "cva", "cvb", "cg", "dq", "dk", "dv", "dg"]
    start = dict(zip(names, np.cumsum([0] + sizes[:-1])))
    out = []
    for name in CHUNKS:
        kind, j = name.rstrip("01"), int(name[-1]) if name[-1].isdigit() else 0
        if name == "bq1":
            kr = start["bkr"] + np.arange(ROPE)
            out.append(np.concatenate([start["bq"] + np.arange(P, QR), kr, np.roll(kr, -(ROPE // 2))]))
        else:
            out.append(start[kind] + j * P + np.arange(P))
    return np.stack(out)


def _q_columns():
    h = np.arange(HEADS)[:, None] * (NOPE + ROPE)
    rot = NOPE + np.arange(ROPE)
    return np.concatenate([(h + np.arange(NOPE)).ravel(), (h + rot).ravel(), (h + np.roll(rot, -(ROPE // 2))).ravel()])


def _kv_columns():
    h = np.arange(HEADS)[:, None] * 2 * HD
    return np.concatenate([(h + np.arange(HD)).ravel(), (h + HD + np.arange(HD)).ravel()])


def kernel(x_prompt, x_sample, g_pre, g_post, w_in, w_out, conv_a_w, conv_a_b, mla_g_q, mla_w_q_up,
           mla_g_kv, mla_w_kv_up, conf_w_dw, conf_b_dw, conf_ln_g, conf_ln_b, conf_w_pw, swa_sink, rel_bias):
    import concourse.bacc as bacc
    from concourse.bass_utils import run_bass_kernel_spmd as run

    (x_prompt, x_sample, g_pre, g_post, w_in, w_out, conv_a_w, conv_a_b, mla_g_q, mla_w_q_up, mla_g_kv,
     mla_w_kv_up, conf_w_dw, conf_b_dw, conf_ln_g, conf_ln_b, conf_w_pw, swa_sink, rel_bias) = map(np.asarray, (
         x_prompt, x_sample, g_pre, g_post, w_in, w_out, conv_a_w, conv_a_b, mla_g_q, mla_w_q_up, mla_g_kv,
         mla_w_kv_up, conf_w_dw, conf_b_dw, conf_ln_g, conf_ln_b, conf_w_pw, swa_sink, rel_bias))

    def blocks(a):
        return a.reshape(L, -1, 2, P).transpose(0, 3, 2, 1).reshape(L, P, -1)

    gq = np.zeros((L, 2 * P), np.float32)
    gq[:, :QR] = mla_g_q
    par = np.concatenate([
        blocks(conv_a_w), blocks(conv_a_b), blocks(conf_w_dw), blocks(conf_b_dw), blocks(conf_ln_g),
        blocks(conf_ln_b), blocks(gq), mla_g_kv[:, :, None],
        np.broadcast_to(swa_sink[:, None, :], (L, P, HEADS))], axis=2)
    wq = np.zeros((L, 2 * P, 512), np.float32)
    wq[:, :QR] = mla_w_q_up[:, :, _q_columns()]
    onehot, band, rope = _constants()
    arrays = {
        "x": np.concatenate([x_prompt, x_sample]),
        "w_in": w_in[:, :, _columns()].reshape(L, KD, P, NC, P).transpose(0, 3, 2, 1, 4).reshape(L, NC, P, D),
        "w_out": w_out,
        "w_q": wq.reshape(L, 2, P, 512).transpose(0, 2, 1, 3).reshape(L, P, 1024),
        "w_kv": mla_w_kv_up[:, :, _kv_columns()],
        "w_pw": conf_w_pw.reshape(L, 2, P, GW).transpose(0, 2, 1, 3).reshape(L, P, 2 * GW),
        "par": par, "g_pre": g_pre, "g_post": g_post, "rel_bias": rel_bias,
        "onehot": onehot, "band": band, "rope": rope,
    }
    arrays = {n: np.ascontiguousarray(a) for n, a in arrays.items()}
    nc = bacc.Bacc("TRN2", target_bir_lowering=False, num_devices=1,
                   dynamic_dma_scratch_size=1024)
    ins = [nc.dram_tensor(n, a.shape, mybir.dt.from_np(a.dtype), kind="ExternalInput").ap() for n, a in arrays.items()]
    y = nc.dram_tensor("y", (S, T, D), F32, kind="ExternalOutput").ap()
    build(nc, *ins, y)
    out = run(nc, [arrays], core_ids=[0]).results[0]["y"]
    return out[0:1], out[1:2]
```

```python
import math
from contextlib import ExitStack

import numpy as np
import concourse.bass as bass
from concourse import mybir

F32 = mybir.dt.float32
F32R = mybir.dt.float32r
ACT = mybir.ActivationFunctionType
ALU = mybir.AluOpType
AX = mybir.AxisListType

P = 128
D = 1024
T = 1024
L = 2
S = 2
KD = D // P
NT = T // P
HALF = 512
GW = D // 4
HD = 64
HEADS = GW // HD
NOPE, ROPE = 64, 32
QR, KVR = 3 * D // 16, D // 8
TAPS_A, TAPS_C = 3, 31
PAD_C = (TAPS_C - 1) // 2
BUCKETS, WINDOW, MAX_DIST = 32, 128, 128
EPS = 1e-6
NEG = -1e30
EARLY = 4
B_SCALE = (NOPE + ROPE) ** -0.5
D_SCALE = HD ** -0.5

CHUNKS = ["dq0", "dq1", "dk", "dv", "dg0", "dg1",
          "cvb0", "cva0", "cvb1", "cva1", "cg0", "cg1",
          "ac0", "ah0", "ab0", "ag0", "ac1", "ah1", "ab1", "ag1",
          "bq0", "bq1", "bkv", "bg0", "bg1"]
C = {name: n for n, name in enumerate(CHUNKS)}
NC = len(CHUNKS)
LATER = ["dv_t", "pw0", "pw1", "bcast_kv", "bv0", "bv1", "rope", "rope_sw",
         "bk0", "bqn0"]
for _n, _name in enumerate(LATER):
    C[_name] = NC + _n
RAW = CHUNKS[:16] + ["w_pw"] + CHUNKS[16:] + ["w_q", "w_kv"] + [f"w_out{k}" for k in range(KD)]
POS = {name: n for n, name in enumerate(RAW)}
RAWS = 3
STATS = 3
XS = 4
XP = 2
TH = ["dg0", "dg1", "cvb0", "cvb1", "cg0", "cg1", "ag0", "ag1", "bg0", "cz0", "cz1", "bg1"]
TH = {name: n + 1 for n, name in enumerate(TH)}
CAT = {"ag0": 0, "ag1": 1, "bg0": 2, "bg1": 3, "cg0": 4, "cg1": 5, "dg0": 6, "dg1": 7}

P_AW, P_AB = 0, 2 * TAPS_A
P_CW = P_AB + 2
P_CB = P_CW + 2 * TAPS_C
P_LG, P_LB = P_CB + 2, P_CB + 4
P_GQ, P_GKV = P_CB + 6, P_CB + 8
P_SINK = P_GKV + 1
P_N = P_SINK + HEADS


NB = HEADS * NT
HEAD_AT = {NT + 2: 2, NT + 3: 2, 2 * NT + 2: 3, 2 * NT + 3: 3}
K_AT = {name: (kv, r) for name, (kv, r) in zip(CHUNKS[3:], [(0, 0), (0, HD), (1, HD), (1, 0)])}
LAT_AT = {3: 0, 4: 1, 5: 2}
KE_AT = 6
UP_AT = {10: "w_q", 11: "w_kv"}
W_OUT_AT = {NB * 5 // 8 + 2 * k: k for k in range(EARLY)}


class Chain:

    def __init__(self, eng, sem):
        self.eng, self.sem, self.n = eng, sem, 0

    def add(self, ins):
        self.n += 1
        ins.then_inc(self.sem, 1)
        return self.n

    def wait(self, n=None):
        n = self.n if n is None else n
        if n > 0:
            self.eng.wait_ge(self.sem, n)


def build(nc, x, w_in, w_out, w_q, w_kv, w_pw, par, g_pre, g_post, rel_bias, onehot, band, rope, y):
    with ExitStack() as ctx:
        base = nc.sbuf_base
        top = [(base + 63) // 64 * 64]

        def region(kb):
            at = top[0]
            top[0] += int(kb * 1024)
            assert top[0] <= nc.sbuf_usable_end, (top[0], nc.sbuf_usable_end)
            return at

        def at(name, shape, dt, addr):
            return nc.alloc_sbuf_tensor_at(name, shape, dt, offset=addr)

        def sem(name):
            return ctx.enter_context(nc.semaphore(name))

        r_big = region(64)
        r_cat = region(32)
        r_stat = region(24)
        r_raw = region(12)
        r_x = region(16)
        r_u = region(8.25)
        r_d = region(16)
        r_b = region(12)
        r_bias = region(6)
        r_rope = region(8)
        r_g = region(4)
        r_pw = region(4)
        r_small = region(3)
        r_xp = region(4 * XP)
        r_gpre = region(4)

        K = 1024
        hT = at("hT", [P, 2, KD, T], F32R, r_big)
        woR = [at(f"woR{k}", [P, 2, D], F32R, a) for k, a in enumerate(
            [r_b, r_u, r_big + 56 * K, r_stat + 16 * K] + [r_big + 8 * K * k for k in range(KD - EARLY)])]
        Qst = at("Qst", [P, HEADS, T], F32R, r_big)
        Kst = [[at(f"Kst{kv}{part}", [P, T], F32R, a) for part, a in enumerate(places)]
               for kv, places in enumerate(((r_xp, r_xp + 4 * K), (r_g, r_gpre)))]
        Vd = at("Vd", [P, NT, 2, 2, HD], F32R, r_big + 32 * K)
        Pd = at("Pd", [P, 2, 2, 384], F32, r_big + 40 * K)
        PTd = at("PTd", [P, 3, 2, 768], F32R, r_big + 46 * K)
        Vb = at("Vb", [P, NT, HEADS, 2, HD], F32R, r_big)
        PTb = at("PTb", [P, 2, 2, NT, 256], F32R, r_big + 16 * K)
        Pb = at("Pb", [P, 2, T], F32, r_big + 48 * K)
        qrF = at("qrF", [P, 2, T], F32, r_big + 48 * K)
        qrR = at("qrR", [P, 2, T], F32R, r_big + 56 * K)
        cat = at("cat", [P, KD, T], F32, r_cat)
        stat = at("stat", [P, STATS, 2, KD, P], F32R, r_stat)
        catR = at("catR", [P, 2, 2, KD, P], F32R, r_stat)
        qlR = at("qlR", [P, 2, 2, T], F32R, r_stat)
        kvR = at("kvR", [P, 2, T], F32R, r_stat + 16 * K)
        raw = at("raw", [P, RAWS, 1024], F32, r_raw)
        xs = at("xs", [P, XS, D], F32, r_x)
        xp = at("xp", [P, XP, D], F32, r_xp)
        gpre = at("gpre", [P, D], F32, r_gpre)
        accC = at("accC", [P, 2, T], F32, r_x)
        cLo = at("cLo", [P, 2, T], F32R, r_x)
        th = at("th", [P, T], F32, r_x + 8 * K)
        aC = at("aC", [P, T], F32, r_x + 12 * K)
        Qo = at("Qo", [P, 2, T], F32R, r_x)
        Ko = at("Ko", [P, 2, T], F32R, r_x + 8 * K)
        UP = T + 2 * PAD_C + 2
        uC = at("uC", [P, 2, UP], F32, r_u)
        cHi = at("cHi", [P, 2, T], F32R, r_u)
        rbc = at("rbc", [P, T], F32, r_u)
        krt = at("krt", [P, T], F32, r_u + 4 * K)
        kF2 = at("kF2", [P, T], F32, r_stat + 16 * K)
        qF2 = at("qF2", [P, T], F32, r_stat)
        rawD = at("rawD", [P, 4, T], F32, r_d)
        Qe = at("Qe", [P, 2, T], F32R, r_d)
        Ke = at("Ke", [P, 2, T], F32R, r_d + 8 * K)
        rawB = at("rawB", [P, 3, T], F32, r_b)
        wup = at("wup", [P, 2, 3, 512], F32R, r_b)
        aU = at("aU", [P, T + 2], F32, r_b)
        bias = at("bias", [P, HEADS, 384], F32, r_bias)
        ropeT = at("ropeT", [P, 2, T], F32, r_rope)
        gvec = at("gvec", [P, D], F32, r_g)
        wpR = at("wpR", [P, 2, 2, GW], F32R, r_pw)

        small = [r_small]

        def sm(name, cols, dt=F32, rows=P):
            t = at(name, [rows, cols], dt, small[0])
            small[0] += (4 * cols + 31) // 32 * 32
            assert small[0] <= top[0]
            return t

        ident = sm("ident", P)
        ones = sm("ones", 2)
        expo = sm("expo", NT)
        parT = sm("parT", P_N)
        ss = sm("ss", NT)
        rs = sm("rs", NT)
        mcol = sm("mcol", NT)
        cvar = sm("cvar", NT)
        crs = sm("crs", NT)
        bvar = sm("bvar", 3 * NT)
        brs = sm("brs", 2 * NT)
        rsq = sm("rsq", NT)
        ngs = sm("ngs", HEADS)
        oss = sm("oss", NT)
        ors = sm("ors", NT)
        dmx = sm("dmx", 4)
        dnm = sm("dnm", 4)
        dsm = sm("dsm", 4 * NT)
        dex = sm("dex", 4 * NT)
        drc = sm("drc", 4 * NT)
        bmx = sm("bmx", NB)
        bnb = sm("bnb", NB)
        bsm = sm("bsm", NB)
        brc = sm("brc", NB)
        tmpD = at("tmpD", [P, 2, P], F32, r_pw)
        tmpB = at("tmpB", [P, 2, 256], F32, r_pw)
        rbB = at("rbB", [P, 2, 256], F32, r_pw + 2 * K)
        junk = at("junk", [P, D], F32, r_b + 8 * K)
        oh = at("oh", [BUCKETS, 512], F32, r_cat)
        rb = at("rb", [BUCKETS, HEADS], F32, r_cat + 2 * K)
        bandT = at("bandT", [HEADS, 512], F32, r_cat + 4 * K)
        bvec = at("bvec", [HEADS, 512], F32, r_cat + 6 * K)

        ps = ctx.enter_context(nc.psum_tensor("ps", [P, 8, 512], F32))
        vec_dram = nc.dram_tensor("bias_by_distance", (HEADS, P, 512), F32, kind="Internal")

        p_ld, p_st, p_rd, p_id, p_mm, p_bv = (sem(n) for n in ("p_ld", "p_st", "p_rd", "p_id", "p_mm", "p_bv"))
        with nc.Block() as block:
            @block.gpsimd
            def _(pool):
                pool.memset(ident[:, :], 0.0).then_inc(p_id, 1)
                pool.memset(ones[:, :], 1.0)
                pool.memset(expo[:, :], -0.5)
                pool.wait_ge(p_id, 1)
                pool.affine_select(out=ident[:, :], in_=ident[:, :], compare_op=ALU.not_equal, fill=1.0,
                                   base=0, pattern=[[-1, P]], channel_multiplier=1).then_inc(p_id, 1)

            @block.sync
            def _(sp):
                sp.dma_start(oh[:, :], onehot).then_inc(p_ld, 16)
                sp.dma_start(rb[:, :], rel_bias).then_inc(p_ld, 16)
                sp.dma_start(bandT[:, :], band).then_inc(p_ld, 16)
                sp.dma_start(ropeT[:, :, :], rope.rearrange("a p t -> p a t")).then_inc(p_rd, 16)
                sp.wait_ge(p_bv, 1)
                sp.dma_start(vec_dram.ap(), bvec[:, :].unsqueeze(1).broadcast_to([HEADS, P, 512])).then_inc(p_st, 16)
                sp.wait_ge(p_st, 16)
                sp.dma_start(bias[:, :, :], bass.AP(vec_dram, P - 1, [[511, P], [512 * P, HEADS], [1, 384]])
                             ).then_inc(p_rd, 16)
                for n in range(XP):
                    sp.dma_start(xp[:, n, :], x[0, n * P:(n + 1) * P, :]).then_inc(p_rd, 16)
                sp.dma_start(gpre[:, :], g_pre[0:1].broadcast_to([P, D])).then_inc(p_rd, 16)
                for i in range(RAWS):
                    sp.dma_start(raw[:, i, :], w_in[0, i]).then_inc(p_rd, 16)
                sp.dma_start(parT[:, :], par[0]).then_inc(p_rd, 16)
                sp.wait_ge(p_rd, 16 * (2 + XP + 1 + RAWS + 1))

            @block.tensor
            def _(pe):
                pe.wait_ge(p_ld, 48)
                pe.matmul(ps[0:HEADS, 0, :], rb[:, :], oh[:, :], start=True, stop=True).then_inc(p_mm, 1)

            @block.vector
            def _(dve):
                dve.wait_ge(p_mm, 1)
                dve.tensor_tensor(bvec[:, :], ps[0:HEADS, 0, :], bandT[:, :], ALU.add).then_inc(p_bv, 1)

        names = ("next_ld gpost_ld sq_ok rs_ok xn_ok xt_ok hhi hlo whi wlo ch_done th_ok th_used "
                 "pads_ok own_dve own_pool conv_own conv_ok st_cp mcol_ok xc_ok xsq_ok cvar_ok crs_ok y_ok "
                 "chi_ok clo_ok st_b bsq_ok bstat_ok brs_ok dst_hi dst_lo kd_hi kd_lo vd_hi vd_lo lat_hi lat_lo kr_ok "
                 "ke_hi ke_lo ko_ok zero_ok ds_mm ds_ok dm_ok de_ok dr_ok dt_mm dpt_hi dpt_lo do_mm do_tmp do_ok "
                 "rbc_ok vb_hi vb_lo qr_ok qr_hi qr_lo kt_ok k_hi k_lo q_hi q_lo qrope_ok up2 kf2_ok qf2_ok "
                 "bs_mm bm_ok be_ok br_ok bt_mm bpt_hi bpt_lo bo_mm bo_tmp bo_ok "
                 "chi2 clo2 o_mm osq_ok ovar_ok ors_ok o1_ok o2_ok "
                 "free0 free1").split()
        q = {n: sem(n) for n in names}
        x_ld = [sem(f"x_ld{i}") for i in range(XS)]
        y_st = [sem(f"y_st{i}") for i in range(XS)]
        w_ld = [sem(f"w_ld{i}") for i in range(RAWS)]
        per_pass = list(q.values()) + x_ld + y_st + w_ld

        read_by = {"dv_t": ("vd_lo", 1), "bv0": ("vb_lo", NT // 2), "bv1": ("vb_lo", NT)}
        read_by |= {"bk0": ("kt_ok", 1), "bqn0": ("q_lo", 2)}
        for p in range(2):
            read_by |= {f"cva{p}": ("th_used", TH[f"cvb{p}"]), f"cvb{p}": ("th_ok", TH[f"cvb{p}"])}
        read_by |= {name: ("th_used", TH[name]) for name in CAT}
        counts = [0, 0]
        by_number = {n: name for name, n in C.items()}
        for n in sorted(by_number):
            if by_number[n] not in read_by:
                counts[n % 2] += 1
                read_by[by_number[n]] = (f"free{n % 2}", counts[n % 2])

        def x_tile(n):
            return xp[:, n, :] if n < XP else xs[:, (n - XP) % XS, :]

        def x_landed(n):
            return x_ld[(n - XP) % XS], 16 * ((n - XP) // XS + 1)

        def residual_landed(n):
            before = len([m for m in range(XP, NT) if (m - XP) % XS == n % XS])
            return x_ld[n % XS], 16 * (before + n // XS + 1)

        def free_at(name):
            s_, value = read_by[name]
            return q[s_], value

        def pair(c):
            return ps[:, 2 * (c % 2):2 * (c % 2) + 2, :].rearrange("p b n -> p (b n)")

        def chunk_ps(name):
            return pair(C[name])

        def keys(n):
            k0, k1 = max(0, n - 1), min(NT - 1, n + 1)
            return k0, k1 - k0 + 1, (k0 - n + 1) * P

        DU = [(n, kv) for n in range(NT) for kv in range(2)]

        CONV_STEPS = {C["cg0"] + i: t for i, t in enumerate(
            np.array_split(np.arange(TAPS_C), C["bq0"] - C["cg0"]))}

        with nc.Fori(0, L) as layer:
          with nc.Fori(0, S) as seq:
            with nc.Block() as block:

                @block.sync
                def _(sp):
                    lay = bass.ds(layer, 1)
                    sq_ = bass.ds(seq, 1)

                    def load_g(src, s_):
                        sp.dma_start(gvec[:, :], src[lay].broadcast_to([P, D])).then_inc(s_, 16)

                    def load_x(src, n, slot):
                        sp.dma_start(xs[:, slot, :], src[sq_, n * P:(n + 1) * P, :]
                                     .rearrange("o p d -> (o p) d")).then_inc(x_ld[slot], 16)

                    def load_norm(src):
                        for n in range(XP, NT):
                            if n >= XP + XS:
                                sp.wait_ge(q["xt_ok"], n - XS + 1)
                            load_x(src, n, (n - XP) % XS)

                    def prefetch(src, seq_, lay_):
                        for n in range(XP):
                            sp.dma_start(xp[:, n, :], src[seq_, n * P:(n + 1) * P, :].rearrange("o p d -> (o p) d")
                                         ).then_inc(q["next_ld"], 16)
                        sp.dma_start(gpre[:, :], g_pre[lay_].broadcast_to([P, D])).then_inc(q["next_ld"], 16)
                        for i in range(RAWS):
                            sp.dma_start(raw[:, i, :], w_in[lay_, i].rearrange("o p n -> (o p) n")
                                         ).then_inc(q["next_ld"], 16)
                        sp.dma_start(parT[:, :], par[lay_].rearrange("o p c -> (o p) c")).then_inc(q["next_ld"], 16)

                    def load_raw(name):
                        i = POS[name]
                        if i >= RAWS:
                            sp.wait_ge(q["wlo"], i - RAWS + 1)
                        dst = raw[:, i % RAWS, :]
                        if name in CHUNKS:
                            src = w_in[lay, C[name]].rearrange("o p n -> (o p) n")
                        elif name == "w_pw":
                            dst, src = dst[:, 0:2 * GW], w_pw[lay].rearrange("o p n -> (o p) n")
                        elif name == "w_q":
                            src = w_q[lay].rearrange("o p n -> (o p) n")
                        elif name == "w_kv":
                            dst, src = dst[:, 0:512], w_kv[lay].rearrange("o p n -> (o p) n")
                        else:
                            k = int(name[5:])
                            src = w_out[lay, k * P:(k + 1) * P, :].rearrange("o p n -> (o p) n")
                        sp.dma_start(dst, src).then_inc(w_ld[i % RAWS], 16)

                    with sp.If(layer < 1):
                        load_norm(x)
                    with sp.Else():
                        load_norm(y)

                    for name in RAW[RAWS:]:
                        load_raw(name)
                    sp.wait_ge(q["ds_mm"], 2 * NT)
                    load_g(g_post, q["gpost_ld"])

                    def residual(src):
                        for n in range(NT):
                            if n < XS:
                                sp.wait_ge(q["bs_mm"], NB)
                            else:
                                sp.wait_ge(y_st[n % XS], 16)
                            load_x(src, n, n % XS)
                            if n >= 1:
                                store(n - 1)

                    def store(n):
                        sp.wait_ge(q["o2_ok"], n + 1)
                        sp.dma_start(y[sq_, n * P:(n + 1) * P, :].rearrange("o p d -> (o p) d"),
                                     xs[:, n % XS, :]).then_inc(y_st[n % XS], 16)

                    sp.wait_ge(q["wlo"], len(RAW))
                    with sp.If(seq < 1):
                        with sp.If(layer < 1):
                            prefetch(x, bass.ds(1, 1), lay)
                        with sp.Else():
                            prefetch(y, bass.ds(1, 1), lay)
                    with sp.Else():
                        prefetch(y, bass.ds(0, 1), bass.ds(L - 1, 1))
                    with sp.If(layer < 1):
                        residual(x)
                    with sp.Else():
                        residual(y)
                    store(NT - 1)
                    sp.wait_ge(q["next_ld"], 16 * (XP + 1 + RAWS + 1))
                    for i in range(XS):
                        sp.wait_ge(y_st[i], 16 * (NT // XS))

                @block.tensor
                def _(pe):
                    mm, tr = pe.matmul, pe.transpose
                    three = ((0, 0), (0, 1), (1, 0))

                    def x_transpose(n):
                        pe.wait_ge(q["xn_ok"], n + 1)
                        if n >= 2:
                            pe.wait_ge(q["hlo"], n - 1)
                        b = 4 + 2 * (n % 2)
                        for k in range(KD):
                            last = tr(ps[:, b + k // 4, k % 4 * P:(k % 4 + 1) * P],
                                      x_tile(n)[:, k * P:(k + 1) * P], ident[:, :])
                        last.then_inc(q["xt_ok"], 1)

                    def wait_pair(c):
                        if c >= 2:
                            pe.wait_ge(*free_at(by_number[c - 2]))

                    def project(name, halves=(0, 1)):
                        c = C[name]
                        pe.wait_ge(q["wlo"], POS[name] + 1)
                        wait_pair(c)
                        for k in range(KD):
                            for a, b in three:
                                for h in halves:
                                    last = mm(ps[:, 2 * (c % 2) + h, :], stat[:, c % STATS, a, k, :],
                                              hT[:, b, k, h * HALF:(h + 1) * HALF],
                                              start=(k == 0 and (a, b) == (0, 0)),
                                              stop=(k == KD - 1 and (a, b) == (1, 0)))
                        if halves[-1]:
                            last.then_inc(q["ch_done"], 1)

                    def column_sums(bank, col, parts):
                        for n in range(NT):
                            for j, t in enumerate(parts):
                                last = mm(ps[:, bank, col + n:col + n + 1], t[:, n * P:(n + 1) * P],
                                          ones[0:t.shape[0], 0:1], start=(j == 0), stop=(j == len(parts) - 1))
                        return last

                    def spread(dst, src):
                        for n in range(NT):
                            last = tr(dst[:, n * P:(n + 1) * P], src[:, n:n + 1].broadcast_to([P, P]),
                                      ident[:, :])
                        return last

                    bank45 = ps[:, 4:6, :].rearrange("p b n -> p (b n)")
                    bank67 = ps[:, 6:8, :].rearrange("p b n -> p (b n)")
                    for n in range(NT // 2):
                        x_transpose(n)
                    for j in range(2):
                        x_transpose(NT // 2 + 2 * j)
                        x_transpose(NT // 2 + 2 * j + 1)
                        pe.wait_ge(q["hlo"], NT // 2)
                        project(CHUNKS[j], (0,))
                    pe.wait_ge(q["hlo"], NT)
                    for name in CHUNKS:
                        project(name, (1,) if name in CHUNKS[:2] else (0, 1))
                        if name == "bq0":
                            pe.wait_ge(q["conv_ok"], 2)
                            column_sums(6, 0, [accC[:, 0, :], accC[:, 1, :]]).then_inc(q["st_cp"], 1)
                        if name == "bq1":
                            pe.wait_ge(q["mcol_ok"], 1)
                            spread(bank45, mcol).then_inc(q["st_cp"], 1)
                            pe.wait_ge(q["bsq_ok"], 1)
                            column_sums(7, 0, [aC]).then_inc(q["st_b"], 1)
                        if name == "bkv":
                            pe.wait_ge(q["xsq_ok"], 2)
                            column_sums(6, 16, [uC[:, 0, 0:T], uC[:, 1, 0:T]]).then_inc(q["st_cp"], 1)
                            pe.wait_ge(q["bsq_ok"], 2)
                            pe.wait_ge(q["bstat_ok"], 1)
                            column_sums(7, NT, [aC[0:QR - P]]).then_inc(q["st_b"], 1)
                        if name == "bg0":
                            pe.wait_ge(q["crs_ok"], 1)
                            spread(bank45, crs).then_inc(q["st_cp"], 1)
                            pe.wait_ge(q["bsq_ok"], 3)
                            pe.wait_ge(q["bstat_ok"], 2)
                            column_sums(7, 2 * NT, [aC]).then_inc(q["st_b"], 1)

                    wait_pair(C["dv_t"])
                    for n in range(NT):
                        last = tr(chunk_ps("dv_t")[:, n * P:(n + 1) * P], rawD[:, 3, n * P:(n + 1) * P],
                                  ident[:, :])
                    last.then_inc(q["ch_done"], 1)
                    pe.wait_ge(q["clo_ok"], 2)
                    for m in range(2):
                        c = C[f"pw{m}"]
                        wait_pair(c)
                        for j in range(2):
                            for a, b in three:
                                z = (cHi, cLo)[b]
                                for h in range(2):
                                    last = mm(ps[:, 2 * (c % 2) + h, :], wpR[:, a, j, m * P:(m + 1) * P],
                                              z[:, j, h * HALF:(h + 1) * HALF],
                                              start=(j == 0 and (a, b) == (0, 0)),
                                              stop=(j == 1 and (a, b) == (1, 0)))
                        last.then_inc(q["ch_done"], 1)
                    pe.wait_ge(q["brs_ok"], 1)
                    wait_pair(C["bcast_kv"])
                    spread(chunk_ps("bcast_kv"), brs[:, NT:2 * NT]).then_inc(q["ch_done"], 1)

                    def d_scores(u):
                        n, kv = DU[u]
                        k0, nk, _ = keys(n)
                        if u >= 2:
                            pe.wait_ge(q["ds_ok"], u - 1)
                        else:
                            pe.wait_ge(*free_at(("bcast_kv", "pw1")[u]))
                            pe.wait_ge(q["dst_lo"], 2 * kv + 2)
                        for g in range(2):
                            for part in range(2):
                                last = mm(ps[:, 2 * (u % 2) + g, 0:nk * P],
                                          Qst[:, 2 * kv + g, n * P:(n + 1) * P],
                                          Kst[kv][part][:, k0 * P:(k0 + nk) * P],
                                          start=(part == 0), stop=(part == 1))
                        last.then_inc(q["ds_mm"], 1)

                    def d_transpose(u):
                        n, kv = DU[u]
                        _, nk, _ = keys(n)
                        pe.wait_ge(q["de_ok"], u + 1)
                        if u >= 1:
                            pe.wait_ge(q["dpt_lo"], u)
                        else:
                            pe.wait_ge(q["y_ok"], 2)
                        for b in range(nk):
                            for g in range(2):
                                last = tr(bank45[:, (2 * b + g) * P:(2 * b + g + 1) * P],
                                          Pd[:, u % 2, g, b * P:(b + 1) * P], ident[:, :])
                        last.then_inc(q["dt_mm"], 1)

                    def d_out(n):
                        k0, nk, _ = keys(n)
                        if n >= 1:
                            pe.wait_ge(q["do_ok"], n)
                        else:
                            pe.wait_ge(q["bstat_ok"], 3)
                            pe.wait_ge(q["vd_lo"], 1)
                        pe.wait_ge(q["dr_ok"], n + 1)
                        for kv in range(2):
                            u = 2 * n + kv
                            for g in range(2):
                                tr(ps[:, 6 + kv, (2 + g) * P:(3 + g) * P],
                                   drc[:, 2 * u + g:2 * u + g + 1].broadcast_to([P, P]), ident[:, :])
                        for kv in range(2):
                            pe.wait_ge(q["dpt_lo"], 2 * n + kv + 1)
                            for b in range(nk):
                                for part in range(2):
                                    last = mm(ps[:, 6 + kv, 0:2 * P], Vd[:, k0 + b, kv, :, :],
                                              PTd[:, (2 * n + kv) % 3, part, b * 2 * P:(b + 1) * 2 * P],
                                              start=(b == 0 and part == 0), stop=(b == nk - 1 and part == 1))
                        last.then_inc(q["do_mm"], 1)

                    pe.wait_ge(q["kd_lo"], 4)
                    NU = len(DU)
                    for i in range(NU + 2):
                        if i < NU:
                            d_scores(i)
                        if 1 <= i <= NU:
                            d_transpose(i - 1)
                        if i >= 3 and i % 2:
                            d_out((i - 3) // 2)

                    pe.wait_ge(q["wlo"], POS["w_kv"] + 1)
                    for c, t0 in (("bv0", 0), ("bv1", NT // 2)):
                        pe.wait_ge(q["ds_ok"], NU)
                        wait_pair(C[c])
                        for i in range(NT // 2):
                            for a, b in three:
                                last = mm(chunk_ps(c)[:, i * GW:(i + 1) * GW],
                                          kvR[:, a, (t0 + i) * P:(t0 + i + 1) * P], wup[:, b, 2, GW:2 * GW],
                                          start=((a, b) == (0, 0)), stop=((a, b) == (1, 0)))
                        last.then_inc(q["ch_done"], 1)

                    def q_up(banks, col):
                        for kt, rows in ((0, P), (1, QR - P)):
                            for a, b in three:
                                for h in range(2):
                                    last = mm(banks[:, h * HALF:(h + 1) * HALF], wup[0:rows, a, kt, col:col + P],
                                              qlR[0:rows, kt, b, h * HALF:(h + 1) * HALF],
                                              start=(kt == 0 and (a, b) == (0, 0)),
                                              stop=(kt == 1 and (a, b) == (1, 0)))
                        return last

                    def k_up(banks, p):
                        for a, b in three:
                            for h in range(2):
                                last = mm(banks[:, h * HALF:(h + 1) * HALF], wup[:, a, 2, p * P:(p + 1) * P],
                                          kvR[:, b, h * HALF:(h + 1) * HALF],
                                          start=((a, b) == (0, 0)), stop=((a, b) == (1, 0)))
                        return last

                    for name, col in (("rope", GW), ("rope_sw", GW + P)):
                        wait_pair(C[name])
                        q_up(chunk_ps(name), col).then_inc(q["ch_done"], 1)
                    wait_pair(C["bk0"])
                    k_up(chunk_ps("bk0"), 0).then_inc(q["ch_done"], 1)
                    wait_pair(C["bqn0"])
                    q_up(chunk_ps("bqn0"), 0).then_inc(q["ch_done"], 1)
                    pe.wait_ge(q["dpt_lo"], NU)
                    k_up(bank45, 1).then_inc(q["up2"], 1)
                    pe.wait_ge(q["do_ok"], NT)
                    q_up(bank67, P).then_inc(q["up2"], 1)

                    def b_scores(u):
                        h, i = divmod(u, NT)
                        if i == 0:
                            pe.wait_ge(q["k_lo"], h + 1)
                            pe.wait_ge(q["q_lo"], h + 1)
                            pe.wait_ge(q["qrope_ok"], h + 1)
                            pe.wait_ge(q["ko_ok"], 1)
                            pe.wait_ge(q["zero_ok"], 2)
                        if u < 2:
                            pe.wait_ge(*free_at(("bqn0", "bk0")[u]))
                        if u >= 2:
                            pe.wait_ge(q["be_ok"], u - 1)
                        Q, Kk, rows = ((Qe, Ke, NOPE + ROPE), (Qo, Ko, P))[h % 2]
                        for a, b in three:
                            for half in range(2):
                                last = mm(ps[:, 2 * (u % 2) + half, :], Q[0:rows, a, i * P:(i + 1) * P],
                                          Kk[0:rows, b, half * HALF:(half + 1) * HALF],
                                          start=((a, b) == (0, 0)), stop=((a, b) == (1, 0)))
                        last.then_inc(q["bs_mm"], 1)

                    def b_transpose(u):
                        pe.wait_ge(q["be_ok"], u + 1)
                        for half in range(2):
                            if u >= 1:
                                pe.wait_ge(q["bpt_lo"], 2 * u + half - 1)
                            else:
                                pe.wait_ge(q["kf2_ok"], 1)
                            for k in range(NT // 2):
                                col = half * HALF + k * P
                                last = tr(ps[:, 4 + half, k * P:(k + 1) * P], Pb[:, u % 2, col:col + P], ident[:, :])
                            last.then_inc(q["bt_mm"], 1)

                    def b_out(w, half):
                        h = 2 * w // NT
                        bank = ps[:, 6 + w % 2, :]
                        if half == 0:
                            if w >= 2:
                                pe.wait_ge(q["bo_ok"], w - 1)
                            elif w == 0:
                                pe.wait_ge(q["qf2_ok"], 1)
                            pe.wait_ge(q["br_ok"], 2 * w + 2)
                            for i in range(2):
                                tr(bank[:, 256 + i * P:256 + (i + 1) * P],
                                   brc[:, 2 * w + i:2 * w + i + 1].broadcast_to([P, P]), ident[:, :])
                            pe.wait_ge(q["bpt_lo"], 4 * w + 4)
                        for k in range(half * NT // 2, (half + 1) * NT // 2):
                            for part in range(2):
                                last = mm(bank[:, 0:256], Vb[:, k, h, :, :], PTb[:, w % 2, part, k, :],
                                          start=(k == 0 and part == 0), stop=(k == NT - 1 and part == 1))
                        if half:
                            last.then_inc(q["bo_mm"], 1)

                    pe.wait_ge(q["vb_lo"], NT)
                    for i in range(NB + 3):
                        if i < NB:
                            b_scores(i)
                        if 1 <= i <= NB:
                            b_transpose(i - 1)
                        if i >= 3:
                            b_out(*divmod(i - 3, 2))

                    for n in range(NT):
                        pe.wait_ge(q["clo2"], n + 1)
                        if n >= 2:
                            pe.wait_ge(q["o2_ok"], n - 1)
                        for k in range(KD):
                            if n == 0:
                                pe.wait_ge(q["wlo"], POS[f"w_out{k}"] + 1)
                            for a, b in three:
                                for h in range(2):
                                    last = mm(ps[:, 2 * (n % 2) + h, :], catR[:, n % 2, a, k, :],
                                              woR[k][:, b, h * HALF:(h + 1) * HALF],
                                              start=(k == 0 and (a, b) == (0, 0)),
                                              stop=(k == KD - 1 and (a, b) == (1, 0)))
                        last.then_inc(q["o_mm"], 1)

                @block.gpsimd
                def _(pool):
                    own = Chain(pool, q["own_pool"])

                    def rsqrt(dst, src, signal):
                        pool.tensor_tensor(dst, src, expo[:, 0:src.shape[1]], ALU.pow).then_inc(signal, 1)

                    for n in range(NT):
                        pool.wait_ge(q["sq_ok"], n + 1)
                        own.add(pool.tensor_scalar(ss[:, n:n + 1], ss[:, n:n + 1], 1.0 / D, EPS, ALU.mult, ALU.add))
                        own.wait()
                        rsqrt(rs[:, n:n + 1], ss[:, n:n + 1], q["rs_ok"])
                    pool.wait_ge(q["cvar_ok"], 1)
                    rsqrt(crs[:, :], cvar[:, :], q["crs_ok"])
                    pool.wait_ge(q["bstat_ok"], 3)
                    own.add(pool.tensor_tensor(brs[:, 0:NT], bvar[:, 0:NT], expo[:, :], ALU.pow))
                    rsqrt(brs[:, NT:2 * NT], bvar[:, 2 * NT:3 * NT], q["brs_ok"])
                    own.wait()
                    pool.tensor_scalar(rsq[:, :], brs[:, 0:NT], B_SCALE, None, ALU.mult).then_inc(q["brs_ok"], 1)
                    pool.wait_ge(q["ch_done"], C["pw1"] + 1)
                    pool.wait_ge(q["th_used"], len(TH))
                    pool.memset(Ko[0:ROPE, :, :].bitcast(F32), 0.0).then_inc(q["zero_ok"], 1)
                    pool.memset(Qo[0:ROPE, :, :].bitcast(F32), 0.0).then_inc(q["zero_ok"], 1)
                    for n in range(NT):
                        pool.wait_ge(q["ovar_ok"], n + 1)
                        rsqrt(ors[:, n:n + 1], oss[:, n:n + 1], q["ors_ok"])

                @block.scalar
                def _(act):
                    bank45 = ps[:, 4:6, :].rearrange("p b n -> p (b n)")
                    bank67 = ps[:, 6:8, :].rearrange("p b n -> p (b n)")

                    def square_x(n):
                        if n >= XP:
                            act.wait_ge(*x_landed(n))
                        if n >= 1:
                            act.wait_ge(q["sq_ok"], n)
                        act.activation(junk[:, :], x_tile(n), ACT.Square,
                                       accum_out=ss[:, n:n + 1]).then_inc(q["sq_ok"], 1)

                    def h_hi(n):
                        act.wait_ge(q["xt_ok"], n + 1)
                        b = 4 + 2 * (n % 2)
                        act.activation(hT[:, 0, :, n * P:(n + 1) * P],
                                       ps[:, b:b + 2, :].rearrange("p b (k t) -> p (b k) t", t=P),
                                       ACT.Copy).then_inc(q["hhi"], 1)

                    def split_hi(name):
                        i = POS[name]
                        if i >= RAWS:
                            act.wait_ge(w_ld[i % RAWS], 16 * (i // RAWS))
                        src = raw[:, i % RAWS, :]
                        if name in CHUNKS:
                            c = C[name]
                            if c >= STATS:
                                act.wait_ge(q["ch_done"], c - STATS + 1)
                            dst, src = stat[:, c % STATS, 0, :, :], src.rearrange("p (k m) -> p k m", m=P)
                        elif name == "w_pw":
                            dst, src = wpR[:, 0, :, :], src[:, 0:2 * GW].rearrange("p (k m) -> p k m", m=GW)
                        elif name == "w_q":
                            dst, src = wup[:, 0, 0:2, :], src.rearrange("p (k m) -> p k m", m=512)
                        elif name == "w_kv":
                            dst, src = wup[:, 0, 2, :], src[:, 0:512]
                        else:
                            if name == "w_out0":
                                act.wait_ge(q["k_lo"], HEADS)
                                act.wait_ge(q["qrope_ok"], HEADS)
                            dst = woR[int(name[5:])][:, 0, :]
                        act.activation(dst, src, ACT.Copy).then_inc(q["whi"], 1)

                    def tanh_half(name, src):
                        n = TH[name]
                        if n > 1:
                            act.wait_ge(q["th_used"], n - 1)
                        return act.activation(th[:, :], src, ACT.Tanh, scale=0.5).then_inc(q["th_ok"], 1)

                    def evacuate(name):
                        kind = name.rstrip("01")
                        act_reads = kind in ("dq", "dk", "dv", "bq", "bkv", "ac", "cvb") or name in TH
                        if not act_reads:
                            return
                        act.wait_ge(q["ch_done"], C[name] + 1)
                        if name in TH:
                            tanh_half(name, chunk_ps(name))
                            return
                        if kind[0] == "d":
                            dst = rawD[:, C[name], :]
                        elif kind == "ac":
                            if name == "ac1":
                                act.wait_ge(q["th_used"], TH["ag0"])
                                act.wait_ge(*free_at("ag0"))
                            dst = aC[:, :]
                        else:
                            if name == "bq0":
                                act.wait_ge(*free_at("ag1"))
                            dst = rawB[:, C[name] - C["bq0"], :]
                        act.activation(dst, chunk_ps(name), ACT.Copy).then_inc(free_at(name)[0], 1)

                    def b_square(j):
                        rows = (P, QR - P, P)[j]
                        act.wait_ge(*free_at(("bq0", "bq1", "bkv")[j]))
                        if j:
                            act.wait_ge(q["st_b"], j)
                        act.activation(aC[0:rows, :], rawB[0:rows, j, :], ACT.Square).then_inc(q["bsq_ok"], 1)

                    for n in range(NT + 1):
                        if n < NT:
                            square_x(n)
                        if n == 2:
                            split_hi(CHUNKS[0])
                            split_hi(CHUNKS[1])
                        if n >= 1:
                            h_hi(n - 1)
                    ahead = [n for n in RAW if n in CHUNKS or n == "w_pw"][2:]
                    for c, name in enumerate(CHUNKS):
                        if ahead:
                            split_hi(ahead.pop(0))
                            if ahead and ahead[0] == "w_pw":
                                split_hi(ahead.pop(0))
                        evacuate(name)
                        if name in ("bq0", "bq1", "bkv"):
                            b_square(("bq0", "bq1", "bkv").index(name))
                        if name in K_AT:
                            kv, r2 = K_AT[name]
                            r = HD * kv
                            act.wait_ge(*free_at("dk"))
                            act.activation(Kst[kv][0][r2:r2 + HD, :], rawD[r:r + HD, 2, :], ACT.Copy).then_inc(q["kd_hi"], 1)
                        if name == "bq1":
                            for j in range(2):
                                act.wait_ge(q["xc_ok"], j + 1)
                                act.activation(uC[:, j, 0:T], accC[:, j, :], ACT.Square).then_inc(q["xsq_ok"], 1)
                        if name == "bg0":
                            for j in range(2):
                                act.wait_ge(q["y_ok"], j + 1)
                                tanh_half(f"cz{j}", accC[:, j, :])
                            for j in range(2):
                                act.wait_ge(q["th_used"], TH[f"cz{j}"])
                                if j == 0:
                                    act.wait_ge(q["st_cp"], 3)
                                act.activation(cHi[:, j, :], accC[:, j, :], ACT.Copy).then_inc(q["chi_ok"], 1)

                    act.wait_ge(q["ch_done"], NC)

                    def qd_hi(h):
                        r = HD * (h % 2)
                        act.activation(Qst[r:r + HD, h, :], rawD[r:r + HD, h // 2, :], ACT.Copy).then_inc(q["dst_hi"], 1)

                    qd_hi(0)
                    act.wait_ge(q["ch_done"], C["dv_t"] + 1)
                    act.activation(Vd[:, :, :, 0, :], chunk_ps("dv_t").rearrange("p (t v d) -> p t v d", t=NT, v=2),
                                   ACT.Copy).then_inc(q["vd_hi"], 1)
                    for h in range(1, HEADS):
                        qd_hi(h)
                    act.wait_ge(q["ch_done"], C["bcast_kv"] + 1)
                    act.activation(rbc[:, :], chunk_ps("bcast_kv"), ACT.Copy).then_inc(free_at("bcast_kv")[0], 1)

                    def between(i):
                        if i in LAT_AT:
                            j = LAT_AT[i]
                            rows, dst = ((P, qlR[:, 0, 0, :]), (QR - P, qlR[0:QR - P, 1, 0, :]), (P, kvR[:, 0, :]))[j]
                            act.activation(dst, rawB[0:rows, j, :], ACT.Copy,
                                           scale=parT[0:rows, P_GQ + j:P_GQ + j + 1]).then_inc(q["lat_hi"], 1)
                        if i == KE_AT:
                            act.wait_ge(q["kr_ok"], 1)
                            act.wait_ge(q["dst_lo"], HEADS)
                            act.wait_ge(q["kd_lo"], 4)
                            act.activation(Ke[HD:HD + ROPE, 0, :], rawB[HD:HD + ROPE, 1, :], ACT.Copy).then_inc(q["ke_hi"], 1)
                        if i == KE_AT + 2:
                            act.wait_ge(q["ke_lo"], 1)
                            act.wait_ge(q["th_used"], len(TH))
                            act.wait_ge(q["bstat_ok"], 3)
                            act.activation(Ko[ROPE:2 * ROPE, :, :], Ke[HD:HD + ROPE, :, :].bitcast(F32), ACT.Copy).then_inc(q["ko_ok"], 1)
                        if i in UP_AT:
                            act.wait_ge(q["lat_lo"], 3)
                            act.wait_ge(q["ke_lo"], 1)
                            split_hi(UP_AT[i])

                    def d_exp(u):
                        n, kv = DU[u]
                        _, nk, _ = keys(n)
                        act.wait_ge(q["dm_ok"], u + 1)
                        for g in range(2):
                            c, m = 2 * u + g, dnm[:, 2 * (u % 2) + g:2 * (u % 2) + g + 1]
                            act.activation(dex[:, c:c + 1], parT[:, P_SINK + 2 * kv + g:P_SINK + 2 * kv + g + 1],
                                           ACT.Exp, bias=m)
                            last = act.activation(Pd[:, u % 2, g, 0:nk * P], Pd[:, u % 2, g, 0:nk * P], ACT.Exp,
                                                  bias=m, accum_out=dsm[:, c:c + 1])
                        last.then_inc(q["de_ok"], 1)

                    def d_hi(u):
                        n, kv = DU[u]
                        _, nk, _ = keys(n)
                        act.wait_ge(q["dt_mm"], u + 1)
                        if u >= 4:
                            act.wait_ge(q["do_mm"], (u - 3) // 2 + 1)
                        act.activation(PTd[:, u % 3, 0, 0:nk * 2 * P], bank45[:, 0:nk * 2 * P], ACT.Copy).then_inc(q["dpt_hi"], 1)

                    def d_half(n):
                        act.wait_ge(q["do_mm"], n + 1)
                        if n == 0:
                            act.wait_ge(q["ch_done"], C["pw1"] + 1)
                        else:
                            act.wait_ge(q["do_ok"], n)
                        act.activation(tmpD[0:HD, :, :], ps[HD:P, 6:8, 0:P], ACT.Copy)
                        act.activation(tmpD[HD:P, :, :], ps[0:HD, 6:8, P:2 * P], ACT.Copy).then_inc(q["do_tmp"], 1)

                    NU = len(DU)
                    for i in range(NU + 3):
                        if 1 <= i <= NU:
                            d_hi(i - 1)
                        if i < NU:
                            d_exp(i)
                        if i >= 3 and i % 2:
                            d_half((i - 3) // 2)
                        between(i)

                    act.wait_ge(q["brs_ok"], 2)
                    for n in range(NT):
                        name = ("bv0", "bv1")[2 * n // NT]
                        i = n % (NT // 2)
                        if i == 0:
                            act.wait_ge(q["ch_done"], C[name] + 1)
                        act.activation(Vb[:, n, :, 0, :], chunk_ps(name)[:, i * GW:(i + 1) * GW]
                                       .rearrange("p (h d) -> p h d", d=HD), ACT.Copy,
                                       scale=brs[:, NT + n:NT + n + 1]).then_inc(q["vb_hi"], 1)
                    act.wait_ge(q["qr_ok"], 1)
                    act.activation(qrR[:, 0, :], qrF[:, 0, :], ACT.Copy).then_inc(q["qr_hi"], 1)

                    def k_hi(h):
                        if h >= 2:
                            act.wait_ge(q["bs_mm"], (h - 1) * NT)
                        Kk, rows = ((Ke, slice(0, HD)), (Ko, slice(HD, P)))[h % 2]
                        act.wait_ge(*((q["kt_ok"], 1) if h < 2 else (q["kf2_ok"], 1)))
                        act.activation(Kk[rows, 0, :], (krt, kF2)[h // 2][rows, :], ACT.Copy).then_inc(q["k_hi"], 1)

                    def q_hi(h):
                        Q, rows = ((Qe, slice(0, HD)), (Qo, slice(HD, P)))[h % 2]
                        act.wait_ge(*((q["ch_done"], C["bqn0"] + 1) if h < 2 else (q["qf2_ok"], 1)))
                        act.activation(Q[rows, 0, :], (chunk_ps("bqn0"), qF2)[h // 2][rows, :], ACT.Copy).then_inc(q["q_hi"], 1)

                    def b_exp(u):
                        act.wait_ge(q["bm_ok"], u + 1)
                        if u >= 2:
                            act.wait_ge(q["bt_mm"], 2 * u - 2)
                        elif u == 0:
                            act.wait_ge(q["qr_lo"], 1)
                        act.activation(Pb[:, u % 2, :], pair(u), ACT.Exp, bias=bnb[:, u:u + 1],
                                       scale=rsq[:, u % NT:u % NT + 1], accum_out=bsm[:, u:u + 1]).then_inc(q["be_ok"], 1)

                    def b_hi(u):
                        w = u // 2
                        if w >= 2:
                            act.wait_ge(q["bo_mm"], w - 1)
                        for half in range(2):
                            act.wait_ge(q["bt_mm"], 2 * u + half + 1)
                            act.activation(PTb[:, w % 2, 0, half * NT // 2:(half + 1) * NT // 2, u % 2 * P:(u % 2 + 1) * P],
                                           ps[:, 4 + half, :].rearrange("p (k t) -> p k t", t=P), ACT.Copy
                                           ).then_inc(q["bpt_hi"], 1)

                    def b_half(w):
                        h = 2 * w // NT
                        act.wait_ge(q["bo_mm"], w + 1)
                        if w >= 2:
                            act.wait_ge(q["bo_ok"], w - 1)
                        r, o = ((0, HD), (HD, 0))[h % 2]
                        b = ps[:, 6 + w % 2, :]
                        act.activation(tmpB[r:r + HD, w % 2, :], b[o:o + HD, 0:256], ACT.Copy)
                        act.activation(rbB[r:r + HD, w % 2, :], b[r:r + HD, 256:512], ACT.Copy).then_inc(q["bo_tmp"], 1)

                    def cat_hi(n):
                        if n >= 2:
                            act.wait_ge(q["o_mm"], n - 1)
                        act.activation(catR[:, n % 2, 0, :, :], cat[:, :, n * P:(n + 1) * P], ACT.Copy).then_inc(q["chi2"], 1)

                    k_hi(0)
                    q_hi(0)
                    q_hi(1)
                    k_hi(1)
                    act.wait_ge(q["up2"], 2)
                    act.activation(qF2[:, :], bank67, ACT.Copy).then_inc(q["qf2_ok"], 1)
                    for i in range(NB + 4):
                        if i in HEAD_AT:
                            h = HEAD_AT[i]
                            (q_hi if i % 2 else k_hi)(h)
                        if 1 <= i <= NB:
                            b_hi(i - 1)
                        if i < NB:
                            b_exp(i)
                        if i >= 5 and i % 2 == 1:
                            b_half((i - 5) // 2)
                        if i in W_OUT_AT:
                            split_hi(f"w_out{W_OUT_AT[i]}")
                    act.wait_ge(q["bo_mm"], NB // 2)
                    for k in range(EARLY, EARLY + 2):
                        split_hi(f"w_out{k}")
                    act.wait_ge(q["bo_ok"], NB // 2)
                    cat_hi(0)
                    for k in range(EARLY + 2, KD):
                        split_hi(f"w_out{k}")
                    cat_hi(1)
                    for n in range(NT):
                        if n >= 1 and n + 1 < NT:
                            cat_hi(n + 1)
                        act.wait_ge(q["o_mm"], n + 1)
                        if n >= 1:
                            act.wait_ge(q["osq_ok"], n)
                        act.activation(junk[:, :], pair(n), ACT.Square, accum_out=oss[:, n:n + 1]).then_inc(q["osq_ok"], 1)

                @block.vector
                def _(dve):
                    own = Chain(dve, q["own_dve"])
                    conv = Chain(dve, q["conv_own"])
                    tt, ts, stt = dve.tensor_tensor, dve.tensor_scalar, dve.scalar_tensor_tensor
                    bank45 = ps[:, 4:6, :].rearrange("p b n -> p (b n)")

                    def minus(dst, a, hi):
                        return tt(dst, a, hi.bitcast(F32), ALU.subtract)

                    def norm_x(n):
                        dve.wait_ge(q["rs_ok"], n + 1)
                        stt(x_tile(n), x_tile(n), rs[:, n:n + 1], gpre[:, :],
                            ALU.mult, ALU.mult).then_inc(q["xn_ok"], 1)

                    def h_lo(n):
                        dve.wait_ge(q["hhi"], n + 1)
                        b = 4 + 2 * (n % 2)
                        minus(hT[:, 1, :, n * P:(n + 1) * P],
                              ps[:, b:b + 2, :].rearrange("p b (k t) -> p (b k) t", t=P),
                              hT[:, 0, :, n * P:(n + 1) * P]).then_inc(q["hlo"], 1)

                    def split_lo(name):
                        i = POS[name]
                        dve.wait_ge(q["whi"], i + 1)
                        src = raw[:, i % RAWS, :]
                        if name in CHUNKS:
                            s_ = stat[:, C[name] % STATS]
                            minus(s_[:, 1, :, :], src.rearrange("p (k m) -> p k m", m=P), s_[:, 0, :, :]).then_inc(q["wlo"], 1)
                        elif name == "w_pw":
                            minus(wpR[:, 1, :, :], src[:, 0:2 * GW].rearrange("p (k m) -> p k m", m=GW), wpR[:, 0, :, :]).then_inc(q["wlo"], 1)
                        elif name == "w_q":
                            minus(wup[:, 1, 0:2, :], src.rearrange("p (k m) -> p k m", m=512), wup[:, 0, 0:2, :]).then_inc(q["wlo"], 1)
                        elif name == "w_kv":
                            minus(wup[:, 1, 2, :], src[:, 0:512], wup[:, 0, 2, :]).then_inc(q["wlo"], 1)
                        else:
                            k = int(name[5:])
                            minus(woR[k][:, 1, :], src, woR[k][:, 0, :]).then_inc(q["wlo"], 1)

                    def gate(name):
                        dve.wait_ge(q["th_ok"], TH[name])
                        stt(cat[:, CAT[name], :], th[:, :], 1.0, chunk_ps(name), ALU.add, ALU.mult
                            ).then_inc(q["th_used"], 1)

                    def evacuate(name):
                        kind, j = name.rstrip("01"), int(name[-1]) if name[-1].isdigit() else 0
                        if kind == "cva":
                            dve.wait_ge(q["ch_done"], C[name] + 1)
                            dve.wait_ge(q["th_ok"], TH[f"cvb{j}"])
                            stt(uC[:, j, PAD_C:PAD_C + T], th[:, :], 1.0, chunk_ps(name), ALU.add, ALU.mult
                                ).then_inc(q["th_used"], 1)
                        elif kind == "ah":
                            dve.wait_ge(q["ch_done"], C[name] + 1)
                            dve.wait_ge(*free_at(f"ac{j}"))
                            tt(aU[:, 1:T + 1], chunk_ps(name), aC[:, :], ALU.mult).then_inc(free_at(name)[0], 1)
                            dve.wait_ge(*free_at(name))
                            own.wait()
                            w = P_AW + TAPS_A * j
                            own.add(ts(aC[:, :], aU[:, 0:T], parT[:, w:w + 1], parT[:, P_AB + j:P_AB + j + 1], ALU.mult, ALU.add))
                            for t in range(1, TAPS_A):
                                own.wait()
                                own.add(stt(aC[:, :], aU[:, t:t + T], parT[:, w + t:w + t + 1], aC[:, :], ALU.mult, ALU.add))
                        elif kind == "ab":
                            dve.wait_ge(q["ch_done"], C[name] + 1)
                            own.wait()
                            tt(aC[:, :], chunk_ps(name), aC[:, :], ALU.mult).then_inc(free_at(name)[0], 1)
                        elif kind == "ag":
                            dve.wait_ge(q["th_ok"], TH[name])
                            own.add(stt(cat[:, CAT[name], :], th[:, :], 1.0, chunk_ps(name), ALU.add, ALU.mult))
                            own.wait()
                            dve.wait_ge(*free_at(f"ab{j}"))
                            stt(cat[:, CAT[name], :], cat[:, CAT[name], :], 0.5, aC[:, :], ALU.mult, ALU.mult
                                ).then_inc(q["th_used"], 1)
                        elif kind[1:] == "g":
                            gate(name)

                    def conv_taps(taps):
                        for t in taps:
                            for j in range(2):
                                w = parT[:, P_CW + TAPS_C * j + int(t):P_CW + TAPS_C * j + int(t) + 1]
                                if t == 0:
                                    conv.add(ts(accC[:, j, :], uC[:, j, 0:T], w, None, ALU.mult))
                                else:
                                    conv.wait(conv.n - 1)
                                    conv.add(stt(accC[:, j, :], uC[:, j, int(t):int(t) + T], w, accC[:, j, :],
                                                 ALU.mult, ALU.add))

                    k_r, k_s = slice(HD, HD + ROPE), slice(HD + ROPE, P)

                    for n in range(NT + 1):
                        if n < NT:
                            norm_x(n)
                        if n == 2:
                            split_lo(CHUNKS[0])
                            split_lo(CHUNKS[1])
                        if n >= 1:
                            h_lo(n - 1)
                    own.add(dve.memset(aU[:, 0:1], 0.0))
                    own.add(dve.memset(aU[:, T + 1:T + 2], 0.0))
                    own.add(dve.memset(uC[:, :, 0:PAD_C], 0.0))
                    own.add(dve.memset(uC[:, :, PAD_C + T:UP], 0.0))
                    own.add(ts(ngs[:, :], parT[:, P_SINK:P_SINK + HEADS], -1.0, None, ALU.mult))

                    ahead = [n for n in RAW if n in CHUNKS or n == "w_pw"][2:]
                    for c, name in enumerate(CHUNKS):
                        if ahead:
                            split_lo(ahead.pop(0))
                            if ahead and ahead[0] == "w_pw":
                                split_lo(ahead.pop(0))
                        evacuate(name)
                        if c in CONV_STEPS:
                            if c == C["cg0"]:
                                dve.wait_ge(*free_at("cva0"))
                                dve.wait_ge(*free_at("cva1"))
                                own.wait()
                            conv_taps(CONV_STEPS[c])
                        if name in K_AT:
                            kv, r2 = K_AT[name]
                            r = HD * kv
                            dve.wait_ge(q["kd_hi"], list(K_AT).index(name) + 1)
                            minus(Kst[kv][1][r2:r2 + HD, :], rawD[r:r + HD, 2, :], Kst[kv][0][r:r + HD, :]).then_inc(q["kd_lo"], 1)
                        if name == "ag1":
                            conv.wait()
                            for j in range(2):
                                ts(accC[:, j, :], accC[:, j, :], 0.5, parT[:, P_CB + j:P_CB + j + 1],
                                   ALU.mult, ALU.add).then_inc(q["conv_ok"], 1)
                        if name == "bq0":
                            dve.wait_ge(q["st_cp"], 1)
                            ts(mcol[:, :], ps[:, 6, 0:NT], 1.0 / GW, None, ALU.mult).then_inc(q["mcol_ok"], 1)
                        if name == "bq1":
                            dve.wait_ge(q["st_cp"], 2)
                            for j in range(2):
                                tt(accC[:, j, :], accC[:, j, :], bank45, ALU.subtract).then_inc(q["xc_ok"], 1)
                            dve.wait_ge(q["st_b"], 1)
                            ts(bvar[:, 0:NT], ps[:, 7, 0:NT], 1.0 / QR, EPS, ALU.mult, ALU.add).then_inc(q["bstat_ok"], 1)
                        if name == "bkv":
                            dve.wait_ge(q["st_cp"], 3)
                            ts(cvar[:, :], ps[:, 6, 16:16 + NT], 1.0 / GW, EPS, ALU.mult, ALU.add).then_inc(q["cvar_ok"], 1)
                            dve.wait_ge(q["st_b"], 2)
                            dve.wait_ge(q["bstat_ok"], 1)
                            stt(bvar[:, 0:NT], ps[:, 7, NT:2 * NT], 1.0 / QR, bvar[:, 0:NT], ALU.mult, ALU.add
                                ).then_inc(q["bstat_ok"], 1)
                            dve.wait_ge(*free_at("bq1"))
                            own.add(tt(cat[k_r, 3, :], rawB[k_s, 1, :], ropeT[k_s, 1, :], ALU.mult))
                            own.add(tt(rawB[k_r, 1, :], rawB[k_r, 1, :], ropeT[k_r, 0, :], ALU.mult))
                            own.wait()
                            tt(rawB[k_r, 1, :], rawB[k_r, 1, :], cat[k_r, 3, :], ALU.add).then_inc(q["kr_ok"], 1)
                            dve.wait_ge(q["kr_ok"], 1)
                        if name == "bg0":
                            dve.wait_ge(q["st_cp"], 4)
                            dve.wait_ge(q["xsq_ok"], 2)
                            for j in range(2):
                                own.add(tt(accC[:, j, :], accC[:, j, :], bank45, ALU.mult))
                            for j in range(2):
                                own.wait(own.n - 1 + j)
                                ts(accC[:, j, :], accC[:, j, :], parT[:, P_LG + j:P_LG + j + 1],
                                   parT[:, P_LB + j:P_LB + j + 1], ALU.mult, ALU.add).then_inc(q["y_ok"], 1)
                            dve.wait_ge(q["st_b"], 3)
                            ts(bvar[:, 2 * NT:3 * NT], ps[:, 7, 2 * NT:3 * NT], 1.0 / KVR, EPS, ALU.mult, ALU.add
                               ).then_inc(q["bstat_ok"], 1)
                            for j in range(2):
                                dve.wait_ge(q["th_ok"], TH[f"cz{j}"])
                                stt(accC[:, j, :], th[:, :], 1.0, accC[:, j, :], ALU.add, ALU.mult
                                    ).then_inc(q["th_used"], 1)
                            for j in range(2):
                                dve.wait_ge(q["chi_ok"], j + 1)
                                minus(cLo[:, j, :], accC[:, j, :], cHi[:, j, :]).then_inc(q["clo_ok"], 1)

                    def qd_lo(h):
                        r = HD * (h % 2)
                        dve.wait_ge(q["dst_hi"], h + 1)
                        minus(Qst[HD - r:P - r, h, :], rawD[r:r + HD, h // 2, :], Qst[r:r + HD, h, :]).then_inc(q["dst_lo"], 1)

                    qd_lo(0)
                    dve.wait_ge(q["vd_hi"], 1)
                    minus(Vd[:, :, :, 1, :], chunk_ps("dv_t").rearrange("p (t v d) -> p t v d", t=NT, v=2),
                          Vd[:, :, :, 0, :]).then_inc(q["vd_lo"], 1)
                    qd_lo(1)
                    for m in range(2):
                        dve.wait_ge(q["ch_done"], C[f"pw{m}"] + 1)
                        dve.wait_ge(*free_at(f"cg{m}"))
                        stt(cat[:, 4 + m, :], chunk_ps(f"pw{m}"), 0.25, cat[:, 4 + m, :], ALU.mult, ALU.mult
                            ).then_inc(free_at(f"pw{m}")[0], 1)
                        qd_lo(2 + m)

                    def between(i):
                        if i in LAT_AT:
                            j = LAT_AT[i]
                            rows, dst = ((P, qlR[:, 0, :, :]), (QR - P, qlR[0:QR - P, 1, :, :]), (P, kvR[:, :, :]))[j]
                            dve.wait_ge(q["lat_hi"], j + 1)
                            stt(dst[:, 1, :], rawB[0:rows, j, :], parT[0:rows, P_GQ + j:P_GQ + j + 1],
                                dst[:, 0, :].bitcast(F32), ALU.mult, ALU.subtract).then_inc(q["lat_lo"], 1)
                        if i == KE_AT:
                            dve.wait_ge(q["ke_hi"], 1)
                            minus(Ke[k_r, 1, :], rawB[k_r, 1, :], Ke[k_r, 0, :]).then_inc(q["ke_lo"], 1)
                        if i in UP_AT:
                            split_lo(UP_AT[i])

                    def d_max(u):
                        n, kv = DU[u]
                        k0, nk, b0 = keys(n)
                        s2 = 2 * (u % 2)
                        dve.wait_ge(q["ds_mm"], u + 1)
                        if u >= 2:
                            dve.wait_ge(q["dt_mm"], u - 1)
                        stt(Pd[:, u % 2, :, 0:nk * P], ps[:, s2:s2 + 2, 0:nk * P], D_SCALE,
                            bias[:, 2 * kv:2 * kv + 2, b0:b0 + nk * P], ALU.mult, ALU.add).then_inc(q["ds_ok"], 1)
                        dve.wait_ge(q["ds_ok"], u + 1)
                        own.add(dve.tensor_reduce(dmx[:, s2:s2 + 2], Pd[:, u % 2, :, 0:nk * P], AX.X, ALU.max))
                        own.wait()
                        stt(dnm[:, s2:s2 + 2], dmx[:, s2:s2 + 2], -1.0, ngs[:, 2 * kv:2 * kv + 2],
                            ALU.mult, ALU.min).then_inc(q["dm_ok"], 1)

                    def d_recip(n):
                        c = slice(4 * n, 4 * n + 4)
                        dve.wait_ge(q["de_ok"], 2 * n + 2)
                        own.add(tt(dsm[:, c], dsm[:, c], dex[:, c], ALU.add))
                        own.wait()
                        dve.reciprocal(drc[:, c], dsm[:, c]).then_inc(q["dr_ok"], 1)

                    def d_lo(u):
                        n, kv = DU[u]
                        _, nk, _ = keys(n)
                        dve.wait_ge(q["dpt_hi"], u + 1)
                        minus(PTd[:, u % 3, 1, 0:nk * 2 * P], bank45[:, 0:nk * 2 * P],
                              PTd[:, u % 3, 0, 0:nk * 2 * P]).then_inc(q["dpt_lo"], 1)

                    def d_combine(n):
                        dve.wait_ge(q["do_tmp"], n + 1)
                        own.add(tt(tmpD[0:HD, :, :], ps[0:HD, 6:8, 0:P], tmpD[0:HD, :, :], ALU.add))
                        own.add(tt(tmpD[HD:P, :, :], ps[HD:P, 6:8, P:2 * P], tmpD[HD:P, :, :], ALU.add))
                        own.wait()
                        own.add(tt(tmpD[0:HD, :, :], ps[0:HD, 6:8, 2 * P:3 * P], tmpD[0:HD, :, :], ALU.mult))
                        own.add(tt(tmpD[HD:P, :, :], ps[HD:P, 6:8, 3 * P:4 * P], tmpD[HD:P, :, :], ALU.mult))
                        own.wait()
                        y_ = cat[:, 6:8, n * P:(n + 1) * P]
                        stt(y_, tmpD[:, :, :], 0.5, y_, ALU.mult, ALU.mult).then_inc(q["do_ok"], 1)

                    NU = len(DU)
                    for i in range(NU + 3):
                        if i < NU:
                            d_max(i)
                        if i >= 2 and i % 2 == 0 and i <= NU:
                            d_recip((i - 2) // 2)
                        if 1 <= i <= NU:
                            d_lo(i - 1)
                        if i >= 4 and i % 2 == 0:
                            d_combine((i - 4) // 2)
                        between(i)

                    dve.wait_ge(q["brs_ok"], 2)
                    for n in range(NT):
                        name = ("bv0", "bv1")[2 * n // NT]
                        i = n % (NT // 2)
                        dve.wait_ge(q["vb_hi"], (n | 1) + 1)
                        stt(Vb[:, n, :, 1, :], chunk_ps(name)[:, i * GW:(i + 1) * GW].rearrange("p (h d) -> p h d", d=HD),
                                brs[:, NT + n:NT + n + 1], Vb[:, n, :, 0, :].bitcast(F32), ALU.mult, ALU.subtract
                                ).then_inc(q["vb_lo"], 1)
                    dve.wait_ge(q["ch_done"], C["rope"] + 1)
                    tt(qrF[:, 0, :], chunk_ps("rope"), ropeT[:, 0, :], ALU.mult).then_inc(free_at("rope")[0], 1)
                    dve.wait_ge(q["ch_done"], C["rope_sw"] + 1)
                    tt(qrF[:, 1, :], chunk_ps("rope_sw"), ropeT[:, 1, :], ALU.mult).then_inc(free_at("rope_sw")[0], 1)
                    dve.wait_ge(*free_at("rope"))
                    dve.wait_ge(*free_at("rope_sw"))
                    tt(qrF[:, 0, :], qrF[:, 0, :], qrF[:, 1, :], ALU.add).then_inc(q["qr_ok"], 1)
                    dve.wait_ge(q["qr_hi"], 1)
                    minus(qrR[:, 1, :], qrF[:, 0, :], qrR[:, 0, :]).then_inc(q["qr_lo"], 1)
                    dve.wait_ge(q["qr_lo"], 1)

                    def k_lo(h):
                        Kk, rows = ((Ke, slice(0, HD)), (Ko, slice(HD, P)))[h % 2]
                        dve.wait_ge(q["k_hi"], h + 1)
                        minus(Kk[rows, 1, :], (krt, kF2)[h // 2][rows, :], Kk[rows, 0, :]).then_inc(q["k_lo"], 1)

                    def q_lo(h):
                        Q, rows = ((Qe, slice(0, HD)), (Qo, slice(HD, P)))[h % 2]
                        dve.wait_ge(q["q_hi"], h + 1)
                        minus(Q[rows, 1, :], (chunk_ps("bqn0"), qF2)[h // 2][rows, :], Q[rows, 0, :]).then_inc(q["q_lo"], 1)

                    def q_rope(h):
                        if h >= 2:
                            dve.wait_ge(q["bs_mm"], (h - 1) * NT)
                        Q, r = ((Qe, HD), (Qo, ROPE))[h % 2]
                        dve.tensor_copy(Q[r:r + ROPE, :, :], qrR[ROPE * h:ROPE * (h + 1), :, :].bitcast(F32)).then_inc(q["qrope_ok"], 1)

                    def b_max(u):
                        dve.wait_ge(q["bs_mm"], u + 1)
                        own.add(dve.tensor_reduce(bmx[:, u:u + 1], pair(u), AX.X, ALU.max))
                        own.wait()
                        ts(bnb[:, u:u + 1], bmx[:, u:u + 1], rsq[:, u % NT:u % NT + 1], -1.0,
                           ALU.mult, ALU.mult).then_inc(q["bm_ok"], 1)

                    def b_lo(u):
                        w = u // 2
                        for half in range(2):
                            dve.wait_ge(q["bpt_hi"], 2 * u + half + 1)
                            dst = PTb[:, w % 2, :, half * NT // 2:(half + 1) * NT // 2, u % 2 * P:(u % 2 + 1) * P]
                            minus(dst[:, 1], ps[:, 4 + half, :].rearrange("p (k t) -> p k t", t=P), dst[:, 0]
                                  ).then_inc(q["bpt_lo"], 1)

                    def b_recip(u):
                        dve.wait_ge(q["be_ok"], u + 1)
                        dve.reciprocal(brc[:, u:u + 1], bsm[:, u:u + 1]).then_inc(q["br_ok"], 1)

                    def b_combine(w):
                        h, i = divmod(2 * w, NT)
                        dve.wait_ge(q["bo_tmp"], w + 1)
                        r = HD * (h % 2)
                        rows = slice(r, r + HD)
                        b, t = ps[:, 6 + w % 2, :], tmpB[rows, w % 2, :]
                        own.add(tt(t, b[rows, 0:256], t, ALU.add))
                        own.wait()
                        own.add(tt(t, t, rbB[rows, w % 2, :], ALU.mult))
                        own.wait()
                        y_ = cat[rows, 2 + h // 2, i * P:(i + 2) * P]
                        stt(y_, t, 0.5, y_, ALU.mult, ALU.mult).then_inc(q["bo_ok"], 1)

                    def cat_lo(n):
                        dve.wait_ge(q["chi2"], n + 1)
                        minus(catR[:, n % 2, 1, :, :], cat[:, :, n * P:(n + 1) * P], catR[:, n % 2, 0, :, :]).then_inc(q["clo2"], 1)

                    dve.wait_ge(q["ch_done"], C["bk0"] + 1)
                    own.wait()
                    dve.wait_ge(q["kr_ok"], 1)
                    dve.wait_ge(*free_at("bcast_kv"))
                    tt(krt[:, :], chunk_ps("bk0"), rbc[:, :], ALU.mult).then_inc(q["kt_ok"], 1)
                    q_rope(0)
                    k_lo(0)
                    q_lo(0)
                    q_lo(1)
                    dve.wait_ge(q["up2"], 1)
                    tt(kF2[:, :], bank45, rbc[:, :], ALU.mult).then_inc(q["kf2_ok"], 1)
                    for i in range(NB + 4):
                        if i == 2:
                            q_rope(1)
                        if i == 3:
                            k_lo(1)
                        if i in HEAD_AT:
                            h = HEAD_AT[i]
                            if i % 2:
                                q_lo(h)
                            else:
                                q_rope(h)
                                k_lo(h)
                        if i < NB:
                            b_max(i)
                        if 1 <= i <= NB:
                            b_recip(i - 1)
                            b_lo(i - 1)
                        if i >= 5 and i % 2 == 1:
                            b_combine((i - 5) // 2)
                        if i in W_OUT_AT:
                            split_lo(f"w_out{W_OUT_AT[i]}")

                    for k in range(EARLY, EARLY + 2):
                        split_lo(f"w_out{k}")
                    cat_lo(0)
                    for k in range(EARLY + 2, KD):
                        split_lo(f"w_out{k}")
                    cat_lo(1)
                    dve.wait_ge(q["gpost_ld"], 16)
                    for n in range(NT):
                        if n >= 1 and n + 1 < NT:
                            cat_lo(n + 1)
                        dve.wait_ge(q["osq_ok"], n + 1)
                        ts(oss[:, n:n + 1], oss[:, n:n + 1], 1.0 / D, EPS, ALU.mult, ALU.add).then_inc(q["ovar_ok"], 1)
                        dve.wait_ge(q["ors_ok"], n + 1)
                        stt(pair(n), pair(n), ors[:, n:n + 1], gvec[:, :], ALU.mult, ALU.mult).then_inc(q["o1_ok"], 1)
                        dve.wait_ge(q["o1_ok"], n + 1)
                        dve.wait_ge(*residual_landed(n))
                        tt(xs[:, n % XS, :], xs[:, n % XS, :], pair(n), ALU.add).then_inc(q["o2_ok"], 1)

            nc.all_engine_barrier()
            nc.sync.sem_clear(range(per_pass[0].num, per_pass[-1].num + 1))
            nc.all_engine_barrier()


def _buckets(rel):
    half = BUCKETS // 2
    exact = half // 2
    n = np.abs(rel)
    large = exact + (np.log(np.maximum(n, 1) / exact) / math.log(MAX_DIST / exact) * (half - exact)).astype(np.int32)
    large = np.minimum(large, half - 1)
    return (rel > 0).astype(np.int32) * half + np.where(n < exact, n, large).astype(np.int32)


def _constants():
    dist = np.arange(512) - 255
    onehot = (np.arange(BUCKETS)[:, None] == _buckets(dist)[None, :]).astype(np.float32)
    band = np.broadcast_to(np.where(np.abs(dist) <= WINDOW, 0.0, NEG).astype(np.float32), (HEADS, 512))
    inv = np.float32(10000.0) ** (-np.arange(0, ROPE, 2, dtype=np.float32) / np.float32(ROPE))
    ang = np.arange(T, dtype=np.float32)[None, :] * inv[:, None]
    cos, sin = np.cos(ang), np.sin(ang)
    rope = np.stack([np.tile(np.concatenate([cos, cos]), (4, 1)), np.tile(np.concatenate([-sin, sin]), (4, 1))])
    return onehot, np.ascontiguousarray(band), rope.astype(np.float32)


def _columns():
    sizes = [GW, GW, GW, GW, QR, KVR, ROPE, GW, GW, GW, GW, HEADS * HD, 2 * HD, 2 * HD, GW]
    names = ["ab", "ac", "ah", "ag", "bq", "bkv", "bkr", "bg", "cva", "cvb", "cg", "dq", "dk", "dv", "dg"]
    start = dict(zip(names, np.cumsum([0] + sizes[:-1])))
    out = []
    for name in CHUNKS:
        kind, j = name.rstrip("01"), int(name[-1]) if name[-1].isdigit() else 0
        if name == "bq1":
            kr = start["bkr"] + np.arange(ROPE)
            out.append(np.concatenate([start["bq"] + np.arange(P, QR), kr, np.roll(kr, -(ROPE // 2))]))
        else:
            out.append(start[kind] + j * P + np.arange(P))
    return np.stack(out)


def _q_columns():
    h = np.arange(HEADS)[:, None] * (NOPE + ROPE)
    rot = NOPE + np.arange(ROPE)
    return np.concatenate([(h + np.arange(NOPE)).ravel(), (h + rot).ravel(), (h + np.roll(rot, -(ROPE // 2))).ravel()])


def _kv_columns():
    h = np.arange(HEADS)[:, None] * 2 * HD
    return np.concatenate([(h + np.arange(HD)).ravel(), (h + HD + np.arange(HD)).ravel()])


def kernel(x_prompt, x_sample, g_pre, g_post, w_in, w_out, conv_a_w, conv_a_b, mla_g_q, mla_w_q_up,
           mla_g_kv, mla_w_kv_up, conf_w_dw, conf_b_dw, conf_ln_g, conf_ln_b, conf_w_pw, swa_sink, rel_bias):
    import concourse.bacc as bacc
    from concourse.bass_utils import run_bass_kernel_spmd as run

    (x_prompt, x_sample, g_pre, g_post, w_in, w_out, conv_a_w, conv_a_b, mla_g_q, mla_w_q_up, mla_g_kv,
     mla_w_kv_up, conf_w_dw, conf_b_dw, conf_ln_g, conf_ln_b, conf_w_pw, swa_sink, rel_bias) = map(np.asarray, (
         x_prompt, x_sample, g_pre, g_post, w_in, w_out, conv_a_w, conv_a_b, mla_g_q, mla_w_q_up, mla_g_kv,
         mla_w_kv_up, conf_w_dw, conf_b_dw, conf_ln_g, conf_ln_b, conf_w_pw, swa_sink, rel_bias))

    def blocks(a):
        return a.reshape(L, -1, 2, P).transpose(0, 3, 2, 1).reshape(L, P, -1)

    gq = np.zeros((L, 2 * P), np.float32)
    gq[:, :QR] = mla_g_q
    par = np.concatenate([
        blocks(conv_a_w), blocks(conv_a_b), blocks(conf_w_dw), blocks(conf_b_dw), blocks(conf_ln_g),
        blocks(conf_ln_b), blocks(gq), mla_g_kv[:, :, None],
        np.broadcast_to(swa_sink[:, None, :], (L, P, HEADS))], axis=2)
    wq = np.zeros((L, 2 * P, 512), np.float32)
    wq[:, :QR] = mla_w_q_up[:, :, _q_columns()]
    onehot, band, rope = _constants()
    arrays = {
        "x": np.concatenate([x_prompt, x_sample]),
        "w_in": w_in[:, :, _columns()].reshape(L, KD, P, NC, P).transpose(0, 3, 2, 1, 4).reshape(L, NC, P, D),
        "w_out": w_out,
        "w_q": wq.reshape(L, 2, P, 512).transpose(0, 2, 1, 3).reshape(L, P, 1024),
        "w_kv": mla_w_kv_up[:, :, _kv_columns()],
        "w_pw": conf_w_pw.reshape(L, 2, P, GW).transpose(0, 2, 1, 3).reshape(L, P, 2 * GW),
        "par": par, "g_pre": g_pre, "g_post": g_post, "rel_bias": rel_bias,
        "onehot": onehot, "band": band, "rope": rope,
    }
    arrays = {n: np.ascontiguousarray(a) for n, a in arrays.items()}
    nc = bacc.Bacc("TRN2", target_bir_lowering=False, num_devices=1,
                   dynamic_dma_scratch_size=1024)
    ins = [nc.dram_tensor(n, a.shape, mybir.dt.from_np(a.dtype), kind="ExternalInput").ap() for n, a in arrays.items()]
    y = nc.dram_tensor("y", (S, T, D), F32, kind="ExternalOutput").ap()
    build(nc, *ins, y)
    out = run(nc, [arrays], core_ids=[0]).results[0]["y"]
    return out[0:1], out[1:2]
```

```python
import math
from contextlib import ExitStack

import numpy as np
import concourse.bass as bass
from concourse import mybir

F32 = mybir.dt.float32
F32R = mybir.dt.float32r
ACT = mybir.ActivationFunctionType
ALU = mybir.AluOpType
AX = mybir.AxisListType

P = 128
D = 1024
T = 1024
L = 2
S = 2
KD = D // P
NT = T // P
HALF = 512
GW = D // 4
HD = 64
HEADS = GW // HD
NOPE, ROPE = 64, 32
QR, KVR = 3 * D // 16, D // 8
TAPS_A, TAPS_C = 3, 31
PAD_C = (TAPS_C - 1) // 2
BUCKETS, WINDOW, MAX_DIST = 32, 128, 128
EPS = 1e-6
NEG = -1e30
EARLY = 4
B_SCALE = (NOPE + ROPE) ** -0.5
D_SCALE = HD ** -0.5

CHUNKS = ["dq0", "dq1", "dk", "dv", "dg0", "dg1",
          "cvb0", "cva0", "cvb1", "cva1", "cg0", "cg1",
          "ac0", "ah0", "ab0", "ag0", "ac1", "ah1", "ab1", "ag1",
          "bq0", "bq1", "bkv", "bg0", "bg1"]
C = {name: n for n, name in enumerate(CHUNKS)}
NC = len(CHUNKS)
LATER = ["dv_t", "pw0", "pw1", "bcast_kv", "rope", "rope_sw", "bv0", "bv1", "bk0", "bqn0"]
for _n, _name in enumerate(LATER):
    C[_name] = NC + _n
RAW = CHUNKS[:16] + ["w_pw"] + CHUNKS[16:] + ["w_q", "w_kv"] + [f"w_out{k}" for k in range(KD)]
POS = {name: n for n, name in enumerate(RAW)}
RAWS = 3
STATS = 3
XS = 4
XP = 6
XP0 = 2
PRE = 2
TH = ["dg0", "dg1", "cvb0", "cvb1", "cg0", "cg1", "ag0", "ag1", "bg0", "cz0", "cz1", "bg1"]
TH = {name: n + 1 for n, name in enumerate(TH)}
CAT = {"ag0": 0, "ag1": 1, "bg0": 2, "bg1": 3, "cg0": 4, "cg1": 5, "dg0": 6, "dg1": 7}

P_AW, P_AB = 0, 2 * TAPS_A
P_CW = P_AB + 2
P_CB = P_CW + 2 * TAPS_C
P_LG, P_LB = P_CB + 2, P_CB + 4
P_GQ, P_GKV = P_CB + 6, P_CB + 8
P_SINK = P_GKV + 1
P_N = P_SINK + HEADS

NB = HEADS * NT
HEAD_AT = {NT + 2: 2, NT + 3: 2, 2 * NT + 2: 3, 2 * NT + 3: 3}
B_SQ = {"bq1": 0, "bkv": 1, "bg0": 2}
K_AT = dict(zip(CHUNKS[3:], [(0, 0), (0, HD), (1, HD), (1, 0)]))
LAT_AT = {3: 0, 4: 1, 5: 2}
KE_AT = 6
UP_AT = {10: "w_q", 11: "w_kv"}
W_OUT_AT = {NB * 5 // 8 + 2 * k: k for k in range(EARLY)}


class Chain:

    def __init__(self, eng, sem):
        self.eng, self.sem, self.n = eng, sem, 0

    def add(self, ins):
        self.n += 1
        ins.then_inc(self.sem, 1)
        return self.n

    def wait(self, n=None):
        n = self.n if n is None else n
        if n > 0:
            self.eng.wait_ge(self.sem, n)


def build(nc, x, w_in, w_out, w_q, w_kv, w_pw, par, g_pre, g_post, rel_bias, onehot, band, rope, y):
    with ExitStack() as ctx:
        base = nc.sbuf_base
        top = [(base + 63) // 64 * 64]

        def region(kb):
            at = top[0]
            top[0] += int(kb * 1024)
            assert top[0] <= nc.sbuf_usable_end, (top[0], nc.sbuf_usable_end)
            return at

        def at(name, shape, dt, addr):
            return nc.alloc_sbuf_tensor_at(name, shape, dt, offset=addr)

        def sem(name):
            return ctx.enter_context(nc.semaphore(name))

        r_big = region(64)
        r_cat = region(32)
        r_stat = region(24)
        r_raw = region(12)
        r_x = region(16)
        r_u = region(8.25)
        r_d = region(16)
        r_b = region(12)
        r_bias = region(6)
        r_rope = region(8)
        r_g = region(4)
        r_pw = region(4)
        r_small = region(3)
        r_xp = region(4 * XP0)
        r_gpre = region(4)

        K = 1024
        hT = at("hT", [P, 2, KD, T], F32R, r_big)
        woR = [at(f"woR{k}", [P, 2, D], F32R, a) for k, a in enumerate(
            [r_b, r_u, r_big + 56 * K, r_stat + 16 * K] + [r_big + 8 * K * k for k in range(KD - EARLY)])]
        Qst = at("Qst", [P, HEADS, T], F32R, r_big)
        Kst = [[at(f"Kst{kv}{part}", [P, T], F32R, a) for part, a in enumerate(places)]
               for kv, places in enumerate(((r_xp, r_xp + 4 * K), (r_g, r_gpre)))]
        biasR = at("biasR", [P, 2, HEADS, 384], F32R, r_big + 16 * K)
        Vd = at("Vd", [P, NT, 2, 2, HD], F32R, r_big + 32 * K)
        Pd = at("Pd", [P, 2, 2, 384], F32, r_big + 40 * K)
        PTd = at("PTd", [P, 3, 2, 768], F32R, r_big + 46 * K)
        Vb = at("Vb", [P, NT, HEADS, 2, HD], F32R, r_big)
        PTb = at("PTb", [P, 2, 2, NT, 256], F32R, r_big + 16 * K)
        Pb = at("Pb", [P, 2, T], F32, r_big + 48 * K)
        qrF = at("qrF", [P, 2, T], F32, r_big + 16 * K)
        qrR = at("qrR", [P, 2, T], F32R, r_big + 56 * K)
        cat = at("cat", [P, KD, T], F32, r_cat)
        stat = at("stat", [P, STATS, 2, KD, P], F32R, r_stat)
        statE = at("statE", [P, PRE, 2, KD, P], F32R, r_cat)
        catR = at("catR", [P, 2, 2, KD, P], F32R, r_stat)
        qlR = at("qlR", [P, 2, 2, T], F32R, r_stat)
        kvR = at("kvR", [P, 2, T], F32R, r_stat + 16 * K)
        raw = at("raw", [P, RAWS, 1024], F32, r_raw)
        xs = at("xs", [P, XS, D], F32, r_x)
        xp = at("xp", [P, XP0, D], F32, r_xp)
        xd = at("xd", [P, XP - XP0, D], F32, r_d)
        gpre = at("gpre", [P, D], F32, r_gpre)
        accC = at("accC", [P, 2, T], F32, r_x)
        cLo = at("cLo", [P, 2, T], F32R, r_x)
        th = at("th", [P, T], F32, r_x + 8 * K)
        aC = at("aC", [P, T], F32, r_x + 12 * K)
        Qo = at("Qo", [P, 2, T], F32R, r_x)
        Ko = at("Ko", [P, 2, T], F32R, r_x + 8 * K)
        UP = T + 2 * PAD_C + 2
        uC = at("uC", [P, 2, UP], F32, r_u)
        cHi = at("cHi", [P, 2, T], F32R, r_u)
        rbc = at("rbc", [P, T], F32, r_u)
        krt = at("krt", [P, T], F32, r_u + 4 * K)
        kF2 = at("kF2", [P, T], F32, r_stat + 16 * K)
        qF2 = at("qF2", [P, T], F32, r_stat)
        rawD = at("rawD", [P, 4, T], F32, r_d)
        Qe = at("Qe", [P, 2, T], F32R, r_d)
        Ke = at("Ke", [P, 2, T], F32R, r_d + 8 * K)
        rawB = at("rawB", [P, 3, T], F32, r_b)
        wup = at("wup", [P, 2, 3, 512], F32R, r_b)
        aU = at("aU", [P, T + 2], F32, r_b)
        bias = at("bias", [P, HEADS, 384], F32, r_bias)
        ropeT = at("ropeT", [P, 2, T], F32, r_rope)
        gvec = at("gvec", [P, D], F32, r_g)
        wpR = at("wpR", [P, 2, 2, GW], F32R, r_pw)

        small = [r_small]

        def sm(name, cols, dt=F32, rows=P):
            t = at(name, [rows, cols], dt, small[0])
            small[0] += (4 * cols + 31) // 32 * 32
            assert small[0] <= top[0]
            return t

        ident = sm("ident", P)
        identR = sm("identR", P, F32R)
        ones = sm("ones", 2)
        expo = sm("expo", NT)
        parT = sm("parT", P_N)
        ss = sm("ss", NT)
        rs = sm("rs", NT)
        cvar = sm("cvar", NT)
        crs = sm("crs", NT)
        bvar = sm("bvar", 3 * NT)
        brs = sm("brs", 2 * NT)
        rsq = sm("rsq", NT)
        ngs = sm("ngs", HEADS)
        oss = sm("oss", NT)
        ors = sm("ors", NT)
        dmx = sm("dmx", 4)
        dnm = sm("dnm", 4)
        dsm = sm("dsm", 4 * NT)
        dex = sm("dex", 4 * NT)
        drc = sm("drc", 4 * NT)
        bmx = sm("bmx", NB)
        bnb = sm("bnb", NB)
        bsm = sm("bsm", NB)
        brc = sm("brc", NB)
        tmpD = at("tmpD", [P, 2, P], F32, r_pw)
        tmpB = at("tmpB", [P, 2, 256], F32, r_pw)
        rbB = at("rbB", [P, 2, 256], F32, r_pw + 2 * K)
        junk = at("junk", [P, D], F32, r_b + 8 * K)
        oh = at("oh", [BUCKETS, 512], F32, r_cat + 16 * K)
        rb = at("rb", [BUCKETS, HEADS], F32, r_cat + 18 * K)
        bandT = at("bandT", [HEADS, 512], F32, r_cat + 20 * K)
        bvec = at("bvec", [HEADS, 512], F32, r_cat + 22 * K)

        ps = ctx.enter_context(nc.psum_tensor("ps", [P, 8, 512], F32))
        vec_dram = nc.dram_tensor("bias_by_distance", (HEADS, P, 512), F32, kind="Internal")

        def x_tile(n):
            return xp[:, n, :] if n < XP0 else xd[:, n - XP0, :] if n < XP else xs[:, (n - XP) % XS, :]

        def square_x(act, n, signal):
            act.activation(junk[:, :], x_tile(n), ACT.Square, accum_out=ss[:, n:n + 1]).then_inc(signal, 1)

        def rstd_x(pool, n, own, signal):
            own.add(pool.tensor_scalar(ss[:, n:n + 1], ss[:, n:n + 1], 1.0 / D, EPS, ALU.mult, ALU.add))
            own.wait()
            pool.tensor_tensor(rs[:, n:n + 1], ss[:, n:n + 1], expo[:, 0:1], ALU.pow).then_inc(signal, 1)

        def norm_x(dve, n, signal):
            dve.scalar_tensor_tensor(x_tile(n), x_tile(n), rs[:, n:n + 1], gpre[:, :],
                                     ALU.mult, ALU.mult).then_inc(signal, 1)

        def first_hi(act, c, signal):
            act.activation(statE[:, c, 0, :, :], raw[:, c, :].rearrange("p (k m) -> p k m", m=P), ACT.Copy
                           ).then_inc(signal, 1)

        def first_lo(dve, c, signal):
            dve.tensor_tensor(statE[:, c, 1, :, :], raw[:, c, :].rearrange("p (k m) -> p k m", m=P),
                              statE[:, c, 0, :, :].bitcast(F32), ALU.subtract).then_inc(signal, 1)

        def transpose_x(pe, n, signal):
            b = 4 + 2 * (n % 2)
            for k in range(KD):
                last = pe.transpose(ps[:, b + k // 4, k % 4 * P:(k % 4 + 1) * P],
                                    x_tile(n)[:, k * P:(k + 1) * P], ident[:, :])
            last.then_inc(signal, 1)

        p_ld, p_st, p_rd, p_id, p_mm, p_bv, p_x, p_sq, p_own, p_rs, p_xn, p_ex, p_raw, p_whi, p_wlo, p_xt, p_bias = (sem(n) for n in (
            "p_ld", "p_st", "p_rd", "p_id", "p_mm", "p_bv", "p_x", "p_sq", "p_own", "p_rs", "p_xn", "p_ex",
            "p_raw", "p_whi", "p_wlo", "p_xt", "p_bias"))
        with nc.Block() as block:
            @block.gpsimd
            def _(pool):
                pool.memset(ident[:, :], 0.0).then_inc(p_id, 1)
                pool.memset(ones[:, :], 1.0)
                pool.memset(expo[:, :], -0.5).then_inc(p_ex, 1)
                pool.wait_ge(p_id, 1)
                pool.affine_select(out=ident[:, :], in_=ident[:, :], compare_op=ALU.not_equal, fill=1.0,
                                   base=0, pattern=[[-1, P]], channel_multiplier=1).then_inc(p_id, 1)
                own = Chain(pool, p_own)
                pool.wait_ge(p_ex, 1)
                for n in range(XP):
                    pool.wait_ge(p_sq, n + 1)
                    rstd_x(pool, n, own, p_rs)

            @block.sync
            def _(sp):
                for n in range(XP):
                    sp.dma_start(x_tile(n), x[0, n * P:(n + 1) * P, :]).then_inc(p_x, 16)
                sp.dma_start(gpre[:, :], g_pre[0:1].broadcast_to([P, D])).then_inc(p_x, 16)
                sp.dma_start(oh[:, :], onehot).then_inc(p_ld, 16)
                sp.dma_start(rb[:, :], rel_bias).then_inc(p_ld, 16)
                sp.dma_start(bandT[:, :], band).then_inc(p_ld, 16)
                sp.dma_start(ropeT[:, :, :], rope.rearrange("a p t -> p a t")).then_inc(p_rd, 16)
                sp.wait_ge(p_bv, 1)
                sp.dma_start(vec_dram.ap(), bvec[:, :].unsqueeze(1).broadcast_to([HEADS, P, 512])).then_inc(p_st, 16)
                sp.wait_ge(p_st, 16)
                sp.dma_start(bias[:, :, :], bass.AP(vec_dram, P - 1, [[511, P], [512 * P, HEADS], [1, 384]])
                             ).then_inc(p_bias, 16)
                for i in range(RAWS):
                    sp.dma_start(raw[:, i, :], w_in[0, i]).then_inc(p_raw, 16)
                sp.dma_start(parT[:, :], par[0]).then_inc(p_rd, 16)
                sp.wait_ge(p_rd, 16 * (1 + 1))

            @block.tensor
            def _(pe):
                pe.wait_ge(p_ld, 48)
                pe.matmul(ps[0:HEADS, 0, :], rb[:, :], oh[:, :], start=True, stop=True).then_inc(p_mm, 1)
                pe.wait_ge(p_id, 2)
                for n in range(PRE):
                    pe.wait_ge(p_xn, n + 1)
                    transpose_x(pe, n, p_xt)

            @block.vector
            def _(dve):
                dve.wait_ge(p_mm, 1)
                dve.tensor_tensor(bvec[:, :], ps[0:HEADS, 0, :], bandT[:, :], ALU.add).then_inc(p_bv, 1)
                for n in range(XP):
                    dve.wait_ge(p_rs, n + 1)
                    norm_x(dve, n, p_xn)
                for c in range(PRE):
                    dve.wait_ge(p_whi, c + 1)
                    first_lo(dve, c, p_wlo)
                dve.wait_ge(p_bias, 16)
                dve.tensor_scalar(bias[:, :, :], bias[:, :, :], 1 / D_SCALE, None, ALU.mult)

            @block.scalar
            def _(act):
                act.wait_ge(p_x, 16 * (XP + 1))
                for n in range(XP):
                    if n >= 1:
                        act.wait_ge(p_sq, n)
                    square_x(act, n, p_sq)
                act.wait_ge(p_id, 2)
                act.activation(identR[:, :], ident[:, :], ACT.Copy)
                act.wait_ge(p_raw, 16 * RAWS)
                for c in range(PRE):
                    first_hi(act, c, p_whi)

        names = ("next_ld nwhi nwlo nxt_ok nx0_ld nx1_ld nsq_ok nrs_ok nxn_ok gpost_ld sq_ok rs_ok xn_ok xt_ok hhi hlo whi wlo ch_done th_ok th_used "
                 "own_dve own_pool conv_own conv_ok st_cp xsum_ok xc_ok xsq_ok cvar_ok crs_ok y_ok "
                 "chi_ok clo_ok st_b bsq_ok bstat_ok brs_ok dst_hi dst_lo kd_hi kd_lo vd_hi vd_lo lat_hi lat_lo kr_ok "
                 "ke_hi ke_lo ko_ok zero_ok ds_mm bias_hi bias_lo dm_ok de_ok dr_ok dt_mm dpt_hi dpt_lo do_mm do_tmp do_ok "
                 "vb_hi vb_lo qr_ok qr_hi qr_lo kt_ok k_hi k_lo q_hi q_lo qrope_ok up2 kf2_ok qf2_ok "
                 "bs_mm bm_ok be_ok br_ok bt_mm bpt_hi bpt_lo bo_mm bo_tmp bo_ok "
                 "chi2 clo2 o_mm osq_ok ovar_ok ors_ok o1_ok o2_ok "
                 "free0 free1").split()
        q = {n: sem(n) for n in names}
        x_ld = [sem(f"x_ld{i}") for i in range(XS)]
        y_st = [sem(f"y_st{i}") for i in range(XS)]
        w_ld = [sem(f"w_ld{i}") for i in range(RAWS)]
        per_pass = list(q.values()) + x_ld + y_st + w_ld

        read_by = {"dv_t": ("vd_lo", 1), "bv0": ("vb_lo", NT // 2), "bv1": ("vb_lo", NT)}
        read_by |= {"bk0": ("kt_ok", 1), "bqn0": ("q_lo", 2)}
        for p in range(2):
            read_by |= {f"cva{p}": ("th_used", TH[f"cvb{p}"]), f"cvb{p}": ("th_ok", TH[f"cvb{p}"])}
        read_by |= {name: ("th_used", TH[name]) for name in CAT}
        counts = [0, 0]
        by_number = {n: name for name, n in C.items()}
        for n in sorted(by_number):
            if by_number[n] not in read_by:
                counts[n % 2] += 1
                read_by[by_number[n]] = (f"free{n % 2}", counts[n % 2])

        def x_landed(n):
            return x_ld[(n - XP) % XS], 16 * ((n - XP) // XS + 1)

        def residual_landed(n):
            before = len([m for m in range(XP, NT) if (m - XP) % XS == n % XS])
            return x_ld[n % XS], 16 * (before + n // XS + 1)

        def free_at(name):
            s_, value = read_by[name]
            return q[s_], value

        def pair(c):
            return ps[:, 2 * (c % 2):2 * (c % 2) + 2, :].rearrange("p b n -> p (b n)")

        def chunk_ps(name):
            return pair(C[name])

        def keys(n):
            k0, k1 = max(0, n - 1), min(NT - 1, n + 1)
            return k0, k1 - k0 + 1, (k0 - n + 1) * P

        DU = [(n, kv) for n in range(NT) for kv in range(2)]

        CONV_STEPS = {C["cg0"] + i: t for i, t in enumerate(
            np.array_split(np.arange(TAPS_C), C["bq0"] - C["cg0"]))}

        with nc.Fori(0, L) as layer:
          with nc.Fori(0, S) as seq:
            with nc.Block() as block:

                @block.sync
                def _(sp):
                    lay = bass.ds(layer, 1)
                    sq_ = bass.ds(seq, 1)

                    def load_g(src, s_):
                        sp.dma_start(gvec[:, :], src[lay].broadcast_to([P, D])).then_inc(s_, 16)

                    def load_x(src, n, slot):
                        sp.dma_start(xs[:, slot, :], src[sq_, n * P:(n + 1) * P, :]
                                     .rearrange("o p d -> (o p) d")).then_inc(x_ld[slot], 16)

                    def load_norm(src):
                        for n in range(XP, NT):
                            load_x(src, n, (n - XP) % XS)

                    def prefetch(src, seq_, lay_):
                        for n in range(XP0):
                            load_next(src, seq_, n, q["nx0_ld"])
                        sp.dma_start(gpre[:, :], g_pre[lay_].broadcast_to([P, D])).then_inc(q["nx0_ld"], 16)
                        for i in range(RAWS):
                            sp.dma_start(raw[:, i, :], w_in[lay_, i].rearrange("o p n -> (o p) n")
                                         ).then_inc(q["next_ld"], 16)
                        sp.dma_start(parT[:, :], par[lay_].rearrange("o p c -> (o p) c")).then_inc(q["next_ld"], 16)

                    def prefetch_rest(src, seq_):
                        for n in range(XP0, XP):
                            load_next(src, seq_, n, q["nx1_ld"])

                    def load_next(src, seq_, n, signal):
                        sp.dma_start(x_tile(n), src[seq_, n * P:(n + 1) * P, :].rearrange("o p d -> (o p) d")
                                     ).then_inc(signal, 16)

                    def load_raw(name):
                        i = POS[name]
                        if i >= RAWS + PRE:
                            sp.wait_ge(q["wlo"], i - RAWS + 1 - PRE)
                        dst = raw[:, i % RAWS, :]
                        if name in CHUNKS:
                            src = w_in[lay, C[name]].rearrange("o p n -> (o p) n")
                        elif name == "w_pw":
                            dst, src = dst[:, 0:2 * GW], w_pw[lay].rearrange("o p n -> (o p) n")
                        elif name == "w_q":
                            src = w_q[lay].rearrange("o p n -> (o p) n")
                        elif name == "w_kv":
                            dst, src = dst[:, 0:512], w_kv[lay].rearrange("o p n -> (o p) n")
                        else:
                            k = int(name[5:])
                            src = w_out[lay, k * P:(k + 1) * P, :].rearrange("o p n -> (o p) n")
                        sp.dma_start(dst, src).then_inc(w_ld[i % RAWS], 16)

                    with sp.If(layer < 1):
                        load_norm(x)
                    with sp.Else():
                        load_norm(y)

                    for name in RAW[RAWS:-1]:
                        load_raw(name)
                    sp.wait_ge(q["ds_mm"], 2 * NT)
                    load_g(g_post, q["gpost_ld"])

                    def residual(src, tiles):
                        for n in tiles:
                            if n < XS:
                                sp.wait_ge(q["bs_mm"], NB)
                            else:
                                store(n - XS)
                                sp.wait_ge(y_st[n % XS], 16)
                            load_x(src, n, n % XS)

                    def store(n):
                        sp.wait_ge(q["o2_ok"], n + 1)
                        sp.dma_start(y[sq_, n * P:(n + 1) * P, :].rearrange("o p d -> (o p) d"),
                                     xs[:, n % XS, :]).then_inc(y_st[n % XS], 16)

                    def for_next(what):
                        with sp.If(seq < 1):
                            with sp.If(layer < 1):
                                what(x, bass.ds(1, 1), lay)
                            with sp.Else():
                                what(y, bass.ds(1, 1), lay)
                        with sp.Else():
                            what(y, bass.ds(0, 1), bass.ds(L - 1, 1))

                    def for_this(what, tiles):
                        with sp.If(layer < 1):
                            what(x, tiles)
                        with sp.Else():
                            what(y, tiles)

                    for_this(residual, range(XS))
                    load_raw(RAW[-1])
                    sp.wait_ge(q["wlo"], len(RAW) - PRE)
                    for_next(prefetch)
                    for_next(lambda src, seq_, lay_: prefetch_rest(src, seq_))
                    for_this(residual, range(XS, NT))
                    for n in range(NT - XS, NT):
                        store(n)
                    sp.wait_ge(q["next_ld"], 16 * (RAWS + 1))
                    sp.wait_ge(q["nx0_ld"], 16 * (XP0 + 1))
                    sp.wait_ge(q["nx1_ld"], 16 * (XP - XP0))
                    for i in range(XS):
                        sp.wait_ge(y_st[i], 16 * (NT // XS))

                @block.tensor
                def _(pe):
                    mm, tr = pe.matmul, pe.transpose
                    three = ((0, 0), (0, 1), (1, 0))

                    def x_transpose(n):
                        if n >= XP:
                            pe.wait_ge(q["xn_ok"], n - XP + 1)
                        pe.wait_ge(q["hlo"], n - 1)
                        transpose_x(pe, n, q["xt_ok"])

                    def wait_pair(c):
                        if c >= 2:
                            pe.wait_ge(*free_at(by_number[c - 2]))

                    def project(name, halves=(0, 1), blocks=range(KD)):
                        c = C[name]
                        if c >= PRE:
                            pe.wait_ge(q["wlo"], POS[name] + 1 - PRE)
                        w = statE[:, c] if c < PRE else stat[:, c % STATS]
                        wait_pair(c)
                        for k in blocks:
                            for a, b in three:
                                for h in halves:
                                    last = mm(ps[:, 2 * (c % 2) + h, :], w[:, a, k, :],
                                              hT[:, b, k, h * HALF:(h + 1) * HALF],
                                              start=(k == 0 and (a, b) == (0, 0)),
                                              stop=(k == KD - 1 and (a, b) == (1, 0)))
                        if halves[-1] and blocks[-1] == KD - 1:
                            last.then_inc(q["ch_done"], 1)

                    def column_sums(bank, col, t):
                        for n in range(NT):
                            last = mm(ps[:, bank, col + n:col + n + 1], t[:, n * P:(n + 1) * P],
                                      ones[0:t.shape[0], 0:1], start=True, stop=True)
                        return last

                    def spread(dst, src):
                        for n in range(NT):
                            last = tr(dst[:, n * P:(n + 1) * P], src[:, n:n + 1].broadcast_to([P, P]),
                                      ident[:, :])
                        return last

                    bank45 = ps[:, 4:6, :].rearrange("p b n -> p (b n)")
                    bank67 = ps[:, 6:8, :].rearrange("p b n -> p (b n)")
                    for n in range(PRE, NT // 2):
                        x_transpose(n)
                    pe.wait_ge(q["hlo"], NT // 2)
                    project(CHUNKS[0], (0,))
                    x_transpose(NT // 2)
                    x_transpose(NT // 2 + 1)
                    project(CHUNKS[1], (0,), range(KD // 2))
                    x_transpose(NT // 2 + 2)
                    x_transpose(NT // 2 + 3)
                    project(CHUNKS[1], (0,), range(KD // 2, KD))
                    pe.wait_ge(q["hlo"], NT)
                    for name in CHUNKS:
                        halves = (1,) if name in CHUNKS[:2] else (0, 1)
                        project(name, halves, range(KD // 2))
                        if name == "bq1":
                            pe.wait_ge(q["conv_ok"], 2)
                            for h in range(2):
                                for j in range(2):
                                    last = mm(ps[:, 4 + h, :], ones[:, 0:1].broadcast_to([P, P]),
                                              accC[:, j, h * HALF:(h + 1) * HALF], start=(j == 0), stop=(j == 1))
                            last.then_inc(q["st_cp"], 1)
                        if name == "bkv":
                            pe.wait_ge(q["xsum_ok"], 1)
                            column_sums(6, 0, uC[:, 0, 0:T]).then_inc(q["st_cp"], 1)
                        if name == "bg0":
                            pe.wait_ge(q["crs_ok"], 1)
                            spread(bank45, crs).then_inc(q["st_cp"], 1)
                        project(name, halves, range(KD // 2, KD))
                        if name in B_SQ:
                            j = B_SQ[name]
                            pe.wait_ge(q["bsq_ok"], j + 1)
                            if j:
                                pe.wait_ge(q["bstat_ok"], j)
                            column_sums(7, j * NT, aC[0:(P, QR - P, P)[j], :]).then_inc(q["st_b"], 1)

                    wait_pair(C["dv_t"])
                    for n in range(NT):
                        last = tr(chunk_ps("dv_t")[:, n * P:(n + 1) * P], rawD[:, 3, n * P:(n + 1) * P],
                                  ident[:, :])
                    last.then_inc(q["ch_done"], 1)
                    pe.wait_ge(q["clo_ok"], 2)
                    for m in range(2):
                        c = C[f"pw{m}"]
                        wait_pair(c)
                        for j in range(2):
                            for a, b in three:
                                z = (cHi, cLo)[b]
                                for h in range(2):
                                    last = mm(ps[:, 2 * (c % 2) + h, :], wpR[:, a, j, m * P:(m + 1) * P],
                                              z[:, j, h * HALF:(h + 1) * HALF],
                                              start=(j == 0 and (a, b) == (0, 0)),
                                              stop=(j == 1 and (a, b) == (1, 0)))
                        last.then_inc(q["ch_done"], 1)
                    pe.wait_ge(q["brs_ok"], 1)
                    wait_pair(C["bcast_kv"])
                    spread(chunk_ps("bcast_kv"), brs[:, NT:2 * NT]).then_inc(q["ch_done"], 1)

                    def d_scores(u):
                        n, kv = DU[u]
                        k0, nk, b0 = keys(n)
                        if u >= 2:
                            pe.wait_ge(q["de_ok"], u - 1)
                        else:
                            pe.wait_ge(*free_at(("bcast_kv", "pw1")[u]))
                            pe.wait_ge(q["dst_lo"], 2 * kv + 2)
                        if u < 2:
                            pe.wait_ge(q["bias_lo"], kv + 1)
                        for g in range(2):
                            h = 2 * kv + g
                            for part in range(2):
                                mm(ps[:, 2 * (u % 2) + g, 0:nk * P], Qst[:, h, n * P:(n + 1) * P],
                                   Kst[kv][part][:, k0 * P:(k0 + nk) * P], start=(part == 0), stop=False)
                            for part in range(2):
                                last = mm(ps[:, 2 * (u % 2) + g, 0:nk * P], identR[:, :],
                                          biasR[:, part, h, b0:b0 + nk * P], start=False, stop=(part == 1))
                        last.then_inc(q["ds_mm"], 1)

                    def d_transpose(u):
                        n, kv = DU[u]
                        _, nk, _ = keys(n)
                        pe.wait_ge(q["de_ok"], u + 1)
                        if u >= 1:
                            pe.wait_ge(q["dpt_lo"], u)
                        else:
                            pe.wait_ge(q["y_ok"], 2)
                        for b in range(nk):
                            for g in range(2):
                                last = tr(bank45[:, (2 * b + g) * P:(2 * b + g + 1) * P],
                                          Pd[:, u % 2, g, b * P:(b + 1) * P], ident[:, :])
                        last.then_inc(q["dt_mm"], 1)

                    def d_out(n):
                        k0, nk, _ = keys(n)
                        if n >= 1:
                            pe.wait_ge(q["do_ok"], n)
                        else:
                            pe.wait_ge(q["bstat_ok"], 3)
                            pe.wait_ge(q["vd_lo"], 1)
                        pe.wait_ge(q["dr_ok"], n + 1)
                        for kv in range(2):
                            u = 2 * n + kv
                            for g in range(2):
                                tr(ps[:, 6 + kv, (2 + g) * P:(3 + g) * P],
                                   drc[:, 2 * u + g:2 * u + g + 1].broadcast_to([P, P]), ident[:, :])
                        for kv in range(2):
                            pe.wait_ge(q["dpt_lo"], 2 * n + kv + 1)
                            for b in range(nk):
                                for part in range(2):
                                    last = mm(ps[:, 6 + kv, 0:2 * P], Vd[:, k0 + b, kv, :, :],
                                              PTd[:, (2 * n + kv) % 3, part, b * 2 * P:(b + 1) * 2 * P],
                                              start=(b == 0 and part == 0), stop=(b == nk - 1 and part == 1))
                        last.then_inc(q["do_mm"], 1)

                    def q_up(banks, col):
                        for kt, rows in ((0, P), (1, QR - P)):
                            for a, b in three:
                                for h in range(2):
                                    last = mm(banks[:, h * HALF:(h + 1) * HALF], wup[0:rows, a, kt, col:col + P],
                                              qlR[0:rows, kt, b, h * HALF:(h + 1) * HALF],
                                              start=(kt == 0 and (a, b) == (0, 0)),
                                              stop=(kt == 1 and (a, b) == (1, 0)))
                        return last

                    def rope_up(name, col):
                        pe.wait_ge(q["wlo"], POS["w_q"] + 1 - PRE)
                        pe.wait_ge(q["de_ok"], NU)
                        wait_pair(C[name])
                        q_up(chunk_ps(name), col).then_inc(q["ch_done"], 1)

                    pe.wait_ge(q["kd_lo"], 4)
                    NU = len(DU)
                    for i in range(NU + 2):
                        if i < NU:
                            d_scores(i)
                        if 1 <= i <= NU:
                            d_transpose(i - 1)
                        if i == NU:
                            rope_up("rope", GW)
                            rope_up("rope_sw", GW + P)
                        if i >= 3 and i % 2:
                            d_out((i - 3) // 2)

                    pe.wait_ge(q["wlo"], POS["w_kv"] + 1 - PRE)
                    for c, t0 in (("bv0", 0), ("bv1", NT // 2)):
                        wait_pair(C[c])
                        for i in range(NT // 2):
                            for a, b in three:
                                last = mm(chunk_ps(c)[:, i * GW:(i + 1) * GW],
                                          kvR[:, a, (t0 + i) * P:(t0 + i + 1) * P], wup[:, b, 2, GW:2 * GW],
                                          start=((a, b) == (0, 0)), stop=((a, b) == (1, 0)))
                        last.then_inc(q["ch_done"], 1)

                    def k_up(banks, p):
                        for a, b in three:
                            for h in range(2):
                                last = mm(banks[:, h * HALF:(h + 1) * HALF], wup[:, a, 2, p * P:(p + 1) * P],
                                          kvR[:, b, h * HALF:(h + 1) * HALF],
                                          start=((a, b) == (0, 0)), stop=((a, b) == (1, 0)))
                        return last

                    pe.wait_ge(q["dpt_lo"], NU)
                    k_up(bank45, 1).then_inc(q["up2"], 1)
                    pe.wait_ge(q["do_ok"], NT)
                    q_up(bank67, P).then_inc(q["up2"], 1)
                    wait_pair(C["bk0"])
                    k_up(chunk_ps("bk0"), 0).then_inc(q["ch_done"], 1)
                    wait_pair(C["bqn0"])
                    q_up(chunk_ps("bqn0"), 0).then_inc(q["ch_done"], 1)

                    def b_scores(u):
                        h, i = divmod(u, NT)
                        if i == 0:
                            pe.wait_ge(q["k_lo"], h + 1)
                            pe.wait_ge(q["q_lo"], h + 1)
                            pe.wait_ge(q["qrope_ok"], h + 1)
                            pe.wait_ge(q["ko_ok"], 1)
                            pe.wait_ge(q["zero_ok"], 2)
                        if u < 2:
                            pe.wait_ge(*free_at(("bqn0", "bk0")[u]))
                        if u >= 2:
                            pe.wait_ge(q["be_ok"], u - 1)
                        Q, Kk, rows = ((Qe, Ke, NOPE + ROPE), (Qo, Ko, P))[h % 2]
                        for a, b in three:
                            for half in range(2):
                                last = mm(ps[:, 2 * (u % 2) + half, :], Q[0:rows, a, i * P:(i + 1) * P],
                                          Kk[0:rows, b, half * HALF:(half + 1) * HALF],
                                          start=((a, b) == (0, 0)), stop=((a, b) == (1, 0)))
                        last.then_inc(q["bs_mm"], 1)

                    def b_transpose(u):
                        pe.wait_ge(q["be_ok"], u + 1)
                        for half in range(2):
                            if u >= 1:
                                pe.wait_ge(q["bpt_lo"], 2 * u + half - 1)
                            else:
                                pe.wait_ge(q["kf2_ok"], 1)
                            for k in range(NT // 2):
                                col = half * HALF + k * P
                                last = tr(ps[:, 4 + half, k * P:(k + 1) * P], Pb[:, u % 2, col:col + P], ident[:, :])
                            last.then_inc(q["bt_mm"], 1)

                    def b_out(w, half):
                        h = 2 * w // NT
                        bank = ps[:, 6 + w % 2, :]
                        if half == 0:
                            if w >= 2:
                                pe.wait_ge(q["bo_ok"], w - 1)
                            elif w == 0:
                                pe.wait_ge(q["qf2_ok"], 1)
                            pe.wait_ge(q["br_ok"], 2 * w + 2)
                            for i in range(2):
                                tr(bank[:, 256 + i * P:256 + (i + 1) * P],
                                   brc[:, 2 * w + i:2 * w + i + 1].broadcast_to([P, P]), ident[:, :])
                            pe.wait_ge(q["bpt_lo"], 4 * w + 4)
                        for k in range(half * NT // 2, (half + 1) * NT // 2):
                            for part in range(2):
                                last = mm(bank[:, 0:256], Vb[:, k, h, :, :], PTb[:, w % 2, part, k, :],
                                          start=(k == 0 and part == 0), stop=(k == NT - 1 and part == 1))
                        if half:
                            last.then_inc(q["bo_mm"], 1)

                    def out_product(n, blocks):
                        if blocks[0] == 0:
                            pe.wait_ge(q["clo2"], n + 1)
                            if n >= 2:
                                pe.wait_ge(q["o2_ok"], n - 1)
                        for k in blocks:
                            if n == 0:
                                pe.wait_ge(q["wlo"], POS[f"w_out{k}"] + 1 - PRE)
                            for a, b in three:
                                for h in range(2):
                                    last = mm(ps[:, 2 * (n % 2) + h, :], catR[:, n % 2, a, k, :],
                                              woR[k][:, b, h * HALF:(h + 1) * HALF],
                                              start=(k == 0 and (a, b) == (0, 0)),
                                              stop=(k == KD - 1 and (a, b) == (1, 0)))
                        if blocks[-1] == KD - 1:
                            last.then_inc(q["o_mm"], 1)

                    pe.wait_ge(q["vb_lo"], NT)
                    for i in range(NB + 3):
                        if i < NB:
                            b_scores(i)
                        if 1 <= i <= NB:
                            b_transpose(i - 1)
                        if i == NB + 1:
                            out_product(0, (0, 1))
                        if i >= 3:
                            b_out(*divmod(i - 3, 2))

                    out_product(0, range(2, KD))
                    for n in range(1, NT):
                        if n == NT - 1:
                            pe.wait_ge(q["bo_ok"], NB // 2)
                            for m in range(PRE):
                                pe.wait_ge(q["nxn_ok"], m + 1)
                                transpose_x(pe, m, q["nxt_ok"])
                        out_product(n, range(KD))

                @block.gpsimd
                def _(pool):
                    own = Chain(pool, q["own_pool"])

                    def rsqrt(dst, src, signal):
                        pool.tensor_tensor(dst, src, expo[:, 0:src.shape[1]], ALU.pow).then_inc(signal, 1)

                    for n in range(XP, NT):
                        pool.wait_ge(q["sq_ok"], n - XP + 1)
                        rstd_x(pool, n, own, q["rs_ok"])
                    pool.wait_ge(q["cvar_ok"], 1)
                    rsqrt(crs[:, :], cvar[:, :], q["crs_ok"])
                    pool.wait_ge(q["bstat_ok"], 3)
                    own.add(pool.tensor_tensor(brs[:, 0:NT], bvar[:, 0:NT], expo[:, :], ALU.pow))
                    rsqrt(brs[:, NT:2 * NT], bvar[:, 2 * NT:3 * NT], q["brs_ok"])
                    own.wait()
                    pool.tensor_scalar(rsq[:, :], brs[:, 0:NT], B_SCALE, None, ALU.mult).then_inc(q["brs_ok"], 1)
                    for kv in range(2):
                        pool.wait_ge(q["bias_hi"], kv + 1)
                        h = slice(2 * kv, 2 * kv + 2)
                        pool.tensor_tensor(biasR[:, 1, h, :], bias[:, h, :], biasR[:, 0, h, :].bitcast(F32),
                                           ALU.subtract).then_inc(q["bias_lo"], 1)
                    pool.wait_ge(q["ch_done"], C["pw1"] + 1)
                    pool.wait_ge(q["th_used"], len(TH))
                    pool.memset(Ko[0:ROPE, :, :].bitcast(F32), 0.0).then_inc(q["zero_ok"], 1)
                    pool.memset(Qo[0:ROPE, :, :].bitcast(F32), 0.0).then_inc(q["zero_ok"], 1)
                    for n in range(NT):
                        pool.wait_ge(q["ovar_ok"], n + 1)
                        rsqrt(ors[:, n:n + 1], oss[:, n:n + 1], q["ors_ok"])
                        if 1 <= n <= XP:
                            pool.wait_ge(q["nsq_ok"], n)
                            rstd_x(pool, n - 1, own, q["nrs_ok"])

                @block.scalar
                def _(act):
                    bank45 = ps[:, 4:6, :].rearrange("p b n -> p (b n)")
                    bank67 = ps[:, 6:8, :].rearrange("p b n -> p (b n)")

                    def h_hi(n):
                        if n >= PRE:
                            act.wait_ge(q["xt_ok"], n - PRE + 1)
                        b = 4 + 2 * (n % 2)
                        act.activation(hT[:, 0, :, n * P:(n + 1) * P],
                                       ps[:, b:b + 2, :].rearrange("p b (k t) -> p (b k) t", t=P),
                                       ACT.Copy).then_inc(q["hhi"], 1)

                    def split_hi(name):
                        i = POS[name]
                        if i >= RAWS:
                            act.wait_ge(w_ld[i % RAWS], 16 * (i // RAWS))
                        src = raw[:, i % RAWS, :]
                        if name in CHUNKS:
                            c = C[name]
                            if c >= STATS + PRE:
                                act.wait_ge(q["ch_done"], c - STATS + 1)
                            dst, src = stat[:, c % STATS, 0, :, :], src.rearrange("p (k m) -> p k m", m=P)
                        elif name == "w_pw":
                            dst, src = wpR[:, 0, :, :], src[:, 0:2 * GW].rearrange("p (k m) -> p k m", m=GW)
                        elif name == "w_q":
                            dst, src = wup[:, 0, 0:2, :], src.rearrange("p (k m) -> p k m", m=512)
                        elif name == "w_kv":
                            dst, src = wup[:, 0, 2, :], src[:, 0:512]
                        else:
                            if name == "w_out0":
                                act.wait_ge(q["k_lo"], HEADS)
                                act.wait_ge(q["qrope_ok"], HEADS)
                            dst = woR[int(name[5:])][:, 0, :]
                        act.activation(dst, src, ACT.Copy).then_inc(q["whi"], 1)

                    def tanh_half(name, src):
                        n = TH[name]
                        if n > 1:
                            act.wait_ge(q["th_used"], n - 1)
                        return act.activation(th[:, :], src, ACT.Tanh, scale=0.5).then_inc(q["th_ok"], 1)

                    def evacuate(name):
                        kind = name.rstrip("01")
                        act_reads = kind in ("dq", "dk", "dv", "bq", "bkv", "ac", "cvb") or name in TH
                        if not act_reads:
                            return
                        act.wait_ge(q["ch_done"], C[name] + 1)
                        if name in TH:
                            tanh_half(name, chunk_ps(name))
                            return
                        if kind[0] == "d":
                            dst = rawD[:, C[name], :]
                        elif kind == "ac":
                            if name == "ac1":
                                act.wait_ge(q["th_used"], TH["ag0"])
                                act.wait_ge(*free_at("ag0"))
                            dst = aC[:, :]
                        else:
                            if name == "bq0":
                                act.wait_ge(*free_at("ag1"))
                            dst = rawB[:, C[name] - C["bq0"], :]
                        act.activation(dst, chunk_ps(name), ACT.Copy).then_inc(free_at(name)[0], 1)

                    def b_square(j):
                        rows = (P, QR - P, P)[j]
                        act.wait_ge(*free_at(("bq0", "bq1", "bkv")[j]))
                        if j:
                            act.wait_ge(q["st_b"], j)
                        act.activation(aC[0:rows, :], rawB[0:rows, j, :], ACT.Square).then_inc(q["bsq_ok"], 1)

                    for n in range(NT):
                        h_hi(n)
                        if n == 3:
                            for m in range(XP, NT):
                                act.wait_ge(*x_landed(m))
                                if m > XP:
                                    act.wait_ge(q["sq_ok"], m - XP)
                                square_x(act, m, q["sq_ok"])
                    ahead = [n for n in RAW if n in CHUNKS or n == "w_pw"][PRE:]
                    for c, name in enumerate(CHUNKS):
                        if ahead:
                            split_hi(ahead.pop(0))
                            if ahead and ahead[0] == "w_pw":
                                split_hi(ahead.pop(0))
                        if name == "bq1":
                            for j in range(2):
                                act.wait_ge(q["xc_ok"], j + 1)
                                act.activation(uC[:, j, 0:T], accC[:, j, :], ACT.Square).then_inc(q["xsq_ok"], 1)
                        evacuate(name)
                        if name in ("bq0", "bq1", "bkv"):
                            b_square(("bq0", "bq1", "bkv").index(name))
                        if name in K_AT:
                            kv, r2 = K_AT[name]
                            r = HD * kv
                            act.wait_ge(*free_at("dk"))
                            act.activation(Kst[kv][0][r2:r2 + HD, :], rawD[r:r + HD, 2, :], ACT.Copy).then_inc(q["kd_hi"], 1)
                        if name == "bg0":
                            for j in range(2):
                                act.wait_ge(q["y_ok"], j + 1)
                                tanh_half(f"cz{j}", accC[:, j, :])
                            for j in range(2):
                                act.wait_ge(q["th_used"], TH[f"cz{j}"])
                                if j == 0:
                                    act.wait_ge(q["st_cp"], 2)
                                act.activation(cHi[:, j, :], accC[:, j, :], ACT.Copy).then_inc(q["chi_ok"], 1)

                    act.wait_ge(q["ch_done"], NC)

                    def qd_hi(h):
                        r = HD * (h % 2)
                        act.activation(Qst[r:r + HD, h, :], rawD[r:r + HD, h // 2, :], ACT.Copy).then_inc(q["dst_hi"], 1)

                    for kv in range(2):
                        act.activation(biasR[:, 0, 2 * kv:2 * kv + 2, :], bias[:, 2 * kv:2 * kv + 2, :], ACT.Copy
                                       ).then_inc(q["bias_hi"], 1)
                        if kv == 0:
                            qd_hi(0)
                    act.wait_ge(q["ch_done"], C["dv_t"] + 1)
                    act.activation(Vd[:, :, :, 0, :], chunk_ps("dv_t").rearrange("p (t v d) -> p t v d", t=NT, v=2),
                                   ACT.Copy).then_inc(q["vd_hi"], 1)
                    for h in range(1, HEADS):
                        qd_hi(h)
                    act.wait_ge(q["ch_done"], C["bcast_kv"] + 1)
                    act.activation(rbc[:, :], chunk_ps("bcast_kv"), ACT.Copy).then_inc(free_at("bcast_kv")[0], 1)

                    def between(i):
                        if i in LAT_AT:
                            j = LAT_AT[i]
                            rows, dst = ((P, qlR[:, 0, 0, :]), (QR - P, qlR[0:QR - P, 1, 0, :]), (P, kvR[:, 0, :]))[j]
                            act.activation(dst, rawB[0:rows, j, :], ACT.Copy,
                                           scale=parT[0:rows, P_GQ + j:P_GQ + j + 1]).then_inc(q["lat_hi"], 1)
                        if i == KE_AT:
                            act.wait_ge(q["kr_ok"], 1)
                            act.wait_ge(q["dst_lo"], HEADS)
                            act.wait_ge(q["kd_lo"], 4)
                            act.activation(Ke[HD:HD + ROPE, 0, :], rawB[HD:HD + ROPE, 1, :], ACT.Copy).then_inc(q["ke_hi"], 1)
                        if i == KE_AT + 2:
                            act.wait_ge(q["ke_lo"], 1)
                            act.wait_ge(q["th_used"], len(TH))
                            act.wait_ge(q["bstat_ok"], 3)
                            act.activation(Ko[ROPE:2 * ROPE, :, :], Ke[HD:HD + ROPE, :, :].bitcast(F32), ACT.Copy).then_inc(q["ko_ok"], 1)
                        if i in UP_AT:
                            act.wait_ge(q["lat_lo"], 3)
                            act.wait_ge(q["ke_lo"], 1)
                            split_hi(UP_AT[i])

                    def d_exp(u):
                        n, kv = DU[u]
                        _, nk, _ = keys(n)
                        act.wait_ge(q["dm_ok"], u + 1)
                        if u >= 2:
                            act.wait_ge(q["dt_mm"], u - 1)
                        for g in range(2):
                            c, m = 2 * u + g, dnm[:, 2 * (u % 2) + g:2 * (u % 2) + g + 1]
                            act.activation(dex[:, c:c + 1], parT[:, P_SINK + 2 * kv + g:P_SINK + 2 * kv + g + 1],
                                           ACT.Exp, bias=m)
                            last = act.activation(Pd[:, u % 2, g, 0:nk * P], ps[:, 2 * (u % 2) + g, 0:nk * P], ACT.Exp,
                                                  bias=m, scale=D_SCALE, accum_out=dsm[:, c:c + 1])
                        last.then_inc(q["de_ok"], 1)

                    def d_hi(u):
                        n, kv = DU[u]
                        _, nk, _ = keys(n)
                        act.wait_ge(q["dt_mm"], u + 1)
                        if u >= 4:
                            act.wait_ge(q["do_mm"], (u - 3) // 2 + 1)
                        act.activation(PTd[:, u % 3, 0, 0:nk * 2 * P], bank45[:, 0:nk * 2 * P], ACT.Copy).then_inc(q["dpt_hi"], 1)

                    def d_half(n):
                        act.wait_ge(q["do_mm"], n + 1)
                        if n == 0:
                            act.wait_ge(q["ch_done"], C["pw1"] + 1)
                        else:
                            act.wait_ge(q["do_ok"], n)
                        act.activation(tmpD[0:HD, :, :], ps[HD:P, 6:8, 0:P], ACT.Copy)
                        act.activation(tmpD[HD:P, :, :], ps[0:HD, 6:8, P:2 * P], ACT.Copy).then_inc(q["do_tmp"], 1)

                    NU = len(DU)
                    for i in range(NU + 3):
                        if 1 <= i <= NU:
                            d_hi(i - 1)
                        if i < NU:
                            d_exp(i)
                        if i >= 3 and i % 2:
                            d_half((i - 3) // 2)
                        between(i)

                    act.wait_ge(q["qr_ok"], 1)
                    act.wait_ge(q["do_mm"], NT)
                    act.activation(qrR[:, 0, :], qrF[:, 0, :], ACT.Copy).then_inc(q["qr_hi"], 1)
                    act.wait_ge(q["brs_ok"], 2)
                    for n in range(NT):
                        name = ("bv0", "bv1")[2 * n // NT]
                        i = n % (NT // 2)
                        if i == 0:
                            act.wait_ge(q["ch_done"], C[name] + 1)
                        act.activation(Vb[:, n, :, 0, :], chunk_ps(name)[:, i * GW:(i + 1) * GW]
                                       .rearrange("p (h d) -> p h d", d=HD), ACT.Copy,
                                       scale=brs[:, NT + n:NT + n + 1]).then_inc(q["vb_hi"], 1)

                    def k_hi(h):
                        if h >= 2:
                            act.wait_ge(q["bs_mm"], (h - 1) * NT)
                        Kk, rows = ((Ke, slice(0, HD)), (Ko, slice(HD, P)))[h % 2]
                        act.wait_ge(*((q["kt_ok"], 1) if h < 2 else (q["kf2_ok"], 1)))
                        act.activation(Kk[rows, 0, :], (krt, kF2)[h // 2][rows, :], ACT.Copy).then_inc(q["k_hi"], 1)

                    def q_hi(h):
                        Q, rows = ((Qe, slice(0, HD)), (Qo, slice(HD, P)))[h % 2]
                        act.wait_ge(*((q["ch_done"], C["bqn0"] + 1) if h < 2 else (q["qf2_ok"], 1)))
                        act.activation(Q[rows, 0, :], (chunk_ps("bqn0"), qF2)[h // 2][rows, :], ACT.Copy).then_inc(q["q_hi"], 1)

                    def b_exp(u):
                        act.wait_ge(q["bm_ok"], u + 1)
                        if u >= 2:
                            act.wait_ge(q["bt_mm"], 2 * u - 2)
                        elif u == 0:
                            act.wait_ge(q["qr_lo"], 1)
                        act.activation(Pb[:, u % 2, :], pair(u), ACT.Exp, bias=bnb[:, u:u + 1],
                                       scale=rsq[:, u % NT:u % NT + 1], accum_out=bsm[:, u:u + 1]).then_inc(q["be_ok"], 1)

                    def b_hi(u):
                        w = u // 2
                        if w >= 2:
                            act.wait_ge(q["bo_mm"], w - 1)
                        for half in range(2):
                            act.wait_ge(q["bt_mm"], 2 * u + half + 1)
                            act.activation(PTb[:, w % 2, 0, half * NT // 2:(half + 1) * NT // 2, u % 2 * P:(u % 2 + 1) * P],
                                           ps[:, 4 + half, :].rearrange("p (k t) -> p k t", t=P), ACT.Copy
                                           ).then_inc(q["bpt_hi"], 1)

                    def b_half(w):
                        h = 2 * w // NT
                        act.wait_ge(q["bo_mm"], w + 1)
                        if w >= 2:
                            act.wait_ge(q["bo_ok"], w - 1)
                        r, o = ((0, HD), (HD, 0))[h % 2]
                        b = ps[:, 6 + w % 2, :]
                        act.activation(tmpB[r:r + HD, w % 2, :], b[o:o + HD, 0:256], ACT.Copy)
                        act.activation(rbB[r:r + HD, w % 2, :], b[r:r + HD, 256:512], ACT.Copy).then_inc(q["bo_tmp"], 1)

                    def cat_hi(n):
                        if n >= 2:
                            act.wait_ge(q["o_mm"], n - 1)
                        act.activation(catR[:, n % 2, 0, :, :], cat[:, :, n * P:(n + 1) * P], ACT.Copy).then_inc(q["chi2"], 1)

                    k_hi(0)
                    q_hi(0)
                    q_hi(1)
                    k_hi(1)
                    act.wait_ge(q["up2"], 2)
                    act.activation(qF2[:, :], bank67, ACT.Copy).then_inc(q["qf2_ok"], 1)
                    for i in range(NB + 4):
                        if i in HEAD_AT:
                            h = HEAD_AT[i]
                            (q_hi if i % 2 else k_hi)(h)
                        if 1 <= i <= NB:
                            b_hi(i - 1)
                        if i < NB:
                            b_exp(i)
                        if i >= 5 and i % 2 == 1:
                            b_half((i - 5) // 2)
                        if i in W_OUT_AT:
                            split_hi(f"w_out{W_OUT_AT[i]}")
                        if i in (NB, NB + 1):
                            act.wait_ge(q["bo_ok"], NB // 2 - NT // 2 + 1)
                            cat_hi(i - NB)
                    act.wait_ge(q["bo_mm"], NB // 2)
                    for k in range(EARLY, KD):
                        split_hi(f"w_out{k}")
                    act.wait_ge(q["bo_ok"], NB // 2)
                    for n in range(NT):
                        if n >= 1 and n + 1 < NT:
                            cat_hi(n + 1)
                        if n == NT - 1:
                            act.wait_ge(q["clo2"], NT)
                            act.wait_ge(q["next_ld"], 16 * (RAWS + 1))
                            for c in range(PRE):
                                first_hi(act, c, q["nwhi"])
                        act.wait_ge(q["o_mm"], n + 1)
                        if n >= 1:
                            act.wait_ge(q["osq_ok"], n)
                        if n >= 2:
                            act.wait_ge(q["nsq_ok"], min(n - 1, XP))
                        act.activation(junk[:, :], pair(n), ACT.Square, accum_out=oss[:, n:n + 1]).then_inc(q["osq_ok"], 1)
                        if 1 <= n <= XP:
                            act.wait_ge(*((q["nx0_ld"], 16 * (XP0 + 1)) if n <= XP0 else (q["nx1_ld"], 16 * (XP - XP0))))
                            act.wait_ge(q["osq_ok"], n + 1)
                            square_x(act, n - 1, q["nsq_ok"])

                @block.vector
                def _(dve):
                    own = Chain(dve, q["own_dve"])
                    conv = Chain(dve, q["conv_own"])
                    tt, ts, stt = dve.tensor_tensor, dve.tensor_scalar, dve.scalar_tensor_tensor
                    bank45 = ps[:, 4:6, :].rearrange("p b n -> p (b n)")

                    def minus(dst, a, hi):
                        return tt(dst, a, hi.bitcast(F32), ALU.subtract)

                    def h_lo(n):
                        dve.wait_ge(q["hhi"], n + 1)
                        b = 4 + 2 * (n % 2)
                        minus(hT[:, 1, :, n * P:(n + 1) * P],
                              ps[:, b:b + 2, :].rearrange("p b (k t) -> p (b k) t", t=P),
                              hT[:, 0, :, n * P:(n + 1) * P]).then_inc(q["hlo"], 1)

                    def split_lo(name):
                        i = POS[name]
                        dve.wait_ge(q["whi"], i + 1 - PRE)
                        src = raw[:, i % RAWS, :]
                        if name in CHUNKS:
                            s_ = stat[:, C[name] % STATS]
                            minus(s_[:, 1, :, :], src.rearrange("p (k m) -> p k m", m=P), s_[:, 0, :, :]).then_inc(q["wlo"], 1)
                        elif name == "w_pw":
                            minus(wpR[:, 1, :, :], src[:, 0:2 * GW].rearrange("p (k m) -> p k m", m=GW), wpR[:, 0, :, :]).then_inc(q["wlo"], 1)
                        elif name == "w_q":
                            minus(wup[:, 1, 0:2, :], src.rearrange("p (k m) -> p k m", m=512), wup[:, 0, 0:2, :]).then_inc(q["wlo"], 1)
                        elif name == "w_kv":
                            minus(wup[:, 1, 2, :], src[:, 0:512], wup[:, 0, 2, :]).then_inc(q["wlo"], 1)
                        else:
                            k = int(name[5:])
                            minus(woR[k][:, 1, :], src, woR[k][:, 0, :]).then_inc(q["wlo"], 1)

                    def gate(name):
                        dve.wait_ge(q["th_ok"], TH[name])
                        stt(cat[:, CAT[name], :], th[:, :], 1.0, chunk_ps(name), ALU.add, ALU.mult
                            ).then_inc(q["th_used"], 1)

                    def evacuate(name):
                        kind, j = name.rstrip("01"), int(name[-1]) if name[-1].isdigit() else 0
                        if kind == "cva":
                            dve.wait_ge(q["ch_done"], C[name] + 1)
                            dve.wait_ge(q["th_ok"], TH[f"cvb{j}"])
                            stt(uC[:, j, PAD_C:PAD_C + T], th[:, :], 1.0, chunk_ps(name), ALU.add, ALU.mult
                                ).then_inc(q["th_used"], 1)
                        elif kind == "ah":
                            dve.wait_ge(q["ch_done"], C[name] + 1)
                            dve.wait_ge(*free_at(f"ac{j}"))
                            tt(aU[:, 1:T + 1], chunk_ps(name), aC[:, :], ALU.mult).then_inc(free_at(name)[0], 1)
                            dve.wait_ge(*free_at(name))
                            own.wait()
                            w = P_AW + TAPS_A * j
                            own.add(ts(aC[:, :], aU[:, 0:T], parT[:, w:w + 1], parT[:, P_AB + j:P_AB + j + 1], ALU.mult, ALU.add))
                            for t in range(1, TAPS_A):
                                own.wait()
                                own.add(stt(aC[:, :], aU[:, t:t + T], parT[:, w + t:w + t + 1], aC[:, :], ALU.mult, ALU.add))
                        elif kind == "ab":
                            dve.wait_ge(q["ch_done"], C[name] + 1)
                            own.wait()
                            tt(aC[:, :], chunk_ps(name), aC[:, :], ALU.mult).then_inc(free_at(name)[0], 1)
                        elif kind == "ag":
                            dve.wait_ge(q["th_ok"], TH[name])
                            own.add(stt(cat[:, CAT[name], :], th[:, :], 1.0, chunk_ps(name), ALU.add, ALU.mult))
                            own.wait()
                            dve.wait_ge(*free_at(f"ab{j}"))
                            stt(cat[:, CAT[name], :], cat[:, CAT[name], :], 0.5, aC[:, :], ALU.mult, ALU.mult
                                ).then_inc(q["th_used"], 1)
                        elif kind[1:] == "g":
                            gate(name)

                    def conv_taps(taps):
                        for t in taps:
                            for j in range(2):
                                w = parT[:, P_CW + TAPS_C * j + int(t):P_CW + TAPS_C * j + int(t) + 1]
                                if t == 0:
                                    conv.add(ts(accC[:, j, :], uC[:, j, 0:T], w, None, ALU.mult))
                                else:
                                    conv.wait(conv.n - 1)
                                    conv.add(stt(accC[:, j, :], uC[:, j, int(t):int(t) + T], w, accC[:, j, :],
                                                 ALU.mult, ALU.add))

                    k_r, k_s = slice(HD, HD + ROPE), slice(HD + ROPE, P)

                    for n in range(NT):
                        h_lo(n)
                        if n == 3:
                            for m in range(XP, NT):
                                dve.wait_ge(q["rs_ok"], m - XP + 1)
                                norm_x(dve, m, q["xn_ok"])
                    own.add(dve.memset(aU[:, 0:1], 0.0))
                    own.add(dve.memset(aU[:, T + 1:T + 2], 0.0))
                    own.add(dve.memset(uC[:, :, 0:PAD_C], 0.0))
                    own.add(dve.memset(uC[:, :, PAD_C + T:UP], 0.0))
                    own.add(ts(ngs[:, :], parT[:, P_SINK:P_SINK + HEADS], -1.0, None, ALU.mult))

                    ahead = [n for n in RAW if n in CHUNKS or n == "w_pw"][PRE:]
                    for c, name in enumerate(CHUNKS):
                        if ahead:
                            split_lo(ahead.pop(0))
                            if ahead and ahead[0] == "w_pw":
                                split_lo(ahead.pop(0))
                        evacuate(name)
                        if c in CONV_STEPS:
                            if c == C["cg0"]:
                                dve.wait_ge(*free_at("cva0"))
                                dve.wait_ge(*free_at("cva1"))
                                own.wait()
                            conv_taps(CONV_STEPS[c])
                        if name in K_AT:
                            kv, r2 = K_AT[name]
                            r = HD * kv
                            dve.wait_ge(q["kd_hi"], list(K_AT).index(name) + 1)
                            minus(Kst[kv][1][r2:r2 + HD, :], rawD[r:r + HD, 2, :], Kst[kv][0][r:r + HD, :]).then_inc(q["kd_lo"], 1)
                        if name == "ag1":
                            conv.wait()
                            for j in range(2):
                                ts(accC[:, j, :], accC[:, j, :], 0.5, parT[:, P_CB + j:P_CB + j + 1],
                                   ALU.mult, ALU.add).then_inc(q["conv_ok"], 1)
                        if name == "bq1":
                            dve.wait_ge(q["st_cp"], 1)
                            dve.wait_ge(q["conv_ok"], 2)
                            for j in range(2):
                                stt(accC[:, j, :], bank45, -1.0 / GW, accC[:, j, :], ALU.mult, ALU.add
                                    ).then_inc(q["xc_ok"], 1)
                            dve.wait_ge(q["xsq_ok"], 2)
                            tt(uC[:, 0, 0:T], uC[:, 0, 0:T], uC[:, 1, 0:T], ALU.add).then_inc(q["xsum_ok"], 1)
                            dve.wait_ge(q["st_b"], 1)
                            ts(bvar[:, 0:NT], ps[:, 7, 0:NT], 1.0 / QR, EPS, ALU.mult, ALU.add).then_inc(q["bstat_ok"], 1)
                        if name == "bkv":
                            dve.wait_ge(q["st_cp"], 2)
                            ts(cvar[:, :], ps[:, 6, 0:NT], 1.0 / GW, EPS, ALU.mult, ALU.add).then_inc(q["cvar_ok"], 1)
                            dve.wait_ge(q["st_b"], 2)
                            dve.wait_ge(q["bstat_ok"], 1)
                            stt(bvar[:, 0:NT], ps[:, 7, NT:2 * NT], 1.0 / QR, bvar[:, 0:NT], ALU.mult, ALU.add
                                ).then_inc(q["bstat_ok"], 1)
                            dve.wait_ge(*free_at("bq1"))
                            own.add(tt(cat[k_r, 3, :], rawB[k_s, 1, :], ropeT[k_s, 1, :], ALU.mult))
                            own.add(tt(rawB[k_r, 1, :], rawB[k_r, 1, :], ropeT[k_r, 0, :], ALU.mult))
                            own.wait()
                            tt(rawB[k_r, 1, :], rawB[k_r, 1, :], cat[k_r, 3, :], ALU.add).then_inc(q["kr_ok"], 1)
                            dve.wait_ge(q["kr_ok"], 1)
                        if name == "bg0":
                            dve.wait_ge(q["st_cp"], 3)
                            for j in range(2):
                                own.add(tt(accC[:, j, :], accC[:, j, :], bank45, ALU.mult))
                            for j in range(2):
                                own.wait(own.n - 1 + j)
                                ts(accC[:, j, :], accC[:, j, :], parT[:, P_LG + j:P_LG + j + 1],
                                   parT[:, P_LB + j:P_LB + j + 1], ALU.mult, ALU.add).then_inc(q["y_ok"], 1)
                            dve.wait_ge(q["st_b"], 3)
                            ts(bvar[:, 2 * NT:3 * NT], ps[:, 7, 2 * NT:3 * NT], 1.0 / KVR, EPS, ALU.mult, ALU.add
                               ).then_inc(q["bstat_ok"], 1)
                            for j in range(2):
                                dve.wait_ge(q["th_ok"], TH[f"cz{j}"])
                                stt(accC[:, j, :], th[:, :], 1.0, accC[:, j, :], ALU.add, ALU.mult
                                    ).then_inc(q["th_used"], 1)
                            for j in range(2):
                                dve.wait_ge(q["chi_ok"], j + 1)
                                minus(cLo[:, j, :], accC[:, j, :], cHi[:, j, :]).then_inc(q["clo_ok"], 1)

                    def qd_lo(h):
                        r = HD * (h % 2)
                        dve.wait_ge(q["dst_hi"], h + 1)
                        minus(Qst[HD - r:P - r, h, :], rawD[r:r + HD, h // 2, :], Qst[r:r + HD, h, :]).then_inc(q["dst_lo"], 1)

                    qd_lo(0)
                    dve.wait_ge(q["vd_hi"], 1)
                    minus(Vd[:, :, :, 1, :], chunk_ps("dv_t").rearrange("p (t v d) -> p t v d", t=NT, v=2),
                          Vd[:, :, :, 0, :]).then_inc(q["vd_lo"], 1)
                    qd_lo(1)
                    for m in range(2):
                        dve.wait_ge(q["ch_done"], C[f"pw{m}"] + 1)
                        dve.wait_ge(*free_at(f"cg{m}"))
                        stt(cat[:, 4 + m, :], chunk_ps(f"pw{m}"), 0.25, cat[:, 4 + m, :], ALU.mult, ALU.mult
                            ).then_inc(free_at(f"pw{m}")[0], 1)
                        qd_lo(2 + m)

                    def between(i):
                        if i in LAT_AT:
                            j = LAT_AT[i]
                            rows, dst = ((P, qlR[:, 0, :, :]), (QR - P, qlR[0:QR - P, 1, :, :]), (P, kvR[:, :, :]))[j]
                            dve.wait_ge(q["lat_hi"], j + 1)
                            stt(dst[:, 1, :], rawB[0:rows, j, :], parT[0:rows, P_GQ + j:P_GQ + j + 1],
                                dst[:, 0, :].bitcast(F32), ALU.mult, ALU.subtract).then_inc(q["lat_lo"], 1)
                        if i == KE_AT:
                            dve.wait_ge(q["ke_hi"], 1)
                            minus(Ke[k_r, 1, :], rawB[k_r, 1, :], Ke[k_r, 0, :]).then_inc(q["ke_lo"], 1)
                        if i in UP_AT:
                            split_lo(UP_AT[i])

                    def d_max(u):
                        n, kv = DU[u]
                        _, nk, _ = keys(n)
                        s2 = 2 * (u % 2)
                        dve.wait_ge(q["ds_mm"], u + 1)
                        if u >= 2:
                            dve.wait_ge(q["de_ok"], u - 1)
                        own.add(dve.tensor_reduce(dmx[:, s2:s2 + 2], ps[:, s2:s2 + 2, 0:nk * P], AX.X, ALU.max))
                        own.wait()
                        stt(dnm[:, s2:s2 + 2], dmx[:, s2:s2 + 2], -D_SCALE, ngs[:, 2 * kv:2 * kv + 2],
                            ALU.mult, ALU.min).then_inc(q["dm_ok"], 1)

                    def d_recip(n):
                        c = slice(4 * n, 4 * n + 4)
                        dve.wait_ge(q["de_ok"], 2 * n + 2)
                        own.add(tt(dsm[:, c], dsm[:, c], dex[:, c], ALU.add))
                        own.wait()
                        dve.reciprocal(drc[:, c], dsm[:, c]).then_inc(q["dr_ok"], 1)

                    def d_lo(u):
                        n, kv = DU[u]
                        _, nk, _ = keys(n)
                        dve.wait_ge(q["dpt_hi"], u + 1)
                        minus(PTd[:, u % 3, 1, 0:nk * 2 * P], bank45[:, 0:nk * 2 * P],
                              PTd[:, u % 3, 0, 0:nk * 2 * P]).then_inc(q["dpt_lo"], 1)

                    def d_combine(n):
                        dve.wait_ge(q["do_tmp"], n + 1)
                        own.add(tt(tmpD[0:HD, :, :], ps[0:HD, 6:8, 0:P], tmpD[0:HD, :, :], ALU.add))
                        own.add(tt(tmpD[HD:P, :, :], ps[HD:P, 6:8, P:2 * P], tmpD[HD:P, :, :], ALU.add))
                        own.wait()
                        own.add(tt(tmpD[0:HD, :, :], ps[0:HD, 6:8, 2 * P:3 * P], tmpD[0:HD, :, :], ALU.mult))
                        own.add(tt(tmpD[HD:P, :, :], ps[HD:P, 6:8, 3 * P:4 * P], tmpD[HD:P, :, :], ALU.mult))
                        own.wait()
                        y_ = cat[:, 6:8, n * P:(n + 1) * P]
                        stt(y_, tmpD[:, :, :], 0.5, y_, ALU.mult, ALU.mult).then_inc(q["do_ok"], 1)

                    NU = len(DU)
                    for i in range(NU + 3):
                        if i < NU:
                            d_max(i)
                        if i >= 2 and i % 2 == 0 and i <= NU:
                            d_recip((i - 2) // 2)
                        if 1 <= i <= NU:
                            d_lo(i - 1)
                        if i == NU + 1:
                            for j, name in enumerate(("rope", "rope_sw")):
                                dve.wait_ge(q["ch_done"], C[name] + 1)
                                tt(qrF[:, j, :], chunk_ps(name), ropeT[:, j, :], ALU.mult).then_inc(free_at(name)[0], 1)
                        if i >= 4 and i % 2 == 0:
                            d_combine((i - 4) // 2)
                        between(i - 1)

                    dve.wait_ge(*free_at("rope"))
                    dve.wait_ge(*free_at("rope_sw"))
                    tt(qrF[:, 0, :], qrF[:, 0, :], qrF[:, 1, :], ALU.add).then_inc(q["qr_ok"], 1)
                    dve.wait_ge(q["qr_hi"], 1)
                    minus(qrR[:, 1, :], qrF[:, 0, :], qrR[:, 0, :]).then_inc(q["qr_lo"], 1)
                    dve.wait_ge(q["qr_lo"], 1)
                    dve.wait_ge(q["brs_ok"], 2)
                    for n in range(NT):
                        name = ("bv0", "bv1")[2 * n // NT]
                        i = n % (NT // 2)
                        dve.wait_ge(q["vb_hi"], (n | 1) + 1)
                        stt(Vb[:, n, :, 1, :], chunk_ps(name)[:, i * GW:(i + 1) * GW].rearrange("p (h d) -> p h d", d=HD),
                                brs[:, NT + n:NT + n + 1], Vb[:, n, :, 0, :].bitcast(F32), ALU.mult, ALU.subtract
                                ).then_inc(q["vb_lo"], 1)
                    def k_lo(h):
                        Kk, rows = ((Ke, slice(0, HD)), (Ko, slice(HD, P)))[h % 2]
                        dve.wait_ge(q["k_hi"], h + 1)
                        minus(Kk[rows, 1, :], (krt, kF2)[h // 2][rows, :], Kk[rows, 0, :]).then_inc(q["k_lo"], 1)

                    def q_lo(h):
                        Q, rows = ((Qe, slice(0, HD)), (Qo, slice(HD, P)))[h % 2]
                        dve.wait_ge(q["q_hi"], h + 1)
                        minus(Q[rows, 1, :], (chunk_ps("bqn0"), qF2)[h // 2][rows, :], Q[rows, 0, :]).then_inc(q["q_lo"], 1)

                    def q_rope(h):
                        if h >= 2:
                            dve.wait_ge(q["bs_mm"], (h - 1) * NT)
                        Q, r = ((Qe, HD), (Qo, ROPE))[h % 2]
                        dve.tensor_copy(Q[r:r + ROPE, :, :], qrR[ROPE * h:ROPE * (h + 1), :, :].bitcast(F32)).then_inc(q["qrope_ok"], 1)

                    def b_max(u):
                        dve.wait_ge(q["bs_mm"], u + 1)
                        own.add(dve.tensor_reduce(bmx[:, u:u + 1], pair(u), AX.X, ALU.max))
                        own.wait()
                        ts(bnb[:, u:u + 1], bmx[:, u:u + 1], rsq[:, u % NT:u % NT + 1], -1.0,
                           ALU.mult, ALU.mult).then_inc(q["bm_ok"], 1)

                    def b_lo(u):
                        w = u // 2
                        for half in range(2):
                            dve.wait_ge(q["bpt_hi"], 2 * u + half + 1)
                            dst = PTb[:, w % 2, :, half * NT // 2:(half + 1) * NT // 2, u % 2 * P:(u % 2 + 1) * P]
                            minus(dst[:, 1], ps[:, 4 + half, :].rearrange("p (k t) -> p k t", t=P), dst[:, 0]
                                  ).then_inc(q["bpt_lo"], 1)

                    def b_recip(u):
                        dve.wait_ge(q["be_ok"], u + 1)
                        dve.reciprocal(brc[:, u:u + 1], bsm[:, u:u + 1]).then_inc(q["br_ok"], 1)

                    def b_combine(w):
                        h, i = divmod(2 * w, NT)
                        dve.wait_ge(q["bo_tmp"], w + 1)
                        r = HD * (h % 2)
                        rows = slice(r, r + HD)
                        b, t = ps[:, 6 + w % 2, :], tmpB[rows, w % 2, :]
                        own.add(tt(t, b[rows, 0:256], t, ALU.add))
                        own.wait()
                        own.add(tt(t, t, rbB[rows, w % 2, :], ALU.mult))
                        own.wait()
                        y_ = cat[rows, 2 + h // 2, i * P:(i + 2) * P]
                        stt(y_, t, 0.5, y_, ALU.mult, ALU.mult).then_inc(q["bo_ok"], 1)

                    def cat_lo(n):
                        dve.wait_ge(q["chi2"], n + 1)
                        minus(catR[:, n % 2, 1, :, :], cat[:, :, n * P:(n + 1) * P], catR[:, n % 2, 0, :, :]).then_inc(q["clo2"], 1)

                    dve.wait_ge(q["ch_done"], C["bk0"] + 1)
                    own.wait()
                    dve.wait_ge(q["kr_ok"], 1)
                    dve.wait_ge(*free_at("bcast_kv"))
                    tt(krt[:, :], chunk_ps("bk0"), rbc[:, :], ALU.mult).then_inc(q["kt_ok"], 1)
                    q_rope(0)
                    k_lo(0)
                    q_lo(0)
                    q_lo(1)
                    dve.wait_ge(q["up2"], 1)
                    tt(kF2[:, :], bank45, rbc[:, :], ALU.mult).then_inc(q["kf2_ok"], 1)
                    for i in range(NB + 5):
                        if i < NB:
                            b_max(i)
                        if 1 <= i <= NB:
                            b_recip(i - 1)
                            b_lo(i - 1)
                        if i >= 6 and i % 2 == 0:
                            b_combine((i - 6) // 2)
                        if i in HEAD_AT:
                            h = HEAD_AT[i]
                            if i % 2:
                                q_lo(h)
                            else:
                                q_rope(h)
                                k_lo(h)
                        if i == 3:
                            q_rope(1)
                        if i == 5:
                            k_lo(1)
                        if i in W_OUT_AT:
                            split_lo(f"w_out{W_OUT_AT[i]}")
                        if i in (NB, NB + 1):
                            cat_lo(i - NB)

                    for k in range(EARLY, KD):
                        split_lo(f"w_out{k}")
                    dve.wait_ge(q["gpost_ld"], 16)
                    for n in range(NT):
                        if n >= 1 and n + 1 < NT:
                            cat_lo(n + 1)
                        if n == NT - 1:
                            for c in range(PRE):
                                dve.wait_ge(q["nwhi"], c + 1)
                                first_lo(dve, c, q["nwlo"])
                        dve.wait_ge(q["osq_ok"], n + 1)
                        ts(oss[:, n:n + 1], oss[:, n:n + 1], 1.0 / D, EPS, ALU.mult, ALU.add).then_inc(q["ovar_ok"], 1)
                        dve.wait_ge(q["ors_ok"], n + 1)
                        stt(pair(n), pair(n), ors[:, n:n + 1], gvec[:, :], ALU.mult, ALU.mult).then_inc(q["o1_ok"], 1)
                        dve.wait_ge(q["o1_ok"], n + 1)
                        dve.wait_ge(*residual_landed(n))
                        tt(xs[:, n % XS, :], xs[:, n % XS, :], pair(n), ALU.add).then_inc(q["o2_ok"], 1)
                        if 1 <= n <= XP:
                            dve.wait_ge(q["nrs_ok"], n)
                            norm_x(dve, n - 1, q["nxn_ok"])

            nc.all_engine_barrier()
            nc.sync.sem_clear(range(per_pass[0].num, per_pass[-1].num + 1))
            nc.all_engine_barrier()


def _buckets(rel):
    half = BUCKETS // 2
    exact = half // 2
    n = np.abs(rel)
    large = exact + (np.log(np.maximum(n, 1) / exact) / math.log(MAX_DIST / exact) * (half - exact)).astype(np.int32)
    large = np.minimum(large, half - 1)
    return (rel > 0).astype(np.int32) * half + np.where(n < exact, n, large).astype(np.int32)


def _constants():
    dist = np.arange(512) - 255
    onehot = (np.arange(BUCKETS)[:, None] == _buckets(dist)[None, :]).astype(np.float32)
    band = np.broadcast_to(np.where(np.abs(dist) <= WINDOW, 0.0, NEG).astype(np.float32), (HEADS, 512))
    inv = np.float32(10000.0) ** (-np.arange(0, ROPE, 2, dtype=np.float32) / np.float32(ROPE))
    ang = np.arange(T, dtype=np.float32)[None, :] * inv[:, None]
    cos, sin = np.cos(ang), np.sin(ang)
    rope = np.stack([np.tile(np.concatenate([cos, cos]), (4, 1)), np.tile(np.concatenate([-sin, sin]), (4, 1))])
    return onehot, np.ascontiguousarray(band), rope.astype(np.float32)


def _columns():
    sizes = [GW, GW, GW, GW, QR, KVR, ROPE, GW, GW, GW, GW, HEADS * HD, 2 * HD, 2 * HD, GW]
    names = ["ab", "ac", "ah", "ag", "bq", "bkv", "bkr", "bg", "cva", "cvb", "cg", "dq", "dk", "dv", "dg"]
    start = dict(zip(names, np.cumsum([0] + sizes[:-1])))
    out = []
    for name in CHUNKS:
        kind, j = name.rstrip("01"), int(name[-1]) if name[-1].isdigit() else 0
        if name == "bq1":
            kr = start["bkr"] + np.arange(ROPE)
            out.append(np.concatenate([start["bq"] + np.arange(P, QR), kr, np.roll(kr, -(ROPE // 2))]))
        else:
            out.append(start[kind] + j * P + np.arange(P))
    return np.stack(out)


def _q_columns():
    h = np.arange(HEADS)[:, None] * (NOPE + ROPE)
    rot = NOPE + np.arange(ROPE)
    return np.concatenate([(h + np.arange(NOPE)).ravel(), (h + rot).ravel(), (h + np.roll(rot, -(ROPE // 2))).ravel()])


def _kv_columns():
    h = np.arange(HEADS)[:, None] * 2 * HD
    return np.concatenate([(h + np.arange(HD)).ravel(), (h + HD + np.arange(HD)).ravel()])


def kernel(x_prompt, x_sample, g_pre, g_post, w_in, w_out, conv_a_w, conv_a_b, mla_g_q, mla_w_q_up,
           mla_g_kv, mla_w_kv_up, conf_w_dw, conf_b_dw, conf_ln_g, conf_ln_b, conf_w_pw, swa_sink, rel_bias):
    import concourse.bacc as bacc
    from concourse.bass_utils import run_bass_kernel_spmd as run

    (x_prompt, x_sample, g_pre, g_post, w_in, w_out, conv_a_w, conv_a_b, mla_g_q, mla_w_q_up, mla_g_kv,
     mla_w_kv_up, conf_w_dw, conf_b_dw, conf_ln_g, conf_ln_b, conf_w_pw, swa_sink, rel_bias) = map(np.asarray, (
         x_prompt, x_sample, g_pre, g_post, w_in, w_out, conv_a_w, conv_a_b, mla_g_q, mla_w_q_up, mla_g_kv,
         mla_w_kv_up, conf_w_dw, conf_b_dw, conf_ln_g, conf_ln_b, conf_w_pw, swa_sink, rel_bias))

    def blocks(a):
        return a.reshape(L, -1, 2, P).transpose(0, 3, 2, 1).reshape(L, P, -1)

    gq = np.zeros((L, 2 * P), np.float32)
    gq[:, :QR] = mla_g_q
    par = np.concatenate([
        blocks(conv_a_w), blocks(conv_a_b), blocks(conf_w_dw), blocks(conf_b_dw), blocks(conf_ln_g),
        blocks(conf_ln_b), blocks(gq), mla_g_kv[:, :, None],
        np.broadcast_to(swa_sink[:, None, :], (L, P, HEADS))], axis=2)
    wq = np.zeros((L, 2 * P, 512), np.float32)
    wq[:, :QR] = mla_w_q_up[:, :, _q_columns()]
    onehot, band, rope = _constants()
    arrays = {
        "x": np.concatenate([x_prompt, x_sample]),
        "w_in": w_in[:, :, _columns()].reshape(L, KD, P, NC, P).transpose(0, 3, 2, 1, 4).reshape(L, NC, P, D),
        "w_out": w_out,
        "w_q": wq.reshape(L, 2, P, 512).transpose(0, 2, 1, 3).reshape(L, P, 1024),
        "w_kv": mla_w_kv_up[:, :, _kv_columns()],
        "w_pw": conf_w_pw.reshape(L, 2, P, GW).transpose(0, 2, 1, 3).reshape(L, P, 2 * GW),
        "par": par, "g_pre": g_pre, "g_post": g_post, "rel_bias": rel_bias,
        "onehot": onehot, "band": band, "rope": rope,
    }
    arrays = {n: np.ascontiguousarray(a) for n, a in arrays.items()}
    nc = bacc.Bacc("TRN2", target_bir_lowering=False, num_devices=1,
                   dynamic_dma_scratch_size=1024)
    ins = [nc.dram_tensor(n, a.shape, mybir.dt.from_np(a.dtype), kind="ExternalInput").ap() for n, a in arrays.items()]
    y = nc.dram_tensor("y", (S, T, D), F32, kind="ExternalOutput").ap()
    build(nc, *ins, y)
    out = run(nc, [arrays], core_ids=[0]).results[0]["y"]
    return out[0:1], out[1:2]
```
